# Optimizing a Trainium2 kernel written in Bass

```python
import math
import jax
import jax.numpy as jnp
from jax import lax
import numpy as np
import jax, jax.numpy as jnp

D_MODEL = 1024
BATCH = 1
SEQ = 256
DEPTH = 2

GRID_W = 64
CTX_LEN = 256
N_EVEN = (DEPTH + 1) // 2
N_ODD = DEPTH // 2
N_MOD = 6
D_FF = 4 * D_MODEL
HEAD_DIM = D_MODEL // 16
MLA_HEADS = 8
MLA_NOPE = HEAD_DIM
MLA_ROPE = HEAD_DIM // 2
MLA_V = HEAD_DIM
MLA_Q_LORA = 3 * D_MODEL // 8
MLA_KV_LORA = D_MODEL // 4
GQA_HEADS = 8
GQA_KV_HEADS = 2
GQA_DIM = HEAD_DIM
ATTN_PARTS = (MLA_Q_LORA, MLA_KV_LORA, MLA_ROPE,
              GQA_HEADS * GQA_DIM, GQA_KV_HEADS * GQA_DIM, GQA_KV_HEADS * GQA_DIM)
ATTN_IN = sum(ATTN_PARTS)
ATTN_SPLITS = tuple(sum(ATTN_PARTS[:i + 1]) for i in range(len(ATTN_PARTS) - 1))
MIX_WIDTH = MLA_HEADS * MLA_V + GQA_HEADS * GQA_DIM
ROPE_THETA = 10000.0
Q_BLOCK = 128
HYENA_ORDER = 2
HYENA_SHORT = 3
HYENA_BANDS = 8
HYENA_EMB = 1 + 2 * HYENA_BANDS
HYENA_FILTER_HIDDEN = 64
HYENA_FAST_DECAY = 0.3
HYENA_SLOW_DECAY = 1.5
HYENA_TARGET = 1e-2
EPS = 1e-6


F32 = jnp.float32

def rmsnorm(x, g):
    xf = x.astype(F32)
    y = xf * lax.rsqrt(jnp.mean(xf * xf, axis=-1, keepdims=True) + EPS)
    return (y * g.astype(F32)).astype(x.dtype)

def modulate(x, g, shift, scale):
    return rmsnorm(x, g) * (1 + scale) + shift

def _rotate(x, ang):
    n = ang.shape[-1]
    cos = jnp.cos(ang)[None, :, None, :]
    sin = jnp.sin(ang)[None, :, None, :]
    a = x[..., :n].astype(F32)
    b = x[..., n:].astype(F32)
    return jnp.concatenate([a * cos - b * sin, a * sin + b * cos], axis=-1).astype(x.dtype)

def rope_2d(x, row, col):
    half = x.shape[-1] // 2
    nf = half // 2
    inv = ROPE_THETA ** (-jnp.arange(nf, dtype=F32) / nf)
    ang_r = row.astype(F32)[:, None] * inv[None]
    ang_c = col.astype(F32)[:, None] * inv[None]
    return jnp.concatenate([_rotate(x[..., :half], ang_r), _rotate(x[..., half:], ang_c)], axis=-1)

def block_attention(q, k, v):
    B, S, Hq, dk = q.shape
    Hk, dv = k.shape[2], v.shape[-1]
    G = Hq // Hk
    nb = S // Q_BLOCK
    scale = 1.0 / math.sqrt(dk)
    qb = q.reshape(B, nb, Q_BLOCK, Hk, G, dk).transpose(1, 0, 2, 3, 4, 5)

    def one(qblk):
        s = jnp.einsum('bqhgd,bkhd->bhgqk', qblk, k, preferred_element_type=F32) * scale
        p = jax.nn.softmax(s, axis=-1).astype(v.dtype)
        return jnp.einsum('bhgqk,bkhe->bqhge', p, v)

    o = lax.map(one, qb)
    return o.transpose(1, 0, 2, 3, 4, 5).reshape(B, S, Hq, dv)

def attn_heads(z, q_a_g, w_q_b, kv_a_g, w_kv_b, q_norm_g, k_norm_g, pos):
    B, L, _ = z.shape
    cq, ckv, kr, gq, gk, gv = jnp.split(z, ATTN_SPLITS, axis=-1)
    q = (rmsnorm(cq, q_a_g) @ w_q_b).reshape(B, L, MLA_HEADS, MLA_NOPE + MLA_ROPE)
    q_nope, q_rope = q[..., :MLA_NOPE], q[..., MLA_NOPE:]
    kv = (rmsnorm(ckv, kv_a_g) @ w_kv_b).reshape(B, L, MLA_HEADS, MLA_NOPE + MLA_V)
    k_nope, v_mla = kv[..., :MLA_NOPE], kv[..., MLA_NOPE:]
    k_rope = kr[:, :, None, :]
    gq = rmsnorm(gq.reshape(B, L, GQA_HEADS, GQA_DIM), q_norm_g)
    gk = rmsnorm(gk.reshape(B, L, GQA_KV_HEADS, GQA_DIM), k_norm_g)
    gv = gv.reshape(B, L, GQA_KV_HEADS, GQA_DIM)
    if pos is not None:
        row, col = pos
        q_rope = rope_2d(q_rope, row, col)
        k_rope = rope_2d(k_rope, row, col)
        gq = rope_2d(gq, row, col)
        gk = rope_2d(gk, row, col)
    q_mla = jnp.concatenate([q_nope, q_rope], axis=-1)
    k_mla = jnp.concatenate([k_nope, jnp.broadcast_to(k_rope, (B, L, MLA_HEADS, MLA_ROPE))], axis=-1)
    return q_mla, k_mla, v_mla, gq, gk, gv

def attention_mixer(hl, hc, w_in, q_a_g, w_q_b, kv_a_g, w_kv_b, q_norm_g, k_norm_g, w_out,
                    row, col, need_ctx):
    B, S, _ = hl.shape
    lat = attn_heads(hl @ w_in, q_a_g, w_q_b, kv_a_g, w_kv_b, q_norm_g, k_norm_g, (row, col))
    cx = attn_heads(hc @ w_in, q_a_g, w_q_b, kv_a_g, w_kv_b, q_norm_g, k_norm_g, None)
    k_mla = jnp.concatenate([cx[1], lat[1]], axis=1)
    v_mla = jnp.concatenate([cx[2], lat[2]], axis=1)
    k_gqa = jnp.concatenate([cx[4], lat[4]], axis=1)
    v_gqa = jnp.concatenate([cx[5], lat[5]], axis=1)
    o_lat = jnp.concatenate([
        block_attention(lat[0], k_mla, v_mla).reshape(B, S, MLA_HEADS * MLA_V),
        block_attention(lat[3], k_gqa, v_gqa).reshape(B, S, GQA_HEADS * GQA_DIM)], axis=-1) @ w_out
    o_ctx = None
    if need_ctx:
        Lc = hc.shape[1]
        o_ctx = jnp.concatenate([
            block_attention(cx[0], cx[1], cx[2]).reshape(B, Lc, MLA_HEADS * MLA_V),
            block_attention(cx[3], cx[4], cx[5]).reshape(B, Lc, GQA_HEADS * GQA_DIM)], axis=-1) @ w_out
    return o_lat, o_ctx

def short_conv(z, w, b):
    L = z.shape[1]
    p = HYENA_SHORT // 2
    zp = jnp.pad(z, ((0, 0), (p, p), (0, 0)))
    out = b
    for j in range(HYENA_SHORT):
        out = out + zp[:, j:j + L] * w[j]
    return out

def hyena_filters(L, f_w1, f_b1, f_w2, f_b2, f_w3, f_b3, f_freq, f_w4):
    t = jnp.arange(L, dtype=F32)
    t_norm = t / L
    w = 2.0 * math.pi * t / L
    bands = jnp.linspace(1e-4, HYENA_BANDS - 1, HYENA_BANDS, dtype=F32)
    fw = w[:, None] * bands[None]
    feats = jnp.concatenate([t_norm[:, None], jnp.cos(fw), -jnp.sin(fw)], axis=-1)
    fr = f_freq.astype(F32)
    h = jnp.sin(fr[0] * (feats @ f_w1.astype(F32) + f_b1.astype(F32)))
    h = jnp.sin(fr[1] * (h @ f_w2.astype(F32) + f_b2.astype(F32)))
    h = jnp.sin(fr[2] * (h @ f_w3.astype(F32) + f_b3.astype(F32)))
    h = (h @ f_w4.astype(F32)).reshape(L, 2, HYENA_ORDER, D_MODEL)
    max_decay = math.log(HYENA_TARGET) / HYENA_FAST_DECAY
    min_decay = math.log(HYENA_TARGET) / HYENA_SLOW_DECAY
    deltas = jnp.abs(jnp.linspace(min_decay, max_decay, D_MODEL, dtype=F32))
    window = jnp.exp(-t_norm[:, None] * deltas[None])
    h = h * window[:, None, None, :]
    h = h * lax.rsqrt(jnp.sum(h * h, axis=(0, 1), keepdims=True) + EPS)
    return h[:, 0], h[:, 1]

def bidir_long_conv(u, hf, hb, skip):
    L = u.shape[1]
    kfull = jnp.concatenate([hf, jnp.zeros_like(hf[:1]), hb[:0:-1]], axis=0)
    K = jnp.fft.rfft(kfull, n=2 * L, axis=0)
    uf = u.astype(F32)
    U = jnp.fft.rfft(uf, n=2 * L, axis=1)
    y = jnp.fft.irfft(U * K[None], n=2 * L, axis=1)[:, :L]
    return (y + uf * skip.astype(F32)).astype(u.dtype)

def hyena_mixer(h, w_in, conv_w, conv_b, f_w1, f_b1, f_w2, f_b2, f_w3, f_b3, f_freq, f_w4,
                skip, w_out):
    L = h.shape[1]
    z = short_conv(h @ w_in, conv_w, conv_b)
    x1, x2, v = jnp.split(z, 3, axis=-1)
    hf, hb = hyena_filters(L, f_w1, f_b1, f_w2, f_b2, f_w3, f_b3, f_freq, f_w4)
    y = v
    for n, gate in enumerate((x1, x2)):
        y = gate * bidir_long_conv(y, hf[:, n], hb[:, n], skip[n])
    return y @ w_out

def sq_relu_mlp(h, w1, w2):
    return jnp.square(jax.nn.relu(h @ w1)) @ w2

def first_inputs(seed: int = 0) -> dict:
    key = jax.random.key(seed)
    ks = list(jax.random.split(key, 40))

    def nrm(shape, scale):
        return jax.random.normal(ks.pop(), shape, F32) * scale

    def gain(shape):
        return 1.0 + nrm(shape, 0.02)

    D = D_MODEL
    return {
        'x': nrm((BATCH, SEQ, D), 1.0),
        'c': nrm((BATCH, D), 1.0),
        'ctx': nrm((BATCH, CTX_LEN, D), 1.0),
        'c_ctx': nrm((D,), 1.0),
        'w_mod': nrm((DEPTH, D, N_MOD * D), 0.5 * D ** -0.5),
        'b_mod': nrm((DEPTH, N_MOD * D), 0.02),
        'norm1_g': gain((DEPTH, D)),
        'norm2_g': gain((DEPTH, D)),
        'mlp_w1': nrm((DEPTH, D, D_FF), D ** -0.5),
        'mlp_w2': nrm((DEPTH, D_FF, D), D_FF ** -0.5),
        'a_w_in': nrm((N_EVEN, D, ATTN_IN), D ** -0.5),
        'a_q_a_g': gain((N_EVEN, MLA_Q_LORA)),
        'a_w_q_b': nrm((N_EVEN, MLA_Q_LORA, MLA_HEADS * (MLA_NOPE + MLA_ROPE)), MLA_Q_LORA ** -0.5),
        'a_kv_a_g': gain((N_EVEN, MLA_KV_LORA)),
        'a_w_kv_b': nrm((N_EVEN, MLA_KV_LORA, MLA_HEADS * (MLA_NOPE + MLA_V)), MLA_KV_LORA ** -0.5),
        'a_q_norm_g': gain((N_EVEN, GQA_DIM)),
        'a_k_norm_g': gain((N_EVEN, GQA_DIM)),
        'a_w_out': nrm((N_EVEN, MIX_WIDTH, D), MIX_WIDTH ** -0.5),
        'h_w_in': nrm((N_ODD, D, 3 * D), D ** -0.5),
        'h_conv_w': nrm((N_ODD, HYENA_SHORT, 3 * D), HYENA_SHORT ** -0.5),
        'h_conv_b': nrm((N_ODD, 3 * D), 0.02),
        'h_f_w1': nrm((N_ODD, HYENA_EMB, HYENA_FILTER_HIDDEN), HYENA_EMB ** -0.5),
        'h_f_b1': nrm((N_ODD, HYENA_FILTER_HIDDEN), 0.1),
        'h_f_w2': nrm((N_ODD, HYENA_FILTER_HIDDEN, HYENA_FILTER_HIDDEN), HYENA_FILTER_HIDDEN ** -0.5),
        'h_f_b2': nrm((N_ODD, HYENA_FILTER_HIDDEN), 0.1),
        'h_f_w3': nrm((N_ODD, HYENA_FILTER_HIDDEN, HYENA_FILTER_HIDDEN), HYENA_FILTER_HIDDEN ** -0.5),
        'h_f_b3': nrm((N_ODD, HYENA_FILTER_HIDDEN), 0.1),
        'h_f_freq': gain((N_ODD, 3, HYENA_FILTER_HIDDEN)),
        'h_f_w4': nrm((N_ODD, HYENA_FILTER_HIDDEN, 2 * HYENA_ORDER * D), HYENA_FILTER_HIDDEN ** -0.5),
        'h_skip': nrm((N_ODD, HYENA_ORDER, D), 0.3),
        'h_w_out': nrm((N_ODD, D, D), D ** -0.5),
        'final_g': gain((D,)),
    }

def first_block(x, c, ctx, c_ctx, w_mod, b_mod, norm1_g, norm2_g, mlp_w1, mlp_w2,
              a_w_in, a_q_a_g, a_w_q_b, a_kv_a_g, a_w_kv_b, a_q_norm_g, a_k_norm_g, a_w_out,
              h_w_in, h_conv_w, h_conv_b, h_f_w1, h_f_b1, h_f_w2, h_f_b2, h_f_w3, h_f_b3,
              h_f_freq, h_f_w4, h_skip, h_w_out, final_g):
    S = x.shape[1]
    rows = S // GRID_W
    rr, cc = jnp.meshgrid(jnp.arange(rows, dtype=jnp.int32), jnp.arange(GRID_W, dtype=jnp.int32),
                          indexing='ij')
    row, col = rr.reshape(-1), cc.reshape(-1)
    silu_c = jax.nn.silu(c)
    silu_cc = jax.nn.silu(c_ctx)
    for i in range(DEPTH):
        ctx_live = any(j % 2 == 0 for j in range(i + 1, DEPTH))
        j = i // 2
        m_l = (silu_c @ w_mod[i] + b_mod[i])[:, None, :]
        m_c = (silu_cc @ w_mod[i] + b_mod[i])[None, None, :]
        sh1, sc1, g1, sh2, sc2, g2 = jnp.split(m_l, N_MOD, axis=-1)
        csh1, csc1, cg1, csh2, csc2, cg2 = jnp.split(m_c, N_MOD, axis=-1)
        hl = modulate(x, norm1_g[i], sh1, sc1)
        if i % 2 == 0:
            hc = modulate(ctx, norm1_g[i], csh1, csc1)
            ol, oc = attention_mixer(hl, hc, a_w_in[j], a_q_a_g[j], a_w_q_b[j], a_kv_a_g[j],
                                     a_w_kv_b[j], a_q_norm_g[j], a_k_norm_g[j], a_w_out[j],
                                     row, col, ctx_live)
        else:
            hy = (h_w_in[j], h_conv_w[j], h_conv_b[j], h_f_w1[j], h_f_b1[j], h_f_w2[j], h_f_b2[j],
                  h_f_w3[j], h_f_b3[j], h_f_freq[j], h_f_w4[j], h_skip[j], h_w_out[j])
            ol = hyena_mixer(hl, *hy)
            oc = None
            if ctx_live:
                oc = hyena_mixer(modulate(ctx, norm1_g[i], csh1, csc1), *hy)
        x = x + g1 * ol
        x = x + g2 * sq_relu_mlp(modulate(x, norm2_g[i], sh2, sc2), mlp_w1[i], mlp_w2[i])
        if ctx_live:
            ctx = ctx + cg1 * oc
            ctx = ctx + cg2 * sq_relu_mlp(modulate(ctx, norm2_g[i], csh2, csc2), mlp_w1[i], mlp_w2[i])
    return rmsnorm(x, final_g)


DEPTH_2 = 1

F_GROUPS = 4
F_GROUP_DIM = 128
F_DIM = F_GROUPS * F_GROUP_DIM
NQK_HEADS = 4
NV_HEADS = 8
DK = 128
DV = 128
QK_DIM = NQK_HEADS * DK
V_DIM = NV_HEADS * DV
QKV_DIM = 2 * QK_DIM + V_DIM
CONV_K = 3
CHUNK = 64
BETA_OFF = QKV_DIM
A_OFF = BETA_OFF + 2 * NV_HEADS
GDN_IN_COLS = A_OFF + 2 * NV_HEADS
Z_OFF = GDN_IN_COLS
F_OFF = Z_OFF + V_DIM
GA_OFF = F_OFF + F_DIM
GB_OFF = GA_OFF + D_MODEL
IN_COLS = GB_OFF + D_MODEL
N_EXPERTS = 32
TOP_K = 4
D_EXPERT = D_MODEL
SWIGLU_ALPHA = 1.702
SWIGLU_LIMIT = 7.0
MOE_BLOCK = 128


def rmsnorm_2(x, g):
    xf = x.astype(jnp.float32)
    y = xf * lax.rsqrt(jnp.mean(xf * xf, axis=-1, keepdims=True) + EPS)
    return (y * g.astype(jnp.float32)).astype(x.dtype)

def modulate_2(h, shift, scale):
    return h * (1.0 + scale) + shift

def l2norm(t):
    t = t.astype(jnp.float32)
    return t * lax.rsqrt(jnp.sum(t * t, axis=-1, keepdims=True) + EPS)

def short_conv_grid(t, w, rows):
    B, L, C = t.shape
    y = lax.conv_general_dilated(t.reshape(B, rows, GRID_W, C), w[:, :, None, :], (1, 1), 'SAME',
                                 dimension_numbers=('NHWC', 'HWIO', 'NHWC'), feature_group_count=C)
    return y.reshape(B, L, C)

def short_conv_seq(t, w):
    C = t.shape[-1]
    return lax.conv_general_dilated(t, w[CONV_K // 2][:, None, :], (1,), 'SAME',
                                    dimension_numbers=('NWC', 'WIO', 'NWC'), feature_group_count=C)

def gdn_inputs(p, conv_w, rows):
    B, L, _ = p.shape
    qkv = p[..., :QKV_DIM]
    qkv = jax.nn.silu(short_conv_grid(qkv, conv_w, rows) if rows is not None else short_conv_seq(qkv, conv_w))
    rep = NV_HEADS // NQK_HEADS
    q = jnp.repeat(l2norm(qkv[..., :QK_DIM].reshape(B, L, NQK_HEADS, DK)) * DK ** -0.5, rep, axis=2)
    k = jnp.repeat(l2norm(qkv[..., QK_DIM:2 * QK_DIM].reshape(B, L, NQK_HEADS, DK)), rep, axis=2)
    v = qkv[..., 2 * QK_DIM:].reshape(B, L, NV_HEADS, DV)
    beta = jax.nn.sigmoid(p[..., BETA_OFF:A_OFF].astype(jnp.float32)).reshape(B, L, 2, NV_HEADS)
    a_raw = p[..., A_OFF:GDN_IN_COLS].astype(jnp.float32).reshape(B, L, 2, NV_HEADS)
    return q, k, v, a_raw, beta

def chunk_gated_delta(q, k, v, log_g, beta, s0):
    B, L, H, _ = q.shape
    n = L // CHUNK
    f32 = jnp.float32

    def blocks(t):
        t = t.astype(f32).reshape((B, n, CHUNK, H) + t.shape[3:])
        return jnp.moveaxis(t, 3, 1)

    qc, kc, vc, bc = blocks(q), blocks(k), blocks(v), blocks(beta)
    gc = jnp.cumsum(blocks(log_g), axis=-1)
    incl = jnp.tril(jnp.ones((CHUNK, CHUNK), bool))
    strict = jnp.tril(jnp.ones((CHUNK, CHUNK), bool), -1)
    decay = jnp.exp(jnp.where(incl, gc[..., :, None] - gc[..., None, :], -jnp.inf))
    kk = jnp.einsum('bhnid,bhnjd->bhnij', kc, kc)
    lower = jnp.where(strict, bc[..., :, None] * kk * decay, 0.0)
    rhs = jnp.concatenate([bc[..., None] * vc, (bc * jnp.exp(gc))[..., None] * kc], axis=-1)
    sol = lax.linalg.triangular_solve(jnp.eye(CHUNK, dtype=f32) + lower, rhs,
                                      left_side=True, lower=True, unit_diagonal=True)
    u_new, w = sol[..., :DV], sol[..., DV:]
    qk = jnp.einsum('bhnid,bhnjd->bhnij', qc, kc) * decay
    q_dec = qc * jnp.exp(gc)[..., None]
    g_end = gc[..., -1]
    k_dec = kc * jnp.exp(g_end[..., None] - gc)[..., None]

    def step(S, xs):
        u_c, w_c, qk_c, qd_c, kd_c, ge_c = xs
        u = u_c - jnp.einsum('bhck,bhkv->bhcv', w_c, S)
        o = jnp.einsum('bhck,bhkv->bhcv', qd_c, S) + jnp.einsum('bhij,bhjv->bhiv', qk_c, u)
        S = jnp.exp(ge_c)[..., None, None] * S + jnp.einsum('bhck,bhcv->bhkv', kd_c, u)
        return S, o

    xs = tuple(jnp.moveaxis(t, 2, 0) for t in (u_new, w, qk, q_dec, k_dec, g_end))
    s_fin, o = lax.scan(step, s0.astype(f32), xs)
    o = jnp.moveaxis(jnp.moveaxis(o, 0, 2), 1, 3).reshape(B, L, H, DV)
    return o, s_fin

def gdn_bidir(q, k, v, a_raw, beta, a_log, dt_bias, s0_f, s0_b):
    log_g = -jnp.exp(a_log.astype(jnp.float32)) * jax.nn.softplus(a_raw + dt_bias.astype(jnp.float32))
    o_f, s_f = chunk_gated_delta(q, k, v, log_g[:, :, 0], beta[:, :, 0], s0_f)
    flip = lambda t: jnp.flip(t, axis=1)
    o_b, s_b = chunk_gated_delta(flip(q), flip(k), flip(v), flip(log_g[:, :, 1]), flip(beta[:, :, 1]), s0_b)
    return o_f + flip(o_b), s_f, s_b

def fourier_mix(f):
    B, L, _ = f.shape
    fg = f.astype(jnp.float32).reshape(B, L, F_GROUPS, F_GROUP_DIM)
    return jnp.fft.fftn(fg, axes=(1, 3), norm='ortho').real.reshape(B, L, F_DIM).astype(f.dtype)

def merge_branches(p, o, gdn_norm_g, w_fourier_out, w_gdn_out, w_merge_out):
    B, L, _ = p.shape
    z = p[..., Z_OFF:F_OFF].astype(jnp.float32).reshape(B, L, NV_HEADS, DV)
    yb = o * lax.rsqrt(jnp.mean(o * o, axis=-1, keepdims=True) + EPS) * gdn_norm_g.astype(jnp.float32) * jax.nn.silu(z)
    yb = yb.reshape(B, L, V_DIM).astype(p.dtype) @ w_gdn_out
    ya = fourier_mix(p[..., F_OFF:GA_OFF]) @ w_fourier_out
    ga = jax.nn.sigmoid(p[..., GA_OFF:GB_OFF])
    gb = jax.nn.sigmoid(p[..., GB_OFF:IN_COLS])
    return (ga * ya + gb * yb) @ w_merge_out

def moe_ffn(h, w_router, b_router, w_gate, b_gate, w_up, b_up, w_down, b_down):
    N, D = h.shape
    logits = h.astype(jnp.float32) @ w_router.astype(jnp.float32) + b_router.astype(jnp.float32)
    top_val, top_idx = lax.top_k(logits, TOP_K)
    top_w = jax.nn.softmax(top_val, axis=-1)
    flat_e = top_idx.reshape(-1)
    flat_tok = jnp.repeat(jnp.arange(N, dtype=jnp.int32), TOP_K)
    order = jnp.argsort(flat_e)
    e_sorted = flat_e[order]
    counts = jnp.bincount(flat_e, length=N_EXPERTS)
    padded = (counts + MOE_BLOCK - 1) // MOE_BLOCK * MOE_BLOCK
    pad_end = jnp.cumsum(padded)
    pad_start = pad_end - padded
    grp_start = jnp.cumsum(counts) - counts
    dest = pad_start[e_sorted] + jnp.arange(N * TOP_K, dtype=jnp.int32) - grp_start[e_sorted]
    n_blocks = -(-(N * TOP_K + N_EXPERTS * (MOE_BLOCK - 1)) // MOE_BLOCK)
    n_slots = n_blocks * MOE_BLOCK
    slot_tok = jnp.full((n_slots,), N, jnp.int32).at[dest].set(flat_tok[order])
    slot_w = jnp.zeros((n_slots,), jnp.float32).at[dest].set(top_w.reshape(-1)[order])
    block_e = jnp.minimum(jnp.searchsorted(pad_end, jnp.arange(n_blocks, dtype=jnp.int32) * MOE_BLOCK, side='right'),
                          N_EXPERTS - 1)
    h_pad = jnp.concatenate([h, jnp.zeros((1, D), h.dtype)], axis=0)
    xb = h_pad[slot_tok].reshape(n_blocks, MOE_BLOCK, D)

    def expert_block(args):
        xe, e = args
        gate = jnp.minimum(xe @ w_gate[e] + b_gate[e], SWIGLU_LIMIT)
        up = jnp.clip(xe @ w_up[e] + b_up[e], -SWIGLU_LIMIT, SWIGLU_LIMIT)
        act = (up + 1.0) * gate * jax.nn.sigmoid(SWIGLU_ALPHA * gate)
        return act @ w_down[e] + b_down[e]

    yb = lax.map(expert_block, (xb, block_e)).reshape(n_slots, D)
    out = jnp.zeros((N + 1, D), jnp.float32).at[slot_tok].add(yb.astype(jnp.float32) * slot_w[:, None])
    return out[:N].astype(h.dtype)

def second_inputs(seed: int = 0) -> dict:
    key = jax.random.key(seed)
    ks = jax.random.split(key, 32)
    D = D_MODEL
    nrm = lambda k, shape, s: jax.random.normal(k, shape, jnp.float32) * s
    dt = jnp.exp(jax.random.uniform(ks[11], (DEPTH_2, 2, NV_HEADS), jnp.float32, math.log(1e-3), math.log(1e-1)))
    return {
        'x': nrm(ks[0], (BATCH, SEQ, D), 1.0),
        'c': nrm(ks[1], (BATCH, D), 1.0),
        'ctx': nrm(ks[2], (BATCH, CTX_LEN, D), 1.0),
        'c_ctx': nrm(ks[3], (D,), 1.0),
        'w_mod': nrm(ks[4], (DEPTH_2, D, 6 * D), 0.5 * D ** -0.5),
        'b_mod': nrm(ks[5], (DEPTH_2, 6 * D), 0.02),
        'norm1_g': 1.0 + nrm(ks[6], (DEPTH_2, D), 0.05),
        'norm2_g': 1.0 + nrm(ks[7], (DEPTH_2, D), 0.05),
        'w_in': nrm(ks[8], (DEPTH_2, D, IN_COLS), D ** -0.5),
        'conv_w': nrm(ks[9], (DEPTH_2, CONV_K, CONV_K, QKV_DIM), 1.0 / CONV_K),
        'a_log': jnp.log(jax.random.uniform(ks[10], (DEPTH_2, 2, NV_HEADS), jnp.float32, 1.0, 16.0)),
        'dt_bias': dt + jnp.log(-jnp.expm1(-dt)),
        'gdn_norm_g': 1.0 + nrm(ks[12], (DEPTH_2, DV), 0.05),
        'w_fourier_out': nrm(ks[13], (DEPTH_2, F_DIM, D), F_DIM ** -0.5),
        'w_gdn_out': nrm(ks[14], (DEPTH_2, V_DIM, D), V_DIM ** -0.5),
        'w_merge_out': nrm(ks[15], (DEPTH_2, D, D), D ** -0.5),
        'w_router': nrm(ks[16], (DEPTH_2, D, N_EXPERTS), D ** -0.5),
        'b_router': nrm(ks[17], (DEPTH_2, N_EXPERTS), 0.01),
        'w_gate': nrm(ks[18], (DEPTH_2, N_EXPERTS, D, D_EXPERT), D ** -0.5),
        'b_gate': nrm(ks[19], (DEPTH_2, N_EXPERTS, D_EXPERT), 0.01),
        'w_up': nrm(ks[20], (DEPTH_2, N_EXPERTS, D, D_EXPERT), D ** -0.5),
        'b_up': nrm(ks[21], (DEPTH_2, N_EXPERTS, D_EXPERT), 0.01),
        'w_down': nrm(ks[22], (DEPTH_2, N_EXPERTS, D_EXPERT, D), D_EXPERT ** -0.5),
        'b_down': nrm(ks[23], (DEPTH_2, N_EXPERTS, D), 0.01),
        'final_norm_g': 1.0 + nrm(ks[24], (D,), 0.05),
    }

def second_block(x, c, ctx, c_ctx, w_mod, b_mod, norm1_g, norm2_g, w_in, conv_w, a_log, dt_bias, gdn_norm_g,
              w_fourier_out, w_gdn_out, w_merge_out, w_router, b_router, w_gate, b_gate, w_up, b_up,
              w_down, b_down, final_norm_g):
    B, L, D = x.shape
    rows = L // GRID_W
    h_ctx = ctx
    for l in range(DEPTH_2):
        last = l == DEPTH_2 - 1
        mod = (jax.nn.silu(c) @ w_mod[l] + b_mod[l])[:, None, :]
        sh1, sc1, g1, sh2, sc2, g2 = jnp.split(mod, 6, axis=-1)
        mod_c = jax.nn.silu(c_ctx) @ w_mod[l] + b_mod[l]
        csh1, csc1, cg1, csh2, csc2, cg2 = jnp.split(mod_c, 6)

        u_ctx = modulate_2(rmsnorm_2(h_ctx, norm1_g[l]), csh1, csc1)
        p_ctx = u_ctx @ (w_in[l][:, :GDN_IN_COLS] if last else w_in[l])
        q, k, v, a_raw, beta = gdn_inputs(p_ctx, conv_w[l], None)
        zero = jnp.zeros((B, NV_HEADS, DK, DV), jnp.float32)
        o_ctx, s_f, s_b = gdn_bidir(q, k, v, a_raw, beta, a_log[l], dt_bias[l], zero, zero)

        u = modulate_2(rmsnorm_2(x, norm1_g[l]), sh1, sc1)
        p = u @ w_in[l]
        q, k, v, a_raw, beta = gdn_inputs(p, conv_w[l], rows)
        o, _, _ = gdn_bidir(q, k, v, a_raw, beta, a_log[l], dt_bias[l], s_f, s_b)
        x = x + g1 * merge_branches(p, o, gdn_norm_g[l], w_fourier_out[l], w_gdn_out[l], w_merge_out[l])

        h2 = modulate_2(rmsnorm_2(x, norm2_g[l]), sh2, sc2)
        x = x + g2 * moe_ffn(h2.reshape(B * L, D), w_router[l], b_router[l], w_gate[l], b_gate[l],
                             w_up[l], b_up[l], w_down[l], b_down[l]).reshape(B, L, D)

        if not last:
            h_ctx = h_ctx + cg1 * merge_branches(p_ctx, o_ctx, gdn_norm_g[l], w_fourier_out[l], w_gdn_out[l], w_merge_out[l])
            hc2 = modulate_2(rmsnorm_2(h_ctx, norm2_g[l]), csh2, csc2)
            n_ctx = h_ctx.shape[1]
            h_ctx = h_ctx + cg2 * moe_ffn(hc2.reshape(B * n_ctx, D), w_router[l], b_router[l], w_gate[l], b_gate[l],
                                          w_up[l], b_up[l], w_down[l], b_down[l]).reshape(B, n_ctx, D)
    return rmsnorm_2(x, final_norm_g)


def setup_inputs(seed=0):
    out = dict(first_inputs(seed))
    for name, value in second_inputs(seed + 1).items():
        if name != "x":
            out[name + "_2"] = value
    return out


def reference(
    x, c, ctx, c_ctx, w_mod, b_mod, norm1_g, norm2_g, mlp_w1, mlp_w2, a_w_in, a_q_a_g, a_w_q_b,
    a_kv_a_g, a_w_kv_b, a_q_norm_g, a_k_norm_g, a_w_out, h_w_in, h_conv_w, h_conv_b, h_f_w1,
    h_f_b1, h_f_w2, h_f_b2, h_f_w3, h_f_b3, h_f_freq, h_f_w4, h_skip, h_w_out, final_g, c_2,
    ctx_2, c_ctx_2, w_mod_2, b_mod_2, norm1_g_2, norm2_g_2, w_in_2, conv_w_2, a_log_2,
    dt_bias_2, gdn_norm_g_2, w_fourier_out_2, w_gdn_out_2, w_merge_out_2, w_router_2,
    b_router_2, w_gate_2, b_gate_2, w_up_2, b_up_2, w_down_2, b_down_2, final_norm_g_2,
):
    x = first_block(
        x, c, ctx, c_ctx, w_mod, b_mod, norm1_g, norm2_g, mlp_w1, mlp_w2, a_w_in, a_q_a_g,
        a_w_q_b, a_kv_a_g, a_w_kv_b, a_q_norm_g, a_k_norm_g, a_w_out, h_w_in, h_conv_w,
        h_conv_b, h_f_w1, h_f_b1, h_f_w2, h_f_b2, h_f_w3, h_f_b3, h_f_freq, h_f_w4, h_skip,
        h_w_out, final_g,
    )
    return second_block(
        x, c_2, ctx_2, c_ctx_2, w_mod_2, b_mod_2, norm1_g_2, norm2_g_2, w_in_2, conv_w_2,
        a_log_2, dt_bias_2, gdn_norm_g_2, w_fourier_out_2, w_gdn_out_2, w_merge_out_2,
        w_router_2, b_router_2, w_gate_2, b_gate_2, w_up_2, b_up_2, w_down_2, b_down_2,
        final_norm_g_2,
    )


_drawn_inputs = setup_inputs


def setup_inputs(seed=0):
    import zlib

    import numpy as np

    out = dict(_drawn_inputs(seed))
    spreads = {}
    factors = {'norm2_g': 2.994,
     'a_q_a_g': 8.0,
     'a_kv_a_g': 8.0,
     'a_q_norm_g': 8.0,
     'a_k_norm_g': 8.0,
     'ctx_2': 4.801,
     'c_ctx_2': 8.0,
     'norm1_g_2': 3.791,
     'gdn_norm_g_2': 5.084,
     'b_router_2': 30.309,
     'b_gate_2': 64.0,
     'b_up_2': 64.0,
     'b_down_2': 64.0,
     'h_f_freq': 2.854,
     'norm2_g_2': 5.402,
     'h_conv_b': 2.818}
    for name, (base, spread) in spreads.items():
        noise = np.random.default_rng([zlib.crc32(name.encode()), seed]).standard_normal(out[name].shape)
        drawn = base * np.exp(spread * noise) if base else spread * noise
        out[name] = jnp.asarray(drawn.astype(out[name].dtype))
    for name, factor in factors.items():
        out[name] = (out[name] * factor).astype(out[name].dtype)
    return out
```

```python
import math
from contextlib import ExitStack

import numpy as np
import concourse.bass as bass
from concourse import mybir

P = 128
D = 1024
KC = D // P
T = 256
T2 = 2 * T
BANK = 512
F32 = mybir.dt.float32
ALU = mybir.AluOpType
ACT = mybir.ActivationFunctionType
AX_X = mybir.AxisListType.X
EPS = 1e-6

N_MOD = 6
MOD_CHUNKS = N_MOD * KC
MLP_CHUNKS = 4 * KC
MLA_HEADS, NOPE, ROPE, DV = 8, 64, 32, 64
QK_MLA = NOPE + ROPE
Q_CHUNKS, KV_CHUNKS = 3, 2
GQA_HEADS, GQA_KV = 8, 2
HEAD = 64
GRID_W = 64
ROWS = T // GRID_W
F_HIDDEN, F_EMB, BANDS, ORDERS = 64, 17, 8, 2
NQK, NV = 4, 8
QKV_CHUNKS = 2 * NQK + NV
F_GROUPS = 4
N_EXPERTS, TOP_K = 32, 4
ALPHA, LIMIT = 1.702, 7.0
LEVELS = 7

RING = 8
GROUP = 2 * RING
STREAM = [("mod", 3 * MOD_CHUNKS),
          ("a_in", 12), ("a_qb", 3), ("a_kvb", 2), ("a_out", KC),
          ("mlp0_up", MLP_CHUNKS), ("mlp0_down", MLP_CHUNKS),
          ("h_in", 3 * KC), ("h_out", KC),
          ("mlp1_up", MLP_CHUNKS), ("mlp1_down", MLP_CHUNKS),
          ("g_qkv", QKV_CHUNKS), ("g_ba", 1), ("g_f", F_GROUPS), ("g_fout", 4), ("g_z", KC), ("g_out", KC),
          ("g_ga", KC), ("g_gb", KC), ("g_merge", KC), ("router", 1),
          ("moe", N_EXPERTS * 3 * KC)]
START = {name: sum(n for _, n in STREAM[:i]) for i, (name, _) in enumerate(STREAM)}
SLABS = sum(n for _, n in STREAM)


class Steps:

    def __init__(self, sem):
        self.sem, self.n, self.turn, self.per = sem, 0, None, 0

    def on(self, eng):
        self.eng = eng
        return self

    def done(self, ins):
        ins.then_inc(self.sem, 1)
        self.n += 1
        return self.n

    def wait(self, n=None):
        n = self.n if n is None else n
        self.eng.wait_ge(self.sem, n if self.turn is None else self.turn * self.per + n)

    def then(self, ins):
        self.done(ins)
        self.wait()

    def loop(self, turn, per):
        self.turn, self.per, self.first = turn, per, self.n

    def end(self, turns):
        assert self.n - self.first == self.per, (self.n - self.first, self.per)
        self.n += (turns - 1) * self.per
        self.turn = None


def small_layout():
    out, at = {}, 0
    for name, width in [
            ("c4", KC * 4), ("b_mod", 3 * MOD_CHUNKS), ("norm_g", 8 * KC), ("q_a_g", Q_CHUNKS),
            ("kv_a_g", KV_CHUNKS), ("q_norm_g", 1), ("k_norm_g", 1), ("h_conv_w", 3 * 3 * KC),
            ("h_conv_b", 3 * KC), ("f_b", 3), ("f_freq", 3), ("h_skip", ORDERS * KC),
            ("g_conv_w", 9 * QKV_CHUNKS), ("dt_bias", 2 * NV), ("a_log", 2 * NV), ("gdn_g", 1),
            ("b_router", N_EXPERTS), ("b_gate", N_EXPERTS * KC), ("b_up", N_EXPERTS * KC),
            ("b_down", N_EXPERTS * KC), ("f_w1", F_HIDDEN), ("f_w2", F_HIDDEN), ("f_w3", F_HIDDEN),
            ("ident", P), ("ones", P), ("blocks64", P), ("eps", 1), ("one", 1),
            ("rope_cos", T), ("rope_sin", T), ("rope_turn", P),
            ("kr_cos", T), ("kr_sin", T), ("kr_turn", QK_MLA),
            ("tri", 2 * P), ("strict", 2 * P), ("level", 2 * LEVELS * P),
            ("four_g", 2 * P), ("four_t", 4 * T)]:
        out[name] = (at, width)
        at += width
    return out, at


class Core:
    pass


def sem(k, name):
    k.sems.append(k.sem_stack.enter_context(k.nc.semaphore(name)))
    return k.sems[-1]


def with_own_semaphores(k, layer):
    nc = k.nc
    k.sems = []
    with ExitStack() as k.sem_stack:
        layer(k)
        with nc.Block() as block:
            @block.sync
            def _(sp):
                for s in k.sems:
                    sp.sem_clear(s)


def take_slab(k, pe, j, turn=None, count=RING):
    value = 16 * (j // RING + 1)
    pe.wait_ge(k.slab_filled[j % RING], value if turn is None else turn * (16 * count // RING) + value)
    return k.ring[:, j % RING, :]


def refill(k, sp, first, count, turns=1):
    def one(j, turn=None):
        n = j + RING
        if turn is None:
            if n >= SLABS:
                return
            sp.wait_ge(k.slab_used, j + 1)
            src = k.stream_dram[n, :, :]
        else:
            sp.wait_ge(k.slab_used, turn * count + j + 1)
            src = k.stream_dram[bass.ds(turn * count + n, 1), :, :].rearrange("a p n -> (a p) n")
        sp.dma_start(k.ring[:, j % RING, :], src).then_inc(k.slab_filled[j % RING], 16)

    whole = turns if first + count * turns + RING <= SLABS else turns - 1
    if turns > 1:
        with sp.Fori(0, whole) as turn:
            for j in range(count):
                one(first + j, turn)
    for j in range(whole * count if turns > 1 else 0, count * turns):
        one(first + j)


def slab_product(k, slab, rhs, out, width=P, chunks=KC, start=True, stop=True, used=True):
    w = slab.rearrange("p (k c) -> p k c", k=chunks)
    for c in range(chunks):
        last = k.nc.tensor.matmul(out, w[:, c, 0:width], rhs(c), start=start and c == 0, stop=stop and c == chunks - 1)
    if used:
        last.then_inc(k.slab_used, 1)
    return last


def stage_load(k):
    nc = k.nc
    with nc.Block() as block:
        @block.sync
        def _(sp):
            for j in range(RING):
                sp.dma_start(k.ring[:, j, :], k.stream_dram[j, :, :]).then_inc(k.slab_filled[j], 16)

        @block.scalar
        def _(act):
            act.dma_start(k.small[:, :], k.small_dram).then_inc(k.small_loaded, 16)
            act.dma_start(k.x[:, :, :], k.x_dram[0]).then_inc(k.x_loaded, 16)
            act.wait_ge(k.small_loaded, 16)
            act.wait_ge(k.x_loaded, 16)


def stage_modulation(k):
    nc = k.nc
    silu_ready, group_taken = (sem(k, n) for n in ("silu_ready", "mod_group_taken"))
    first, turns = START["mod"], 3 * MOD_CHUNKS // GROUP
    with ExitStack() as local:
        c4 = local.enter_context(nc.sbuf_tensor("c4", [P, KC * 4], F32))
        with nc.Block() as block:
            @block.sync
            def _(sp):
                refill(k, sp, first, GROUP, turns)

            @block.scalar
            def _(act):
                nc.scalar.activation(c4[:, :], k.s("c4"), ACT.Silu).then_inc(silu_ready, 1)

            @block.tensor
            def _(pe):
                pe.wait_ge(silu_ready, 1)

                def group(turn=None):
                    for s in range(GROUP):
                        slab = take_slab(k, pe, first + s, turn, GROUP)
                        slab_product(k, slab, lambda c: c4[:, 4 * c:4 * c + 4], k.ps[:, 0, 4 * s:4 * s + 4])

                group()
                with pe.Fori(1, turns) as turn:
                    pe.wait_ge(group_taken, turn)
                    group(turn)

            @block.vector
            def _(dve):
                b = k.s("b_mod")
                with dve.Fori(0, turns) as turn:
                    dve.wait_ge(k.slab_used, turn * GROUP + GROUP)
                    for v in range(4):
                        last = nc.vector.tensor_tensor(
                            k.mod[:, v, bass.ds(turn * GROUP, GROUP)], k.ps[:, 0, v:4 * GROUP:4], b[:, bass.ds(turn * GROUP, GROUP)], ALU.add)
                    last.then_inc(group_taken, 1)
                dve.wait_ge(group_taken, turns)
                for n, (layer, part, v) in enumerate(k.norms):
                    a = layer * MOD_CHUNKS + part * KC
                    nc.vector.scalar_tensor_tensor(k.gain[:, n, :], k.mod[:, v, a:a + KC], 1.0,
                                                   k.s("norm_g")[:, k.norm_of[n] * KC:(k.norm_of[n] + 1) * KC], ALU.add, ALU.mult)


def shift_of(k, n, c):
    layer, part, v = k.norms[n]
    at = layer * MOD_CHUNKS + (part - 1) * KC + c
    return k.mod[:, v, at:at + 1]


def gate_of(k, layer, part, c):
    v = 2 if layer == 2 else 0
    at = layer * MOD_CHUNKS + part * KC + c
    return k.mod[:, v, at:at + 1]


def stage_norm(k, name, parts, chunks=KC, gains=None):
    nc = k.nc
    squares, total, root, scaled, inverse = k.norm_sems
    chunk0, part0 = k.norm_chunks, k.norm_parts
    k.norm_chunks, k.norm_parts = chunk0 + len(parts) * chunks, part0 + len(parts)
    with ExitStack() as local:
        sq = local.enter_context(nc.sbuf_tensor(f"{name}_sq", [P, chunks, T2], F32))
        std = local.enter_context(nc.sbuf_tensor(f"{name}_std", [P, len(parts), T], F32))
        rstd = local.enter_context(nc.sbuf_tensor(f"{name}_rstd", [P, len(parts), T], F32))
        with nc.Block() as block:
            @block.scalar
            def _(act):
                for i, (src, _, _) in enumerate(parts):
                    for c in range(chunks):
                        nc.scalar.activation(sq[:, c, i * T:(i + 1) * T], src(c), ACT.Square).then_inc(squares, 1)
                for i in range(len(parts)):
                    act.wait_ge(total, part0 + i + 1)
                    nc.scalar.activation(std[:, i, :], k.ps[:, i, 0:T], ACT.Sqrt, scale=1.0 / (chunks * P), bias=k.s("eps")).then_inc(root, 1)
                for i, (_, n, dst) in enumerate(parts):
                    for c in range(chunks):
                        act.wait_ge(scaled, chunk0 + i * chunks + c + 1)
                        if n is None:
                            nc.scalar.activation(dst(c), sq[:, c, i * T:(i + 1) * T], ACT.Identity, scale=gains[:, c:c + 1])
                        else:
                            nc.scalar.activation(dst(c), sq[:, c, i * T:(i + 1) * T], ACT.Identity,
                                                 scale=k.gain[:, n, c:c + 1], bias=shift_of(k, n, c))

            @block.tensor
            def _(pe):
                for i in range(len(parts)):
                    for c in range(chunks):
                        pe.wait_ge(squares, chunk0 + i * chunks + c + 1)
                        last = nc.tensor.matmul(k.ps[:, i, 0:T], k.s("ones"), sq[:, c, i * T:(i + 1) * T], start=c == 0, stop=c == chunks - 1)
                    last.then_inc(total, 1)

            @block.vector
            def _(dve):
                for i, (src, _, _) in enumerate(parts):
                    dve.wait_ge(root, part0 + i + 1)
                    nc.vector.reciprocal(rstd[:, i, :], std[:, i, :]).then_inc(inverse, 1)
                    dve.wait_ge(inverse, part0 + i + 1)
                    for c in range(chunks):
                        nc.vector.tensor_tensor(sq[:, c, i * T:(i + 1) * T], src(c), rstd[:, i, :], ALU.mult).then_inc(scaled, 1)


def stage_mlp(k, layer):
    nc = k.nc
    name = f"mlp{layer}"
    bank_free, relu_done, hidden_ready, sum_free = (sem(k, f"{name}_{n}") for n in ("bank_free", "relu_done", "hidden_ready", "sum_free"))
    up, down = START[f"{name}_up"], START[f"{name}_down"]
    turns = MLP_CHUNKS // GROUP
    BANKS = 4
    SUMS = GROUP // 4
    with ExitStack() as local:
        hidden = local.enter_context(nc.sbuf_tensor(f"{name}_hidden", [P, MLP_CHUNKS, T], F32))
        with nc.Block() as block:
            @block.sync
            def _(sp):
                refill(k, sp, up, GROUP, 2 * turns)

            @block.tensor
            def _(pe):
                with pe.Fori(0, turns) as turn:
                    for s in range(GROUP):
                        slab = take_slab(k, pe, up + s, turn, GROUP)
                        pe.wait_ge(bank_free, turn * GROUP + s + 1)
                        slab_product(k, slab, lambda c: k.h[:, c, 0:T], k.ps[:, s % BANKS, 0:T])
                pe.wait_ge(hidden_ready, MLP_CHUNKS)
                with pe.Fori(0, turns) as turn:
                    for m in range(SUMS):
                        pe.wait_ge(sum_free, turn * SUMS + m + 1)
                        for q in range(4):
                            slab = take_slab(k, pe, down + 4 * m + q, turn, GROUP)
                            slab_product(k, slab, lambda c: hidden[:, q * KC + c, :], k.ps[:, BANKS + m, 0:T],
                                         start=q == 0, stop=q == 3)

            @block.vector
            def _(dve):
                dve.sem_inc(bank_free, BANKS)
                dve.sem_inc(sum_free, SUMS)
                with dve.Fori(0, turns) as turn:
                    for s in range(GROUP):
                        out = hidden[:, bass.ds(turn * GROUP + s, 1), :].rearrange("p a t -> p (a t)")
                        dve.wait_ge(k.slab_used, turn * GROUP + up + s + 1)
                        nc.vector.tensor_scalar(out, k.ps[:, s % BANKS, 0:T], 0.0, None, ALU.max).then_inc(bank_free, 1)
                        dve.wait_ge(bank_free, turn * GROUP + BANKS + s + 1)
                        nc.vector.tensor_tensor(out, out, out, ALU.mult).then_inc(hidden_ready, 1)
                with dve.Fori(0, turns) as turn:
                    for m in range(SUMS):
                        x = k.x[:, bass.ds(turn * SUMS + m, 1), :].rearrange("p a t -> p (a t)")
                        gate = k.mod[:, 0, bass.ds(layer * MOD_CHUNKS + (N_MOD - 1) * KC + turn * SUMS + m, 1)]
                        dve.wait_ge(k.slab_used, turn * GROUP + down + 4 * (m + 1))
                        nc.vector.scalar_tensor_tensor(x, k.ps[:, BANKS + m, 0:T], gate, x, ALU.mult, ALU.add).then_inc(sum_free, 1)


def stage_attention_in(k, a):
    nc = k.nc
    taken = sem(k, "a_in_taken")
    first = START["a_in"]
    order = [0, 1, 2, 5, 6, 7, 8, 3, 4, 9, 11, 10]
    with nc.Block() as block:
        @block.sync
        def _(sp):
            refill(k, sp, first, 12)

        @block.tensor
        def _(pe):
            for i, m in enumerate(order):
                slab = take_slab(k, pe, first + i)
                if i >= 8:
                    pe.wait_ge(taken, i - 7)
                bank = k.ps[:, i % 8, :]
                if m == 10:
                    w = slab.rearrange("p (k c) -> p k c", k=KC)
                    for b in range(4):
                        for c in range(KC):
                            last = nc.tensor.matmul(bank[:, b * P:(b + 1) * P], k.h[:, c, b * P:(b + 1) * P], w[:, c, :],
                                                    start=c == 0, stop=c == KC - 1)
                    last.then_inc(k.slab_used, 1)
                else:
                    n = T if m in (0, 1, 2, 5, 6, 7, 8) else T2
                    slab_product(k, slab, lambda c: k.h[:, c, 0:n], bank[:, 0:n])

        @block.vector
        def _(dve):
            for i, m in enumerate(order):
                bank = k.ps[:, i % 8, :]
                if m < 3:
                    dst, src = a.cq[:, m, :], bank[:, 0:T]
                elif m < 5:
                    dst, src = a.ckv[:, m - 3, :], bank
                elif m < 9:
                    dst, src = a.gqk[:, (m - 5) * T:(m - 4) * T], bank[:, 0:T]
                elif m == 9:
                    dst, src = a.gqk[:, 4 * T:4 * T + T2], bank
                elif m == 10:
                    dst, src = a.v[:, :, 4 * P:5 * P], bank.rearrange("p (b c) -> p b c", b=4)
                else:
                    dst, src = a.kr[NOPE:QK_MLA, :], bank[NOPE:QK_MLA, :]
                dve.wait_ge(k.slab_used, first + i + 1)
                nc.vector.tensor_copy(dst, src).then_inc(taken, 1)


def stage_grouped_heads(k, a):
    nc = k.nc
    squared, total, root, gained, turned = (sem(k, f"gqa_{n}") for n in ("squared", "total", "root", "gained", "turned"))
    W = 3 * BANK
    R = 5 * T
    turns = [(0, BANK), (BANK, 2 * BANK), (2 * BANK, R)]
    with ExitStack() as local:
        tmp = local.enter_context(nc.sbuf_tensor("gqa_tmp", [P, W], F32))
        std = local.enter_context(nc.sbuf_tensor("gqa_std", [P, W], F32))
        with nc.Block() as block:
            @block.sync
            def _(sp):
                pass

            @block.scalar
            def _(act):
                nc.scalar.activation(tmp[:, :], a.gqk[:, :], ACT.Square).then_inc(squared, 1)
                act.wait_ge(total, 3)
                nc.scalar.activation(std[:, :], k.ps[:, 0:3, :].rearrange("p b n -> p (b n)"), ACT.Sqrt, scale=1.0 / HEAD, bias=k.s("eps")).then_inc(root, 1)

            @block.tensor
            def _(pe):
                pe.wait_ge(squared, 1)
                for i in range(3):
                    nc.tensor.matmul(k.ps[:, i, :], k.s("blocks64"), tmp[:, i * BANK:(i + 1) * BANK], start=True, stop=True).then_inc(total, 1)
                pe.wait_ge(gained, 1)
                for i, (lo, hi) in enumerate(turns):
                    nc.tensor.matmul(k.ps[:, 4 + i, 0:hi - lo], k.s("rope_turn"), a.gqk[:, lo:hi], start=True, stop=True).then_inc(turned, 1)

            @block.vector
            def _(dve):
                steps = k.dve_steps.on(dve)
                dve.wait_ge(root, 1)
                steps.then(nc.vector.reciprocal(std[:, :], std[:, :]))
                steps.then(nc.vector.tensor_tensor(a.gqk[:, :], a.gqk[:, :], std[:, :], ALU.mult))
                nc.vector.tensor_scalar(a.gqk[:, 0:4 * T], a.gqk[:, 0:4 * T], k.s("q_norm_g"), None, ALU.mult)
                nc.vector.tensor_scalar(a.gqk[:, 4 * T:W], a.gqk[:, 4 * T:W], k.s("k_norm_g"), None, ALU.mult).then_inc(gained, 1)
                dve.wait_ge(turned, 3)
                for i in range(5):
                    bank = k.ps[:, 4 + i // 2, (i % 2) * T:(i % 2 + 1) * T]
                    steps.done(nc.vector.tensor_tensor(tmp[:, i * T:(i + 1) * T], bank, k.s("rope_sin"), ALU.mult))
                for i in range(5):
                    steps.done(nc.vector.tensor_tensor(a.gqk[:, i * T:(i + 1) * T], a.gqk[:, i * T:(i + 1) * T], k.s("rope_cos"), ALU.mult))
                steps.wait()
                nc.vector.tensor_tensor(a.gqk[:, 0:R], a.gqk[:, 0:R], tmp[:, 0:R], ALU.add)


def stage_latent_heads(k, a):
    nc = k.nc
    done, taken, turned, kr_done = (sem(k, f"mla_{n}") for n in ("done", "taken", "turned", "kr_done"))
    qb, kvb = START["a_qb"], START["a_kvb"]
    PER = [3, 3, 2]
    rope = slice(NOPE, QK_MLA)
    with ExitStack() as local:
        tmp = local.enter_context(nc.sbuf_tensor("mla_tmp", [P, 2, T], F32))
        with nc.Block() as block:
            @block.sync
            def _(sp):
                refill(k, sp, qb, 5)

            @block.tensor
            def _(pe):
                for s in range(3):
                    w = take_slab(k, pe, qb + s)[:, 0:Q_CHUNKS * 3 * QK_MLA].rearrange("p (k c) -> p k c", k=Q_CHUNKS)
                    for i in range(PER[s]):
                        h = 3 * s + i
                        for c in range(Q_CHUNKS):
                            last = nc.tensor.matmul(k.ps[0:QK_MLA, h // 2, (h % 2) * T:(h % 2 + 1) * T], w[:, c, i * QK_MLA:(i + 1) * QK_MLA],
                                                    a.cq[:, c, :], start=c == 0, stop=c == Q_CHUNKS - 1)
                    last.then_inc(k.slab_used, 1)
                w = take_slab(k, pe, kvb).rearrange("p (k c) -> p k c", k=KV_CHUNKS)
                for h in range(MLA_HEADS):
                    if h >= 4:
                        pe.wait_ge(taken, h - 3)
                    for c in range(KV_CHUNKS):
                        last = nc.tensor.matmul(k.ps[0:NOPE, 4 + h if h < 4 else h - 4, :], w[:, c, h * NOPE:(h + 1) * NOPE], a.ckv[:, c, :],
                                                start=c == 0, stop=c == KV_CHUNKS - 1)
                    if h < MLA_HEADS - 1:
                        last.then_inc(done, 1)
                    else:
                        last.then_inc(k.slab_used, 1)
                w = take_slab(k, pe, kvb + 1).rearrange("p (k c) -> p k c", k=KV_CHUNKS)
                for b in range(4):
                    pe.wait_ge(taken, 5 + b)
                    for c in range(KV_CHUNKS):
                        last = nc.tensor.matmul(k.ps[:, 4 + b, :], a.ckv[:, c, b * P:(b + 1) * P], w[:, c, :], start=c == 0, stop=c == KV_CHUNKS - 1)
                    if b < 3:
                        last.then_inc(done, 1)
                    else:
                        last.then_inc(k.slab_used, 1)
                turn = k.s("kr_turn")[rope, :]
                for i in range(4):
                    pe.wait_ge(taken, 9 + i)
                    nc.tensor.matmul(k.ps[0:QK_MLA, i, :], turn, a.q[rope, 2 * i:2 * i + 2, :], start=True, stop=True).then_inc(turned, 1)
                pe.wait_ge(taken, 13)
                nc.tensor.matmul(k.ps[0:QK_MLA, 4, 0:T], turn, a.kr[rope, 0:T], start=True, stop=True).then_inc(turned, 1)

            @block.vector
            def _(dve):
                steps = k.dve_steps.on(dve)
                for i in range(4):
                    dve.wait_ge(k.slab_used, qb + min(2, (2 * i + 1) // 3) + 1)
                    nc.vector.tensor_copy(a.q[0:QK_MLA, 2 * i:2 * i + 2, :].rearrange("p h t -> p (h t)"), k.ps[0:QK_MLA, i, :]).then_inc(taken, 1)
                for h in range(MLA_HEADS):
                    if h < MLA_HEADS - 1:
                        dve.wait_ge(done, h + 1)
                    else:
                        dve.wait_ge(k.slab_used, kvb + 1)
                    nc.vector.tensor_copy(a.k[0:NOPE, h, :], k.ps[0:NOPE, 4 + h if h < 4 else h - 4, :]).then_inc(taken, 1)
                for b in range(4):
                    if b < 3:
                        dve.wait_ge(done, MLA_HEADS + b)
                    else:
                        dve.wait_ge(k.slab_used, kvb + 2)
                    nc.vector.tensor_copy(a.v[:, b, 0:4 * P], k.ps[:, 4 + b, :]).then_inc(taken, 1)
                sin, cos = k.s("kr_sin")[rope, :], k.s("kr_cos")[rope, :]
                for i in range(4):
                    dve.wait_ge(turned, i + 1)
                    for j in range(2):
                        nc.vector.tensor_tensor(tmp[rope, j, :], k.ps[rope, i, j * T:(j + 1) * T], sin, ALU.mult)
                        last = nc.vector.tensor_tensor(a.q[rope, 2 * i + j, :], a.q[rope, 2 * i + j, :], cos, ALU.mult)
                    steps.then(last)
                    steps.then(nc.vector.tensor_tensor(a.q[rope, 2 * i:2 * i + 2, :], a.q[rope, 2 * i:2 * i + 2, :], tmp[rope, :, :], ALU.add))
                dve.wait_ge(turned, 5)
                nc.vector.tensor_tensor(tmp[rope, 0, :], k.ps[rope, 4, 0:T], sin, ALU.mult)
                steps.then(nc.vector.tensor_tensor(a.kr[rope, 0:T], a.kr[rope, 0:T], cos, ALU.mult))
                steps.then(nc.vector.tensor_tensor(a.kr[rope, 0:T], a.kr[rope, 0:T], tmp[rope, 0, :], ALU.add))
                for h in range(MLA_HEADS):
                    nc.vector.tensor_copy(a.k[rope, h, :], a.kr[rope, :])


def stage_attention(k, a):
    nc = k.nc
    scores, maxed, exped, normed, flipped, copied, mixed, stored = (sem(k, f"attn_{n}") for n in ("scores", "maxed", "exped", "normed", "flipped", "copied", "mixed", "stored"))
    heads = [("mla", h) for h in range(MLA_HEADS)] + [("gqa", h) for h in range(GQA_HEADS)]
    BLOCKS = T // P
    units = [(n, b) for n in range(len(heads)) for b in range(BLOCKS)]

    def operands(n, b):
        kind, h = heads[n]
        if kind == "mla":
            return a.q[0:QK_MLA, h, b * P:(b + 1) * P], a.k[0:QK_MLA, h, :], 1.0 / math.sqrt(QK_MLA)
        group, c = h % 2, h // 2
        rows = slice(group * HEAD, (group + 1) * HEAD)
        return a.gqk[rows, c * T + b * P:c * T + (b + 1) * P], a.gqk[rows, 4 * T:4 * T + T2], 1.0 / math.sqrt(HEAD)

    with ExitStack() as local:
        probs = local.enter_context(nc.sbuf_tensor("attn_probs", [P, 2, T2], F32))
        turned = local.enter_context(nc.sbuf_tensor("attn_turned", [P, 2, 4, T], F32))
        stat = local.enter_context(nc.sbuf_tensor("attn_stat", [P, 4, len(units)], F32))
        with nc.Block() as block:
            @block.sync
            def _(sp):
                pass

            @block.tensor
            def _(pe):
                def score(i):
                    q, kk, _ = operands(*units[i])
                    if i >= 2:
                        pe.wait_ge(exped, i - 1)
                    nc.tensor.matmul(k.ps[:, i % 2, :], q, kk, start=True, stop=True).then_inc(scores, 1)

                score(0)
                for i, (n, b) in enumerate(units):
                    if i + 1 < len(units):
                        score(i + 1)
                    pe.wait_ge(normed, i + 1)
                    if i >= 2:
                        pe.wait_ge(copied, i - 1)
                    for c in range(4):
                        last = nc.tensor.transpose(k.ps[:, 2 + i % 2, c * P:(c + 1) * P], probs[:, i % 2, c * P:(c + 1) * P], k.s("ident"))
                    last.then_inc(flipped, 1)
                    if b == BLOCKS - 1:
                        pe.wait_ge(copied, i + 1)
                        if n >= 2:
                            pe.wait_ge(stored, n - 1)
                        pair = n // 2 if n < MLA_HEADS else 4
                        for c in range(4):
                            last = nc.tensor.matmul(k.ps[:, 4 + n % 2, 0:T], a.v[:, c, pair * P:(pair + 1) * P], turned[:, n % 2, c, :],
                                                    start=c == 0, stop=c == 3)
                        last.then_inc(mixed, 1)

            @block.vector
            def _(dve):
                steps = k.dve_steps.on(dve)

                def store(n):
                    rows = slice((n % 2) * HEAD, (n % 2 + 1) * HEAD)
                    dve.wait_ge(mixed, n + 1)
                    nc.vector.tensor_copy(a.o[rows, n // 2, :], k.ps[rows, 4 + n % 2, 0:T]).then_inc(stored, 1)

                def largest(i):
                    scale = operands(*units[i])[2]
                    dve.wait_ge(scores, i + 1)
                    steps.then(nc.vector.reduce_max(stat[:, 0, i:i + 1], k.ps[:, i % 2, :], AX_X))
                    nc.vector.tensor_scalar(stat[:, 1, i:i + 1], stat[:, 0, i:i + 1], -scale, None, ALU.mult).then_inc(maxed, 1)

                largest(0)
                for i, (n, b) in enumerate(units):
                    if i + 1 < len(units):
                        largest(i + 1)
                    dve.wait_ge(exped, i + 1)
                    steps.then(nc.vector.reciprocal(stat[:, 3, i:i + 1], stat[:, 2, i:i + 1]))
                    nc.vector.tensor_scalar(probs[:, i % 2, :], probs[:, i % 2, :], stat[:, 3, i:i + 1], None, ALU.mult).then_inc(normed, 1)
                    if b == 0 and n >= 1:
                        store(n - 1)
                store(len(heads) - 1)

            @block.scalar
            def _(act):
                def copy(i):
                    n, b = units[i]
                    act.wait_ge(flipped, i + 1)
                    if n >= 2:
                        act.wait_ge(mixed, n - 1)
                    nc.scalar.activation(turned[:, n % 2, :, b * P:(b + 1) * P], k.ps[:, 2 + i % 2, :].rearrange("p (c q) -> p c q", c=4),
                                         ACT.Identity).then_inc(copied, 1)

                for i in range(len(units)):
                    act.wait_ge(maxed, i + 1)
                    if i >= 2:
                        act.wait_ge(flipped, i - 1)
                    nc.scalar.activation(probs[:, i % 2, :], k.ps[:, i % 2, :], ACT.Exp, scale=operands(*units[i])[2], bias=stat[:, 1, i:i + 1],
                                         accum_out=stat[:, 2, i:i + 1]).then_inc(exped, 1)
                    if i >= 1:
                        copy(i - 1)
                copy(len(units) - 1)


def stage_add_product(k, name, slabs, src, layer, part):
    nc = k.nc
    taken = sem(k, f"{name}_taken")
    first = START[slabs]
    with nc.Block() as block:
        @block.sync
        def _(sp):
            refill(k, sp, first, KC)

        @block.tensor
        def _(pe):
            for m in range(KC):
                slab = take_slab(k, pe, first + m)
                slab_product(k, slab, lambda c: src[:, c, :], k.ps[:, m, 0:T])

        @block.vector
        def _(dve):
            for m in range(KC):
                dve.wait_ge(k.slab_used, first + m + 1)
                nc.vector.scalar_tensor_tensor(k.x[:, m, :], k.ps[:, m, 0:T], gate_of(k, layer, part, m), k.x[:, m, :], ALU.mult, ALU.add)


def attention_layer(k):
    nc = k.nc
    with ExitStack() as local:
        a = Core()
        def sb(name, shape):
            return local.enter_context(nc.sbuf_tensor(f"a_{name}", shape, F32))
        a.cq, a.ckv, a.gqk = sb("cq", [P, Q_CHUNKS, T]), sb("ckv", [P, KV_CHUNKS, T2]), sb("gqk", [P, 3 * BANK])
        a.kr, a.q, a.k = sb("kr", [P, T2]), sb("q", [P, MLA_HEADS, T]), sb("k", [P, MLA_HEADS, T2])
        a.v, a.o = sb("v", [P, 4, 5 * P]), sb("o", [P, KC, T])
        ctx = sb("ctx", [P, KC, T])
        loaded = sem(k, "a_ctx_loaded")
        with nc.Block() as block:
            @block.scalar
            def _(act):
                act.dma_start(ctx[:, :, :], k.x_dram[1]).then_inc(loaded, 16)
                act.wait_ge(loaded, 16)
        stage_norm(k, "a_norm", [(lambda c: k.x[:, c, :], 0, lambda c: k.h[:, c, 0:T]),
                                 (lambda c: ctx[:, c, :], 1, lambda c: k.h[:, c, T:T2])])
        stage_attention_in(k, a)
        stage_norm(k, "cq_norm", [(lambda c: a.cq[:, c, :], None, lambda c: a.cq[:, c, :])], Q_CHUNKS, k.s("q_a_g"))
        stage_norm(k, "ckv_norm", [(lambda c, i=i: a.ckv[:, c, i * T:(i + 1) * T], None, lambda c, i=i: a.ckv[:, c, i * T:(i + 1) * T])
                                   for i in range(2)], KV_CHUNKS, k.s("kv_a_g"))
        stage_grouped_heads(k, a)
        stage_latent_heads(k, a)
        stage_attention(k, a)
        stage_add_product(k, "a_out", "a_out", a.o, 0, 2)


def stage_filters(k, spectra, rstd):
    nc = k.nc
    loaded, layer_done, reduced, sine_ready, filt_done, filt_taken, squares, norm_done, parts_ready, spec_done, spec_taken, normed = (sem(k, f"filt_{n}") for n in ("loaded", "layer_done", "reduced", "sine_ready", "done", "taken", "squares", "norm_done", "parts_ready", "spec_done", "spec_taken", "normed"))
    H, C2PI, MAGIC = F_HIDDEN, 6.28125, 1.5 * 2.0 ** 23
    with ExitStack() as local:
        def sb(name, shape):
            return local.enter_context(nc.sbuf_tensor(f"filt_{name}", shape, F32))
        feats, hid, y, turns_ = sb("feats", [F_EMB, T]), sb("hid", [H, T]), sb("y", [H, T]), sb("turns", [H, T])
        w4, window = sb("w4", [H, 4 * D]), sb("window", [P, 2, D])
        fc, fs, first = sb("fc", [P, 2, T]), sb("fs", [P, 2, T]), sb("first", [P, 2])
        power, sq, even = sb("power", [P, ORDERS, D]), sb("sq", [P, D]), sb("even", [P, 2, D])
        root = sb("root", [P, ORDERS * KC])
        with nc.Block() as block:
            @block.scalar
            def _(act):
                for dst, src in [(feats, "feats"), (w4, "w4"), (window, "window"), (fc, "fc"), (fs, "fs"), (first, "first")]:
                    act.dma_start(dst[:], k.dram[src]).then_inc(loaded, 16)
                act.wait_ge(loaded, 6 * 16)
                for n in range(3):
                    act.wait_ge(reduced, n + 1)
                    nc.scalar.activation(hid[:, :], y[:, :], ACT.Sin).then_inc(sine_ready, 1)
                act.wait_ge(norm_done, 1)
                nc.scalar.activation(root[:, :], k.ps[:, 0, 0:ORDERS * KC], ACT.Sqrt, bias=k.s("eps")).then_inc(normed, 1)
                for o in range(ORDERS):
                    for n in range(8):
                        act.wait_ge(spec_done, o * 8 + n + 1)
                        if n == 0:
                            act.wait_ge(spec_done, o * 8 + 8)
                        nc.scalar.activation(spectra[:, o, n // 2, (n % 2) * BANK:(n % 2 + 1) * BANK], k.ps[:, n, :], ACT.Identity).then_inc(spec_taken, 1)

            @block.tensor
            def _(pe):
                pe.wait_ge(loaded, 6 * 16)
                for n, w in enumerate(("f_w1", "f_w2", "f_w3")):
                    if n:
                        pe.wait_ge(sine_ready, n)
                    rows = F_EMB if n == 0 else H
                    nc.tensor.matmul(k.ps[0:H, n, 0:T], k.s(w)[0:rows, :], (feats if n == 0 else hid)[:, :], start=True, stop=True).then_inc(layer_done, 1)
                pe.wait_ge(sine_ready, 3)
                for t in range(2):
                    for n in range(8):
                        if t:
                            pe.wait_ge(filt_taken, n + 1)
                        nc.tensor.matmul(k.ps[:, n, :], hid[:, t * P:(t + 1) * P], w4[:, n * BANK:(n + 1) * BANK], start=True, stop=True).then_inc(filt_done, 1)
                pe.wait_ge(squares, 1)
                pe.wait_ge(filt_taken, 16)
                for n in range(ORDERS * KC):
                    last = nc.tensor.matmul(k.ps[:, 0, n:n + 1], power[:, n // KC, (n % KC) * P:(n % KC + 1) * P], k.s("ones")[:, 0:1], start=True, stop=True)
                last.then_inc(norm_done, 1)
                pe.wait_ge(normed, 1)
                for o in range(ORDERS):
                    pe.wait_ge(parts_ready, o + 1)
                    for n in range(8):
                        part, f, half = n // 4, n // 2 % 2, n % 2
                        if o:
                            pe.wait_ge(spec_taken, n + 1)
                        for t in range(2):
                            src = even[:, t, :] if part == 0 else spectra[:, o, 2 + t, :]
                            last = nc.tensor.matmul(k.ps[:, n, :], (fc if part == 0 else fs)[:, t, f * P:(f + 1) * P],
                                                    src[:, half * BANK:(half + 1) * BANK], start=t == 0, stop=t == 1)
                        last.then_inc(spec_done, 1)

            @block.vector
            def _(dve):
                steps = k.dve_steps.on(dve)
                for n in range(3):
                    dve.wait_ge(layer_done, n + 1)
                    if n:
                        dve.wait_ge(sine_ready, n)
                    b, f = k.s("f_b")[0:H, n:n + 1], k.s("f_freq")[0:H, n:n + 1]
                    steps.then(nc.vector.tensor_scalar(y[:, :], k.ps[0:H, n, 0:T], b, f, ALU.add, ALU.mult))
                    steps.then(nc.vector.tensor_scalar(turns_[:, :], y[:, :], 1.0 / (2.0 * math.pi), MAGIC, ALU.mult, ALU.add))
                    steps.then(nc.vector.tensor_scalar(turns_[:, :], turns_[:, :], MAGIC, None, ALU.subtract))
                    steps.then(nc.vector.scalar_tensor_tensor(y[:, :], turns_[:, :], -C2PI, y[:, :], ALU.mult, ALU.add))
                    steps.then(nc.vector.scalar_tensor_tensor(y[:, :], turns_[:, :], C2PI - 2.0 * math.pi, y[:, :], ALU.mult, ALU.add))
                    nc.vector.tensor_scalar(y[:, :], y[:, :], 3.1415925, -3.1415925, ALU.min, ALU.max).then_inc(reduced, 1)
                for t in range(2):
                    for n in range(8):
                        d, o, half = n // 4, n // 2 % 2, n % 2
                        cols = slice(half * BANK, (half + 1) * BANK)
                        dve.wait_ge(filt_done, 8 * t + n + 1)
                        nc.vector.tensor_tensor(spectra[:, o, 2 * d + t, cols], k.ps[:, n, :], window[:, t, cols], ALU.mult).then_inc(filt_taken, 1)
                dve.wait_ge(filt_taken, 16)
                for o in range(ORDERS):
                    steps.then(nc.vector.tensor_tensor(power[:, o, :], spectra[:, o, 0, :], spectra[:, o, 0, :], ALU.mult))
                    for n in range(1, 4):
                        steps.then(nc.vector.tensor_tensor(sq[:, :], spectra[:, o, n, :], spectra[:, o, n, :], ALU.mult))
                        steps.then(nc.vector.tensor_tensor(power[:, o, :], power[:, o, :], sq[:, :], ALU.add))
                nc.vector.tensor_copy(sq[:, 0:1], power[:, 0, 0:1]).then_inc(squares, 1)
                dve.wait_ge(normed, 1)
                nc.vector.reciprocal(rstd[:, :], root[:, :])
                for o in range(ORDERS):
                    if o:
                        dve.wait_ge(spec_done, 8)
                    for t in range(2):
                        steps.done(nc.vector.scalar_tensor_tensor(even[:, t, :], spectra[:, o, 2 + t, :], first[:, t:t + 1], spectra[:, o, t, :], ALU.mult, ALU.add))
                    for t in range(2):
                        steps.then(nc.vector.tensor_scalar(spectra[:, o, 2 + t, :], spectra[:, o, 2 + t, :], first[:, t:t + 1], None, ALU.mult))
                        last = nc.vector.tensor_tensor(spectra[:, o, 2 + t, :], spectra[:, o, t, :], spectra[:, o, 2 + t, :], ALU.subtract)
                        steps.done(last) if t == 0 else last.then_inc(parts_ready, 1)


def stage_hyena_in(k, z):
    nc = k.nc
    taken, cleared, convolved = (sem(k, f"h_in_{n}") for n in ("taken", "cleared", "convolved"))
    first = START["h_in"]
    with ExitStack() as local:
        padded = local.enter_context(nc.sbuf_tensor("h_padded", [P, KC, T + 2], F32))
        with nc.Block() as block:
            @block.sync
            def _(sp):
                refill(k, sp, first, 3 * KC)

            @block.gpsimd
            def _(pool):
                nc.gpsimd.memset(padded[:, :, :], 0.0).then_inc(cleared, 1)

            @block.tensor
            def _(pe):
                for m in range(3 * KC):
                    slab = take_slab(k, pe, first + m)
                    if m >= 8:
                        pe.wait_ge(taken, m - 7)
                    slab_product(k, slab, lambda c: k.h[:, c, 0:T], k.ps[:, m % 8, 0:T])

            @block.scalar
            def _(act):
                act.wait_ge(cleared, 1)
                for m in range(3 * KC):
                    act.wait_ge(k.slab_used, first + m + 1)
                    if m >= KC:
                        act.wait_ge(convolved, m - KC + 1)
                    nc.scalar.activation(padded[:, m % KC, 1:T + 1], k.ps[:, m % 8, 0:T], ACT.Identity).then_inc(taken, 1)

            @block.vector
            def _(dve):
                steps = k.dve_steps.on(dve)
                w, b = k.s("h_conv_w"), k.s("h_conv_b")
                for m in range(3 * KC):
                    dve.wait_ge(taken, m + 1)
                    tap = lambda j: (padded[:, m % KC, j:j + T], w[:, j * 3 * KC + m:j * 3 * KC + m + 1])
                    steps.then(nc.vector.tensor_scalar(z[:, m, :], *tap(0), b[:, m:m + 1], ALU.mult, ALU.add))
                    steps.then(nc.vector.scalar_tensor_tensor(z[:, m, :], *tap(1), z[:, m, :], ALU.mult, ALU.add))
                    nc.vector.scalar_tensor_tensor(z[:, m, :], *tap(2), z[:, m, :], ALU.mult, ALU.add).then_inc(convolved, 1)


def stage_long_conv(k, o, spectra, rstd, z):
    nc = k.nc
    loaded, flipped, copied, spec_done, prod_ready, back_done, back_taken = (sem(k, f"conv{o}_{n}") for n in ("loaded", "flipped", "copied", "spec_done", "prod_ready", "back_done", "back_taken"))
    work = k.h[:, :, :].rearrange("p a b -> p (a b)")
    vt, ta, tb = work[:, 0:2 * D].rearrange("p (t d) -> p t d", t=2), work[:, 2 * D:3 * D], work[:, 3 * D:4 * D]
    v = z[:, 2 * KC:3 * KC, :]
    with ExitStack() as local:
        fc, fs, gc, gs = (local.enter_context(nc.sbuf_tensor(f"conv{o}_{n}", [P, 2, T], F32)) for n in ("fc", "fs", "gc", "gs"))
        prod = local.enter_context(nc.sbuf_tensor(f"conv{o}_prod", [P, 4, D], F32))
        tmp = local.enter_context(nc.sbuf_tensor(f"conv{o}_tmp", [P, 2, T], F32))
        with nc.Block() as block:
            @block.scalar
            def _(act):
                for dst, src in [(fc, "fc"), (fs, "fs"), (gc, "gc"), (gs, "gs")]:
                    act.dma_start(dst[:], k.dram[src]).then_inc(loaded, 16)
                for n in range(4):
                    act.wait_ge(flipped, n + 1)
                    nc.scalar.activation(vt[:, n // 2, (n % 2) * BANK:(n % 2 + 1) * BANK], k.ps[:, n, :], ACT.Identity).then_inc(copied, 1)
                act.wait_ge(loaded, 4 * 16)

            @block.tensor
            def _(pe):
                for n in range(4):
                    for c in range(4):
                        last = nc.tensor.transpose(k.ps[:, n, c * P:(c + 1) * P], v[:, (n % 2) * 4 + c, (n // 2) * P:(n // 2 + 1) * P], k.s("ident"))
                    last.then_inc(flipped, 1)
                pe.wait_ge(loaded, 4 * 16)
                pe.wait_ge(copied, 4)
                for f in range(2):
                    for part in range(2):
                        for half in range(2):
                            for t in range(2):
                                last = nc.tensor.matmul(k.ps[:, 4 * part + 2 * f + half, :], (fs if part else fc)[:, t, f * P:(f + 1) * P],
                                                        vt[:, t, half * BANK:(half + 1) * BANK], start=t == 0, stop=t == 1)
                    last.then_inc(spec_done, 1)
                pe.wait_ge(prod_ready, 2)
                for m in range(KC):
                    for n in range(4):
                        last = nc.tensor.matmul(k.ps[:, m, 0:T], prod[:, n, m * P:(m + 1) * P], (gs if n // 2 else gc)[:, n % 2, :], start=n == 0, stop=n == 3)
                    last.then_inc(back_done, 1)

            @block.vector
            def _(dve):
                steps = k.dve_steps.on(dve)
                for f in range(2):
                    dve.wait_ge(spec_done, f + 1)
                    re = k.ps[:, 2 * f:2 * f + 2, :].rearrange("p b n -> p (b n)")
                    im = k.ps[:, 4 + 2 * f:6 + 2 * f, :].rearrange("p b n -> p (b n)")
                    kre, kim = spectra[:, o, f, :], spectra[:, o, 2 + f, :]
                    steps.done(nc.vector.tensor_tensor(ta, re, kre, ALU.mult))
                    steps.then(nc.vector.tensor_tensor(tb, im, kim, ALU.mult))
                    steps.then(nc.vector.tensor_tensor(prod[:, f, :], ta, tb, ALU.subtract))
                    steps.done(nc.vector.tensor_tensor(ta, re, kim, ALU.mult))
                    steps.then(nc.vector.tensor_tensor(tb, im, kre, ALU.mult))
                    nc.vector.tensor_tensor(prod[:, 2 + f, :], ta, tb, ALU.add).then_inc(prod_ready, 1)
                    dve.wait_ge(prod_ready, f + 1)
                for m in range(KC):
                    n = o * KC + m
                    dve.wait_ge(back_done, m + 1)
                    steps.then(nc.vector.tensor_scalar(tmp[:, m % 2, :], k.ps[:, m, 0:T], rstd[:, n:n + 1], None, ALU.mult))
                    steps.then(nc.vector.scalar_tensor_tensor(tmp[:, m % 2, :], v[:, m, :], k.s("h_skip")[:, n:n + 1], tmp[:, m % 2, :], ALU.mult, ALU.add))
                    steps.then(nc.vector.tensor_tensor(v[:, m, :], tmp[:, m % 2, :], z[:, o * KC + m, :], ALU.mult))


def hyena_layer(k):
    nc = k.nc
    with ExitStack() as local:
        spectra = local.enter_context(nc.sbuf_tensor("h_spectra", [P, ORDERS, 4, D], F32))
        rstd = local.enter_context(nc.sbuf_tensor("h_rstd", [P, ORDERS * KC], F32))
        stage_filters(k, spectra, rstd)
        z = local.enter_context(nc.sbuf_tensor("h_z", [P, 3 * KC, T], F32))
        stage_norm(k, "h_norm", [(lambda c: k.x[:, c, :], 2, lambda c: k.h[:, c, 0:T])])
        stage_hyena_in(k, z)
        for o in range(ORDERS):
            stage_long_conv(k, o, spectra, rstd, z)
        stage_add_product(k, "h_out", "h_out", z[:, 2 * KC:3 * KC, :], 1, 2)


def stage_delta_qkv(k, qkv, gates):
    nc = k.nc
    cleared, taken, convolved, ba_done, silu_done = (sem(k, f"gq_{n}") for n in ("cleared", "taken", "convolved", "ba_done", "silu_done"))
    first, ba = START["g_qkv"], START["g_ba"]
    SLOTS = 4
    with ExitStack() as local:
        grid = local.enter_context(nc.sbuf_tensor("g_grid", [P, SLOTS, ROWS + 2, GRID_W + 2], F32))
        line = local.enter_context(nc.sbuf_tensor("g_line", [P, SLOTS, T + 2], F32))
        with nc.Block() as block:
            @block.sync
            def _(sp):
                refill(k, sp, first, QKV_CHUNKS + 1)

            @block.gpsimd
            def _(pool):
                nc.gpsimd.memset(grid[:, :, :, :], 0.0).then_inc(cleared, 1)
                nc.gpsimd.memset(line[:, :, :], 0.0).then_inc(cleared, 1)

            @block.tensor
            def _(pe):
                for m in range(QKV_CHUNKS):
                    slab = take_slab(k, pe, first + m)
                    if m >= 7:
                        pe.wait_ge(taken, m - 6)
                    slab_product(k, slab, lambda c: k.h[:, c, :], k.ps[:, m % 7, :])
                w = take_slab(k, pe, ba).rearrange("p (k c) -> p k c", k=KC)
                for b in range(4):
                    for c in range(KC):
                        last = nc.tensor.matmul(k.ps[:, 7, b * 32:(b + 1) * 32], k.h[:, c, b * P:(b + 1) * P], w[:, c, 0:32], start=c == 0, stop=c == KC - 1)
                last.then_inc(k.slab_used, 1)

            @block.scalar
            def _(act):
                act.wait_ge(cleared, 2)

                def silu(m):
                    act.wait_ge(convolved, m + 1)
                    nc.scalar.activation(qkv[:, m, :], qkv[:, m, :], ACT.Silu).then_inc(silu_done, 1)

                for m in range(QKV_CHUNKS):
                    act.wait_ge(k.slab_used, first + m + 1)
                    if m >= SLOTS:
                        act.wait_ge(convolved, m - SLOTS + 1)
                    nc.scalar.activation(grid[:, m % SLOTS, 1:ROWS + 1, 1:GRID_W + 1],
                                         k.ps[:, m % 7, 0:T].rearrange("p (r c) -> p r c", r=ROWS), ACT.Identity)
                    nc.scalar.activation(line[:, m % SLOTS, 1:T + 1], k.ps[:, m % 7, T:T2], ACT.Identity).then_inc(taken, 1)
                    if m >= 2:
                        silu(m - 2)
                silu(QKV_CHUNKS - 2)
                silu(QKV_CHUNKS - 1)

            @block.vector
            def _(dve):
                steps = k.dve_steps.on(dve)
                w = k.s("g_conv_w")
                for m in range(QKV_CHUNKS):
                    lat = qkv[:, m, 0:T].rearrange("p (r c) -> p r c", r=ROWS)
                    ctx = qkv[:, m, T:T2]
                    tap = lambda dy, dx: w[:, (3 * dy + dx) * QKV_CHUNKS + m:(3 * dy + dx) * QKV_CHUNKS + m + 1]
                    dve.wait_ge(taken, m + 1)
                    for n in range(9):
                        dy, dx = n // 3, n % 3
                        src = grid[:, m % SLOTS, dy:dy + ROWS, dx:dx + GRID_W]
                        if n == 0:
                            steps.done(nc.vector.tensor_scalar(lat, src, tap(dy, dx), None, ALU.mult))
                            steps.then(nc.vector.tensor_scalar(ctx, line[:, m % SLOTS, 0:T], tap(1, 0), None, ALU.mult))
                        else:
                            last = nc.vector.scalar_tensor_tensor(lat, src, tap(dy, dx), lat, ALU.mult, ALU.add)
                            if n in (4, 6):
                                steps.done(last)
                                j = n // 2 - 1
                                steps.then(nc.vector.scalar_tensor_tensor(ctx, line[:, m % SLOTS, j:j + T], tap(1, j), ctx, ALU.mult, ALU.add))
                            elif n < 8:
                                steps.then(last)
                            else:
                                last.then_inc(convolved, 1)
                dve.wait_ge(k.slab_used, ba + 1)
                nc.vector.tensor_copy(gates[:, :, :], k.ps[:, 7, 0:P].rearrange("p (b n) -> p b n", b=4))


def stage_delta_norm(k, qkv):
    nc = k.nc
    squared, total, root = (sem(k, f"gl_{n}") for n in ("squared", "total", "root"))
    heads = 2 * NQK
    with ExitStack() as local:
        sq = local.enter_context(nc.sbuf_tensor("gl_sq", [P, heads, T2], F32))
        with nc.Block() as block:
            @block.scalar
            def _(act):
                for c in range(heads):
                    nc.scalar.activation(sq[:, c, :], qkv[:, c, :], ACT.Square).then_inc(squared, 1)
                for c in range(heads):
                    act.wait_ge(total, c + 1)
                    nc.scalar.activation(sq[:, c, :], k.ps[:, c, :], ACT.Sqrt, bias=k.s("eps")).then_inc(root, 1)

            @block.tensor
            def _(pe):
                for c in range(heads):
                    pe.wait_ge(squared, c + 1)
                    nc.tensor.matmul(k.ps[:, c, :], k.s("ones"), sq[:, c, :], start=True, stop=True).then_inc(total, 1)

            @block.vector
            def _(dve):
                steps = k.dve_steps.on(dve)
                for c in range(heads):
                    dve.wait_ge(root, c + 1)
                    steps.then(nc.vector.reciprocal(sq[:, c, :], sq[:, c, :]))
                    nc.vector.scalar_tensor_tensor(qkv[:, c, :], qkv[:, c, :], P ** -0.5 if c < NQK else 1.0, sq[:, c, :], ALU.mult, ALU.mult)


def stage_delta_turn(k, qkv, g):
    nc = k.nc
    flipped, copied, logs_ready, sums_done = (sem(k, f"gt_{n}") for n in ("flipped", "copied", "logs_ready", "sums_done"))
    chunks = list(range(NQK, QKV_CHUNKS))
    banks = [(b, c) for b in range(4) for c in range(0, len(chunks), 4)]
    with ExitStack() as local:
        def sb(name, shape):
            return local.enter_context(nc.sbuf_tensor(f"gt_{name}", shape, F32))
        raw, soft, rate = sb("raw", [P, 4, 2 * NV]), sb("soft", [P, 4, 2 * NV]), sb("rate", [P, 2 * NV])
        with nc.Block() as block:
            @block.tensor
            def _(pe):
                for n, (b, c) in enumerate(banks):
                    if n >= 6:
                        pe.wait_ge(copied, n - 5)
                    for i in range(4):
                        last = nc.tensor.transpose(k.ps[:, n % 6, i * P:(i + 1) * P], qkv[:, chunks[c + i], b * P:(b + 1) * P], k.s("ident"))
                    last.then_inc(flipped, 1)
                pe.wait_ge(logs_ready, 1)
                for d in range(2):
                    src = g.log[:, d, :]
                    nc.tensor.matmul(k.ps[:, 6, d * 32:(d + 1) * 32], k.s("tri")[:, d * P:(d + 1) * P], src, start=True, stop=True)
                    last = nc.tensor.matmul(k.ps[:, 7, d * 32:(d + 1) * 32], k.s("ones"), src, start=True, stop=True)
                last.then_inc(sums_done, 1)

            @block.scalar
            def _(act):
                steps = k.act_steps.on(act)
                for n, (b, c) in enumerate(banks):
                    dst = g.k_tok[:, b, :] if c == 0 else g.v_tok[:, b, (c // 4 - 1) * BANK:c // 4 * BANK]
                    act.wait_ge(flipped, n + 1)
                    nc.scalar.activation(dst, k.ps[:, n % 6, :], ACT.Identity).then_inc(copied, 1)
                steps.done(nc.scalar.activation(rate[:, :], k.s("a_log"), ACT.Exp))
                act.wait_ge(g.raw_ready, 1)
                steps.then(nc.scalar.activation(soft[:, :, :], raw[:, :, :], ACT.Abs))
                steps.then(nc.scalar.activation(soft[:, :, :], soft[:, :, :], ACT.Exp, scale=-1.0))
                nc.scalar.activation(soft[:, :, :], soft[:, :, :], ACT.Ln, bias=k.s("one")).then_inc(g.soft_ready, 1)
                for d in range(2):
                    last = nc.scalar.activation(g.beta[:, d, :].rearrange("p (b h) -> p b h", b=4), g.gates[:, :, d * NV:(d + 1) * NV], ACT.Sigmoid)
                last.then_inc(g.beta_ready, 1)
                act.wait_ge(g.cum_ready, 1)
                nc.scalar.activation(g.from_start[:, :, :], g.cum[:, :, :], ACT.Exp).then_inc(g.start_ready, 1)
                act.wait_ge(g.cum_ready, 2)
                nc.scalar.activation(g.end[:, :, :], g.end[:, :, :], ACT.Exp)
                steps.then(nc.scalar.activation(g.to_end[:, :, :], g.to_end[:, :, :], ACT.Exp))

            @block.vector
            def _(dve):
                steps = k.dve_steps.on(dve)
                for b in range(4):
                    last = nc.vector.tensor_tensor(raw[:, b, :], g.gates[:, b, 2 * NV:4 * NV], k.s("dt_bias"), ALU.add)
                last.then_inc(g.raw_ready, 1)
                dve.wait_ge(g.soft_ready, 1)
                steps.then(nc.vector.scalar_tensor_tensor(soft[:, :, :], raw[:, :, :], 0.0, soft[:, :, :], ALU.max, ALU.add))
                for d in range(2):
                    for b in range(4):
                        last = nc.vector.scalar_tensor_tensor(g.log[:, d, b * NV:(b + 1) * NV], soft[:, b, d * NV:(d + 1) * NV], -1.0,
                                                              rate[:, d * NV:(d + 1) * NV], ALU.mult, ALU.mult)
                last.then_inc(logs_ready, 1)
                dve.wait_ge(sums_done, 1)
                nc.vector.tensor_copy(g.end[:, :, :].rearrange("p d n -> p (d n)"), k.ps[:, 7, 0:64])
                nc.vector.tensor_copy(g.cum[:, :, :].rearrange("p d n -> p (d n)"), k.ps[:, 6, 0:64]).then_inc(g.cum_ready, 1)
                dve.wait_ge(g.cum_ready, 1)
                nc.vector.tensor_tensor(g.to_end[:, :, :], g.end[:, :, :], g.cum[:, :, :], ALU.subtract).then_inc(g.cum_ready, 1)
                dve.wait_ge(g.start_ready, 1)
                dve.wait_ge(g.beta_ready, 1)
                nc.vector.scalar_tensor_tensor(g.erase[:, :, :], g.beta[:, :, :], -1.0, g.from_start[:, :, :], ALU.mult, ALU.mult)


def stage_delta_solve(k, d, qkv, g):
    nc = k.nc
    gram_done, gram_taken, rows_ready, sums_done, gaps_ready, decay_ready, lower_ready, prod_done, prod_ready, step_done, step_ready, pairs_ready = (
        sem(k, f"gs{d}_{n}") for n in ("gram_done", "gram_taken", "rows_ready", "sums_done", "gaps_ready", "decay_ready", "lower_ready",
                                       "prod_done", "prod_ready", "step_done", "step_ready", "pairs_ready"))
    S, U = 2, 4
    tri, strict = k.s("tri")[:, d * P:(d + 1) * P], k.s("strict")[:, d * P:(d + 1) * P]
    level = lambda dd, n: k.s("level")[:, (dd * LEVELS + n) * P:(dd * LEVELS + n + 1) * P]
    wide = lambda m: m.unsqueeze(1).broadcast_to([P, U, P])
    with ExitStack() as local:
        def sb(name, shape):
            return local.enter_context(nc.sbuf_tensor(f"gs{d}_{name}", shape, F32))
        gram, mixed = sb("gram", [P, 4 * NQK, P]), sb("mixed", [P, 2 * NQK, P])
        rows, fall, rise = sb("rows", [P, S, U, P]), sb("fall", [P, S, U, P]), sb("rise", [P, S, U, P])
        low, prod, inv, inv_t = sb("low", [P, S, U, P]), sb("prod", [P, S, U, P]), sb("inv", [P, S, U, P]), sb("inv_t", [P, S, U, P])

        def bank(n):
            return k.ps[:, n, :].rearrange("p (u t) -> p u t", u=U)

        with nc.Block() as block:
            @block.tensor
            def _(pe):
                for b in range(4):
                    for h in range(NQK):
                        kt = qkv[:, NQK + h, b * P:(b + 1) * P]
                        last = nc.tensor.matmul(k.ps[:, b, h * P:(h + 1) * P], kt, kt, start=True, stop=True)
                    last.then_inc(gram_done, 1)
                for b in range(2):
                    for h in range(NQK):
                        last = nc.tensor.matmul(k.ps[:, 4 + b, h * P:(h + 1) * P], qkv[:, NQK + h, b * P:(b + 1) * P], qkv[:, h, b * P:(b + 1) * P], start=True, stop=True)
                    last.then_inc(gram_done, 1)
                pe.wait_ge(gram_taken, 6)

                def block_of(t):
                    for s in range(S):
                        pe.wait_ge(rows_ready, t * S + s + 1)
                        nc.tensor.matmul(k.ps[:, s, :], k.s("ones"), rows[:, s, :, :].rearrange("p u t -> p (u t)"), start=True, stop=True).then_inc(sums_done, 1)
                    for n in range(LEVELS):
                        for s in range(S):
                            if n == 0:
                                pe.wait_ge(lower_ready, t * S + s + 1)
                            else:
                                pe.wait_ge(step_ready, t * S * LEVELS + (n - 1) * S + s + 2)
                            for u in range(U):
                                last = nc.tensor.matmul(k.ps[:, 2 + s, u * P:(u + 1) * P], low[:, s, u, :], k.s("ident") if n == 0 else inv_t[:, s, u, :], start=True, stop=True)
                            last.then_inc(prod_done, 1)
                        if n == 0:
                            continue
                        for s in range(S):
                            pe.wait_ge(prod_ready, t * S * LEVELS + n * S + s + 1)
                            for u in range(U):
                                last = nc.tensor.matmul(k.ps[:, 4 + s, u * P:(u + 1) * P], inv[:, s, u, :], prod[:, s, u, :], start=True, stop=True)
                            if n < LEVELS - 1:
                                for u in range(U):
                                    last = nc.tensor.matmul(k.ps[:, 6 + s, u * P:(u + 1) * P], prod[:, s, u, :], inv[:, s, u, :], start=True, stop=True)
                            last.then_inc(step_done, 1)

                with pe.Fori(0, 4) as t:
                    block_of(t)

            @block.scalar
            def _(act):
                def block_of(t):
                    for s in range(S):
                        for u in range(U):
                            col = g.log[:, d, bass.ds(t * NV + s * U + u, 1)]
                            last = nc.scalar.activation(rows[:, s, u, :], tri, ACT.Identity, scale=col)
                        last.then_inc(rows_ready, 1)
                    for s in range(S):
                        act.wait_ge(gaps_ready, t * S + s + 1)
                        nc.scalar.activation(fall[:, s, :, :], fall[:, s, :, :], ACT.Exp, scale=-1.0)
                        nc.scalar.activation(rise[:, s, :, :], rise[:, s, :, :], ACT.Exp).then_inc(decay_ready, 1)

                with act.Fori(0, 4) as t:
                    act.wait_ge(step_ready, t * S * LEVELS + 1)
                    block_of(t)

            @block.vector
            def _(dve):
                for b in range(4):
                    dve.wait_ge(gram_done, b + 1)
                    nc.vector.tensor_tensor(gram[:, b * NQK:(b + 1) * NQK, :], bank(b), strict.unsqueeze(1).broadcast_to([P, NQK, P]), ALU.mult).then_inc(gram_taken, 1)
                for b in range(2):
                    dve.wait_ge(gram_done, 4 + b + 1)
                    nc.vector.tensor_tensor(mixed[:, b * NQK:(b + 1) * NQK, :], bank(4 + b), tri.unsqueeze(1).broadcast_to([P, NQK, P]), ALU.mult).then_inc(gram_taken, 1)
                dve.wait_ge(gram_taken, 6)
                dve.sem_inc(step_ready, 1)

                def block_of(t, latents):
                    for s in range(S):
                        dve.wait_ge(sums_done, t * S + s + 1)
                        for u in range(U):
                            col = g.cum[:, d, bass.ds(t * NV + s * U + u, 1)]
                            nc.vector.tensor_scalar(fall[:, s, u, :], bank(s)[:, u, :], col, 0.0, ALU.subtract, ALU.max)
                            last = nc.vector.tensor_scalar(rise[:, s, u, :], bank(s)[:, u, :], col, 0.0, ALU.subtract, ALU.min)
                        last.then_inc(gaps_ready, 1)
                    for s in range(S):
                        dve.wait_ge(decay_ready, t * S + s + 1)
                        for u in range(U):
                            col = g.beta[:, d, bass.ds(t * NV + s * U + u, 1)]
                            kk = gram[:, bass.ds(t * NQK + (s * U + u) // 2, 1), :].rearrange("p a t -> p (a t)")
                            last = nc.vector.scalar_tensor_tensor(low[:, s, u, :], fall[:, s, u, :], col, kk, ALU.mult, ALU.mult)
                        last.then_inc(lower_ready, 1)
                        if latents:
                            for u in range(U):
                                qk = mixed[:, bass.ds(t * NQK + (s * U + u) // 2, 1), :].rearrange("p a t -> p (a t)")
                                out = g.qk[:, bass.ds(t * NV + s * U + u, 1), :].rearrange("p a t -> p (a t)")
                                nc.vector.tensor_tensor(out, rise[:, s, u, :], qk, ALU.mult)
                    for s in range(S):
                        dve.wait_ge(lower_ready, t * S + s + 1)
                        nc.vector.tensor_tensor(inv[:, s, :, :], low[:, s, :, :], wide(level(1 - d, 0)), ALU.mult).then_inc(pairs_ready, 1)
                    for n in range(LEVELS):
                        for s in range(S):
                            dve.wait_ge(prod_done, t * S * LEVELS + n * S + s + 1)
                            nc.vector.tensor_tensor(prod[:, s, :, :], bank(2 + s), wide(level(d, n)), ALU.mult).then_inc(prod_ready, 1)
                        for s in range(S):
                            if n == 0:
                                dve.wait_ge(prod_ready, t * S * LEVELS + s + 1)
                                dve.wait_ge(pairs_ready, t * S + s + 1)
                                nc.vector.tensor_tensor(inv_t[:, s, :, :], wide(k.s("ident")), prod[:, s, :, :], ALU.subtract)
                                nc.vector.tensor_tensor(inv[:, s, :, :], wide(k.s("ident")), inv[:, s, :, :], ALU.subtract).then_inc(step_ready, 1)
                                continue
                            dve.wait_ge(step_done, t * S * (LEVELS - 1) + (n - 1) * S + s + 1)
                            if n < LEVELS - 1:
                                nc.vector.tensor_tensor(inv_t[:, s, :, :], inv_t[:, s, :, :], bank(4 + s), ALU.subtract)
                                nc.vector.tensor_tensor(inv[:, s, :, :], inv[:, s, :, :], bank(6 + s), ALU.subtract).then_inc(step_ready, 1)
                            else:
                                out = g.inv_t[:, bass.ds(t * NV + s * U, U), :]
                                nc.vector.tensor_tensor(out, inv_t[:, s, :, :], bank(4 + s), ALU.subtract).then_inc(step_ready, 1)

                with dve.Fori(0, 2) as t:
                    block_of(t, True)
                with dve.Fori(2, 4) as t:
                    block_of(t, False)


def stage_delta_scan(k, d, qkv, g):
    nc = k.nc
    cleared, asked, scaled, rest_ready, solved, written, updated, state_ready, out_done, out_taken = (sem(k, f"gc{d}_{n}") for n in ("cleared", "asked", "scaled", "rest_ready", "solved", "written", "updated", "state_ready", "out_done", "out_taken"))
    S, U = 2, 4
    blocks = [2, 3, 0, 1] if d == 0 else [3, 2, 1, 0]
    units = [(n, b, s) for n, b in enumerate(blocks) for s in range(S)]
    with ExitStack() as local:
        def sb(name, shape):
            return local.enter_context(nc.sbuf_tensor(f"gc{d}_{name}", shape, F32))
        state, bv, kd, rest, write = sb("state", [P, NV, P]), sb("bv", [P, S, U, P]), sb("kd", [P, S, U, P]), sb("rest", [P, S, U, P]), sb("write", [P, S, U, P])
        with nc.Block() as block:
            @block.gpsimd
            def _(pool):
                nc.gpsimd.memset(state[:, :, :], 0.0).then_inc(cleared, 1)

            @block.tensor
            def _(pe):
                pe.wait_ge(cleared, 1)
                for n, b in enumerate(blocks):
                    for s in range(S):
                        i = n * S + s
                        if n:
                            pe.wait_ge(state_ready, i - S + 1)
                        for u in range(U):
                            h = s * U + u
                            last = nc.tensor.matmul(k.ps[:, s, u * P:(u + 1) * P], qkv[:, NQK + h // 2, b * P:(b + 1) * P], state[:, h, :], start=True, stop=True)
                        last.then_inc(asked, 1)
                    for s in range(S):
                        i = n * S + s
                        pe.wait_ge(rest_ready, i + 1)
                        for u in range(U):
                            last = nc.tensor.matmul(k.ps[:, 2 + s, u * P:(u + 1) * P], g.inv_t[:, b * NV + s * U + u, :], rest[:, s, u, :], start=True, stop=True)
                        last.then_inc(solved, 1)
                    if n >= 2:
                        for s in range(S):
                            j = (n - 2) * S + s
                            if j:
                                pe.wait_ge(out_taken, 2 * j)
                            for u in range(U):
                                h = s * U + u
                                last = nc.tensor.matmul(k.ps[:, 6, u * P:(u + 1) * P], qkv[:, h // 2, b * P:(b + 1) * P], state[:, h, :], start=True, stop=True)
                            last.then_inc(out_done, 1)
                            pe.wait_ge(written, n * S + s + 1)
                            for u in range(U):
                                last = nc.tensor.matmul(k.ps[:, 7, u * P:(u + 1) * P], g.qk[:, b * NV + s * U + u, :], write[:, s, u, :], start=True, stop=True)
                            last.then_inc(out_done, 1)
                    if n < 3:
                        for s in range(S):
                            i = n * S + s
                            pe.wait_ge(written, i + 1)
                            for u in range(U):
                                last = nc.tensor.matmul(k.ps[:, 4 + s, u * P:(u + 1) * P], kd[:, s, u, :], write[:, s, u, :], start=True, stop=True)
                            last.then_inc(updated, 1)

            @block.scalar
            def _(act):
                def scale(i):
                    n, b, s = units[i]
                    if n:
                        act.wait_ge(updated, i - S + 1)
                        act.wait_ge(rest_ready, i - S + 1)
                    for u in range(U):
                        h = s * U + u
                        col = b * NV + h
                        nc.scalar.activation(bv[:, s, u, :], g.v_tok[:, b, h * P:(h + 1) * P], ACT.Identity, scale=g.beta[:, d, col:col + 1])
                        last = nc.scalar.activation(kd[:, s, u, :], g.k_tok[:, b, h // 2 * P:(h // 2 + 1) * P], ACT.Identity, scale=g.to_end[:, d, col:col + 1])
                    last.then_inc(scaled, 1)

                scale(0)
                scale(1)
                for n in range(len(blocks)):
                    for s in range(S):
                        act.wait_ge(solved, n * S + s + 1)
                        if n >= 3:
                            act.wait_ge(out_done, 4 * (n - 2))
                        nc.scalar.activation(write[:, s, :, :], k.ps[:, 2 + s, :].rearrange("p (u t) -> p u t", u=U), ACT.Identity).then_inc(written, 1)
                    if n < 3:
                        scale((n + 1) * S)
                        scale((n + 1) * S + 1)

            @block.vector
            def _(dve):
                steps = k.dve_steps.on(dve)
                for n, b in enumerate(blocks):
                    for s in range(S):
                        i = n * S + s
                        dve.wait_ge(asked, i + 1)
                        dve.wait_ge(scaled, i + 1)
                        for u in range(U):
                            col = b * NV + s * U + u
                            last = nc.vector.scalar_tensor_tensor(rest[:, s, u, :], k.ps[:, s, u * P:(u + 1) * P], g.erase[:, d, col:col + 1], bv[:, s, u, :], ALU.mult, ALU.add)
                        last.then_inc(rest_ready, 1)
                    if n >= 2:
                        for s in range(S):
                            j = (n - 2) * S + s
                            cols = slice(s * U * P, (s + 1) * U * P)
                            dve.wait_ge(out_done, 2 * j + 1)
                            for u in range(U):
                                h = s * U + u
                                col, o = b * NV + h, g.o[:, b, h * P:(h + 1) * P]
                                if d == 0:
                                    last = nc.vector.tensor_scalar(o, k.ps[:, 6, u * P:(u + 1) * P], g.from_start[:, d, col:col + 1], None, ALU.mult)
                                else:
                                    last = nc.vector.scalar_tensor_tensor(o, k.ps[:, 6, u * P:(u + 1) * P], g.from_start[:, d, col:col + 1], o, ALU.mult, ALU.add)
                            last.then_inc(out_taken, 1)
                            dve.wait_ge(out_taken, 2 * j + 1)
                            dve.wait_ge(out_done, 2 * j + 2)
                            nc.vector.tensor_tensor(g.o[:, b, cols], g.o[:, b, cols], k.ps[:, 7, :], ALU.add).then_inc(out_taken, 1)
                    if n < 3:
                        for s in range(S):
                            i = n * S + s
                            dve.wait_ge(updated, i + 1)
                            if n == 2:
                                dve.wait_ge(out_done, 4)
                            for u in range(U):
                                h = s * U + u
                                col = b * NV + h
                                last = nc.vector.scalar_tensor_tensor(state[:, h, :], state[:, h, :], g.end[:, d, col:col + 1], k.ps[:, 4 + s, u * P:(u + 1) * P], ALU.mult, ALU.add)
                            last.then_inc(state_ready, 1)


def stage_fourier(k, ya):
    nc = k.nc
    taken, mid_done, mid_taken, four_done, four_taken, out_done, out_taken = (sem(k, f"ff_{n}") for n in ("taken", "mid_done", "mid_taken", "four_done", "four_taken", "out_done", "out_taken"))
    first, fout = START["g_f"], START["g_fout"]
    with ExitStack() as local:
        ft = local.enter_context(nc.sbuf_tensor("ff_ft", [P, F_GROUPS, T], F32))
        mid = local.enter_context(nc.sbuf_tensor("ff_mid", [P, F_GROUPS, 2, 2 * P], F32))
        out = local.enter_context(nc.sbuf_tensor("ff_out", [P, F_GROUPS, T], F32))
        four_t = k.s("four_t").rearrange("p (a c t) -> p a c t", a=2, c=2)
        with nc.Block() as block:
            @block.sync
            def _(sp):
                refill(k, sp, first, 2 * F_GROUPS)

            @block.tensor
            def _(pe):
                for m in range(F_GROUPS):
                    slab_product(k, take_slab(k, pe, first + m), lambda c: k.h[:, c, 0:T], k.ps[:, m, 0:T])
                for m in range(F_GROUPS):
                    pe.wait_ge(taken, m + 1)
                    for b in range(2):
                        last = nc.tensor.matmul(k.ps[:, 4 + m, b * T:(b + 1) * T], ft[:, m, b * P:(b + 1) * P], k.s("four_g"), start=True, stop=True)
                    last.then_inc(mid_done, 1)
                for m in range(F_GROUPS):
                    pe.wait_ge(mid_taken, m + 1)
                    for n in range(4):
                        part, b = n // 2, n % 2
                        last = nc.tensor.matmul(k.ps[:, m, 0:T], mid[:, m, b, part * P:(part + 1) * P], four_t[:, part, b, :], start=n == 0, stop=n == 3)
                    last.then_inc(four_done, 1)
                pe.wait_ge(four_taken, F_GROUPS)
                for m in range(KC):
                    w = take_slab(k, pe, fout + m // 2).rearrange("p (k c) -> p k c", k=F_GROUPS)
                    for c in range(F_GROUPS):
                        last = nc.tensor.matmul(k.ps[:, m, 0:T], w[:, c, (m % 2) * P:(m % 2 + 1) * P], out[:, c, :], start=c == 0, stop=c == F_GROUPS - 1)
                    last.then_inc(k.slab_used if m % 2 else out_done, 1)

            @block.vector
            def _(dve):
                for m in range(F_GROUPS):
                    dve.wait_ge(k.slab_used, first + m + 1)
                    nc.vector.tensor_copy(ft[:, m, :], k.ps[:, m, 0:T]).then_inc(taken, 1)
                for m in range(F_GROUPS):
                    dve.wait_ge(mid_done, m + 1)
                    nc.vector.tensor_copy(mid[:, m, :, :].rearrange("p b n -> p (b n)"), k.ps[:, 4 + m, :]).then_inc(mid_taken, 1)
                for m in range(F_GROUPS):
                    dve.wait_ge(four_done, m + 1)
                    nc.vector.tensor_copy(out[:, m, :], k.ps[:, m, 0:T]).then_inc(four_taken, 1)
                for m in range(KC):
                    dve.wait_ge(k.slab_used if m % 2 else out_done, fout + m // 2 + 1 if m % 2 else m // 2 + 1)
                    nc.vector.tensor_copy(ya[:, m, :], k.ps[:, m, 0:T])


def stage_delta_out(k, g, yb):
    nc = k.nc
    squared, root, normed, flipped, silu_done, taken = (sem(k, f"go_{n}") for n in ("squared", "root", "normed", "flipped", "silu_done", "taken"))
    first = START["g_z"]
    with ExitStack() as local:
        sq = local.enter_context(nc.sbuf_tensor("go_sq", [P, 2 * D], F32))
        stat = local.enter_context(nc.sbuf_tensor("go_stat", [P, 3, 2 * NV], F32))
        with nc.Block() as block:
            @block.sync
            def _(sp):
                refill(k, sp, first, KC)

            @block.tensor
            def _(pe):
                for m in range(KC):
                    slab = take_slab(k, pe, first + m)
                    if m >= 4:
                        pe.wait_ge(silu_done, m - 3)
                    slab_product(k, slab, lambda c: k.h[:, c, 0:T], k.ps[:, m % 4, 0:T])
                pe.wait_ge(normed, 1)
                for m in range(KC):
                    if m >= 4:
                        pe.wait_ge(taken, m - 3)
                    for b in range(2):
                        last = nc.tensor.transpose(k.ps[:, 4 + m % 4, b * P:(b + 1) * P], g.o[:, b, m * P:(m + 1) * P], k.s("ident"))
                    last.then_inc(flipped, 1)

            @block.scalar
            def _(act):
                for b in range(2):
                    for h in range(NV):
                        n = b * NV + h
                        last = nc.scalar.activation(sq[:, n * P:(n + 1) * P], g.o[:, b, h * P:(h + 1) * P], ACT.Square, accum_out=stat[:, 0, n:n + 1])
                        last.then_inc(squared, 1)
                act.wait_ge(squared, 2 * NV)
                nc.scalar.activation(stat[:, 1, :], stat[:, 0, :], ACT.Sqrt, scale=1.0 / P, bias=k.s("eps")).then_inc(root, 1)
                for m in range(KC):
                    act.wait_ge(k.slab_used, first + m + 1)
                    nc.scalar.activation(yb[:, m, :], k.ps[:, m % 4, 0:T], ACT.Silu).then_inc(silu_done, 1)

            @block.vector
            def _(dve):
                steps = k.dve_steps.on(dve)
                dve.wait_ge(root, 1)
                steps.then(nc.vector.reciprocal(stat[:, 2, :], stat[:, 1, :]))
                for b in range(2):
                    for h in range(NV):
                        n = b * NV + h
                        last = nc.vector.tensor_scalar(g.o[:, b, h * P:(h + 1) * P], g.o[:, b, h * P:(h + 1) * P], stat[:, 2, n:n + 1], None, ALU.mult)
                last.then_inc(normed, 1)
                for m in range(KC):
                    dve.wait_ge(flipped, m + 1)
                    dve.wait_ge(silu_done, m + 1)
                    nc.vector.scalar_tensor_tensor(yb[:, m, :], k.ps[:, 4 + m % 4, 0:T], k.s("gdn_g"), yb[:, m, :], ALU.mult, ALU.mult).then_inc(taken, 1)


def stage_merge(k, ya, yb):
    nc = k.nc
    gated, merged = (sem(k, f"gm_{n}") for n in ("gated", "merged"))
    first, ga, gb = START["g_out"], START["g_ga"], START["g_gb"]
    with ExitStack() as local:
        gate = local.enter_context(nc.sbuf_tensor("gm_gate", [P, 2, KC, T], F32))
        with nc.Block() as block:
            @block.sync
            def _(sp):
                refill(k, sp, first, 3 * KC)

            @block.tensor
            def _(pe):
                for m in range(KC):
                    slab_product(k, take_slab(k, pe, first + m), lambda c: yb[:, c, :], k.ps[:, m // 2, (m % 2) * T:(m % 2 + 1) * T])
                for n in range(2 * KC):
                    if n >= 4:
                        pe.wait_ge(gated, n - 3)
                    slab_product(k, take_slab(k, pe, ga + n), lambda c: k.h[:, c, 0:T], k.ps[:, 4 + n % 4, 0:T])

            @block.scalar
            def _(act):
                for n in range(2 * KC):
                    act.wait_ge(k.slab_used, ga + n + 1)
                    nc.scalar.activation(gate[:, n // KC, n % KC, :], k.ps[:, 4 + n % 4, 0:T], ACT.Sigmoid).then_inc(gated, 1)

            @block.vector
            def _(dve):
                steps = k.dve_steps.on(dve)
                for m in range(KC):
                    dve.wait_ge(gated, m + 1)
                    steps.done(nc.vector.tensor_tensor(ya[:, m, :], ya[:, m, :], gate[:, 0, m, :], ALU.mult))
                for m in range(KC):
                    dve.wait_ge(gated, KC + m + 1)
                    steps.then(nc.vector.tensor_tensor(gate[:, 1, m, :], k.ps[:, m // 2, (m % 2) * T:(m % 2 + 1) * T], gate[:, 1, m, :], ALU.mult))
                    nc.vector.tensor_tensor(ya[:, m, :], ya[:, m, :], gate[:, 1, m, :], ALU.add)


def delta_layer(k):
    nc = k.nc
    with ExitStack() as local:
        def sb(name, shape):
            return local.enter_context(nc.sbuf_tensor(f"g_{name}", shape, F32))
        g = Core()
        g.o = sb("o", [P, 2, D])
        with ExitStack() as inner:
            def sbi(name, shape):
                return inner.enter_context(nc.sbuf_tensor(f"g_{name}", shape, F32))
            g.k_tok, g.v_tok = sbi("k_tok", [P, 4, NQK * P]), sbi("v_tok", [P, 4, NV * P])
            g.gates = sbi("gates", [P, 4, 4 * NV])
            g.log, g.cum, g.beta, g.end, g.from_start, g.to_end, g.erase = (
                sbi(n, [P, 2, 4 * NV]) for n in ("log", "cum", "beta", "end", "from_start", "to_end", "erase"))
            g.raw_ready, g.soft_ready, g.beta_ready, g.cum_ready, g.start_ready = (
                sem(k, f"gt_{n}") for n in ("raw_ready", "soft_ready", "beta_ready", "cum_ready", "start_ready"))
            qkv = sbi("qkv", [P, QKV_CHUNKS, T2])
            with ExitStack() as first:
                ctx = first.enter_context(nc.sbuf_tensor("g_ctx", [P, KC, T], F32))
                loaded = sem(k, "g_ctx_loaded")
                with nc.Block() as block:
                    @block.scalar
                    def _(act):
                        act.dma_start(ctx[:, :, :], k.x_dram[2]).then_inc(loaded, 16)
                        act.wait_ge(loaded, 16)
                stage_norm(k, "final0", [(lambda c: k.x[:, c, :], None, lambda c: k.x[:, c, :])], KC, k.s("norm_g")[:, 4 * KC:5 * KC])
                stage_norm(k, "g_norm", [(lambda c: k.x[:, c, :], 4, lambda c: k.h[:, c, 0:T]),
                                         (lambda c: ctx[:, c, :], 5, lambda c: k.h[:, c, T:T2])])
            stage_delta_qkv(k, qkv, g.gates)
            stage_delta_norm(k, qkv)
            stage_delta_turn(k, qkv, g)
            g.inv_t = qkv[:, 2 * NQK:QKV_CHUNKS, :].rearrange("p c (a t) -> p (c a) t", t=P)
            g.qk = sbi("qk", [P, 2 * NV, P])
            for d in range(2):
                stage_delta_solve(k, d, qkv, g)
                stage_delta_scan(k, d, qkv, g)
        ya, yb = sb("ya", [P, KC, T]), sb("yb", [P, KC, T])
        stage_fourier(k, ya)
        stage_delta_out(k, g, yb)
        stage_merge(k, ya, yb)
        stage_add_product(k, "g_merge", "g_merge", ya, 2, 2)


def stage_router(k, weights):
    nc = k.nc
    less, exped, flipped, weighed, summed = (sem(k, f"rt_{n}") for n in ("less", "exped", "flipped", "weighed", "summed"))
    first = START["router"]
    E = N_EXPERTS
    with ExitStack() as local:
        def sb(name, shape):
            return local.enter_context(nc.sbuf_tensor(f"rt_{name}", shape, F32))
        logit, e, more, same, rank = (sb(n, [P, 2, E]) for n in ("logit", "e", "more", "same", "rank"))
        top, stat = sb("top", [P, 2, 8]), sb("stat", [P, 2, 5])
        with nc.Block() as block:
            @block.sync
            def _(sp):
                refill(k, sp, first, 1)

            @block.tensor
            def _(pe):
                w = take_slab(k, pe, first).rearrange("p (k c) -> p k c", k=KC)
                for b in range(2):
                    for c in range(KC):
                        last = nc.tensor.matmul(k.ps[:, 0, b * E:(b + 1) * E], k.h[:, c, b * P:(b + 1) * P], w[:, c, 0:E], start=c == 0, stop=c == KC - 1)
                last.then_inc(k.slab_used, 1)
                pe.wait_ge(weighed, 2)
                for b in range(2):
                    last = nc.tensor.transpose(k.ps[0:E, 1, b * P:(b + 1) * P], e[:, b, :], k.s("ident"))
                last.then_inc(flipped, 1)

            @block.scalar
            def _(act):
                for b in range(2):
                    act.wait_ge(less, b + 1)
                    nc.scalar.activation(e[:, b, :], logit[:, b, :], ACT.Exp, bias=stat[:, b, 0:1]).then_inc(exped, 1)

            @block.vector
            def _(dve):
                steps = k.dve_steps.on(dve)
                dve.wait_ge(k.slab_used, first + 1)
                for b in range(2):
                    l, fourth = logit[:, b, :], top[:, b, TOP_K - 1:TOP_K]
                    steps.then(nc.vector.tensor_tensor(l, k.ps[:, 0, b * E:(b + 1) * E], k.s("b_router"), ALU.add))
                    steps.then(nc.vector.max(top[:, b, :], l))
                    nc.vector.tensor_scalar(stat[:, b, 0:1], top[:, b, 0:1], -1.0, None, ALU.mult).then_inc(less, 1)
                    steps.done(nc.vector.tensor_scalar(same[:, b, :], l, fourth, None, ALU.is_equal))
                    steps.then(nc.vector.tensor_scalar(more[:, b, :], l, fourth, None, ALU.is_gt))
                    steps.done(nc.vector.reduce_sum(stat[:, b, 1:2], more[:, b, :], AX_X))
                    steps.then(nc.vector.tensor_tensor_scan(rank[:, b, :], k.s("ones")[:, 0:E], same[:, b, :], 0.0, ALU.mult, ALU.add))
                    steps.then(nc.vector.tensor_scalar(rank[:, b, :], rank[:, b, :], stat[:, b, 1:2], float(TOP_K), ALU.add, ALU.is_le))
                    steps.then(nc.vector.tensor_tensor(same[:, b, :], same[:, b, :], rank[:, b, :], ALU.mult))
                    steps.then(nc.vector.tensor_tensor(more[:, b, :], more[:, b, :], same[:, b, :], ALU.add))
                    dve.wait_ge(exped, b + 1)
                    steps.then(nc.vector.tensor_tensor(e[:, b, :], e[:, b, :], more[:, b, :], ALU.mult))
                    steps.then(nc.vector.reduce_sum(stat[:, b, 2:3], e[:, b, :], AX_X))
                    steps.then(nc.vector.reciprocal(stat[:, b, 3:4], stat[:, b, 2:3]))
                    nc.vector.tensor_scalar(e[:, b, :], e[:, b, :], stat[:, b, 3:4], None, ALU.mult).then_inc(weighed, 1)
                dve.wait_ge(flipped, 1)
                nc.vector.tensor_copy(weights[:, :], k.ps[0:E, 1, 0:T])


def stage_experts(k, weights, total):
    nc = k.nc
    row_ready, spread, pair_free, sig_done, gated, act_ready, down_free, biased, cleared = (sem(k, f"ex_{n}") for n in ("row_ready", "spread", "pair_free", "sig_done", "gated", "act_ready", "down_free", "biased", "cleared"))
    first, SLOTS = START["moe"], 3 * KC
    PAIRS = 2
    PER = 3 * KC
    with ExitStack() as local:
        def sb(name, shape):
            return local.enter_context(nc.sbuf_tensor(f"ex_{name}", shape, F32))
        row, cw = sb("row", [N_EXPERTS, T]), sb("cw", [P, T])
        gate, up, sig, hidden = sb("gate", [P, PAIRS, T]), sb("up", [P, PAIRS, T]), sb("sig", [P, PAIRS, T]), sb("hidden", [P, KC, T])
        with nc.Block() as block:
            @block.sync
            def _(sp):
                refill(k, sp, first, SLOTS, N_EXPERTS)

            @block.tensor
            def _(pe):
                with pe.Fori(0, N_EXPERTS) as e:
                    pe.wait_ge(row_ready, e + 1)
                    nc.tensor.matmul(k.ps[:, 6, 0:T], k.s("ones")[0:N_EXPERTS, :], row[:, :], start=True, stop=True).then_inc(spread, 1)
                    for m in range(KC):
                        pe.wait_ge(pair_free, e * KC + m + 1)
                        for part in range(2):
                            slab = take_slab(k, pe, first + 2 * m + part, e, SLOTS)
                            slab_product(k, slab, lambda c: k.h[:, c, 0:T], k.ps[:, 2 * (m % PAIRS) + part, 0:T])
                    for m in range(KC):
                        slab = take_slab(k, pe, first + 2 * KC + m, e, SLOTS)
                        pe.wait_ge(down_free, e * KC + m + 1)
                        if m == 0:
                            pe.wait_ge(act_ready, e * KC + KC)
                        slab_product(k, slab, lambda c: hidden[:, c, :], k.ps[:, 4 + m % 2, 0:T])

            @block.scalar
            def _(act):
                with act.Fori(0, N_EXPERTS) as e:
                    for m in range(KC):
                        act.wait_ge(gated, e * KC + m + 1)
                        nc.scalar.activation(sig[:, m % PAIRS, :], gate[:, m % PAIRS, :], ACT.Sigmoid, scale=ALPHA).then_inc(sig_done, 1)

            @block.gpsimd
            def _(pool):
                nc.gpsimd.memset(total[:, :, :], 0.0).then_inc(cleared, 1)

            @block.vector
            def _(dve):
                dve.wait_ge(cleared, 1)
                dve.sem_inc(pair_free, PAIRS)
                dve.sem_inc(down_free, 2)
                steps = k.dve_steps.on(dve)
                with dve.Fori(0, N_EXPERTS) as e:
                    steps.loop(e, 1 + 4 * KC)
                    nc.vector.tensor_scalar(row[:, :], weights[:, :], k.s("ident")[0:N_EXPERTS, bass.ds(e, 1)], None, ALU.mult).then_inc(row_ready, 1)
                    dve.wait_ge(spread, e + 1)
                    steps.then(nc.vector.tensor_copy(cw[:, :], k.ps[:, 6, 0:T]))

                    def finish(m):
                        n = m % PAIRS
                        dve.wait_ge(sig_done, e * KC + m + 1)
                        steps.then(nc.vector.tensor_tensor(gate[:, n, :], gate[:, n, :], sig[:, n, :], ALU.mult))
                        nc.vector.tensor_tensor(hidden[:, m, :], gate[:, n, :], up[:, n, :], ALU.mult).then_inc(act_ready, 1)

                    for m in range(KC):
                        n = m % PAIRS
                        bias = lambda name: k.s(name)[:, bass.ds(e * KC + m, 1)]
                        dve.wait_ge(k.slab_used, e * SLOTS + first + 2 * m + 2)
                        if m >= PAIRS:
                            dve.wait_ge(act_ready, e * KC + m - 1)
                        nc.vector.tensor_scalar(gate[:, n, :], k.ps[:, 2 * n, 0:T], bias("b_gate"), LIMIT, ALU.add, ALU.min).then_inc(gated, 1)
                        nc.vector.tensor_scalar(up[:, n, :], k.ps[:, 2 * n + 1, 0:T], bias("b_up"), LIMIT, ALU.add, ALU.min).then_inc(pair_free, 1)
                        dve.wait_ge(pair_free, e * KC + m + 1 + PAIRS)
                        steps.then(nc.vector.tensor_scalar(up[:, n, :], up[:, n, :], -LIMIT, 1.0, ALU.max, ALU.add))
                        steps.then(nc.vector.tensor_tensor(up[:, n, :], up[:, n, :], cw[:, :], ALU.mult))
                        if m:
                            finish(m - 1)
                    finish(KC - 1)
                    for m in range(KC):
                        steps.then(nc.vector.scalar_tensor_tensor(total[:, m, :], cw[:, :], k.s("b_down")[:, bass.ds(e * KC + m, 1)], total[:, m, :], ALU.mult, ALU.add))
                        dve.wait_ge(k.slab_used, e * SLOTS + first + 2 * KC + m + 1)
                        nc.vector.tensor_tensor(total[:, m, :], total[:, m, :], k.ps[:, 4 + m % 2, 0:T], ALU.add).then_inc(down_free, 1)
                    steps.end(N_EXPERTS)


def stage_add(k, total):
    nc = k.nc
    with nc.Block() as block:
        @block.vector
        def _(dve):
            for m in range(KC):
                nc.vector.scalar_tensor_tensor(k.x[:, m, :], total[:, m, :], gate_of(k, 2, 5, m), k.x[:, m, :], ALU.mult, ALU.add)


def stage_store(k):
    nc = k.nc
    stored = sem(k, "stored")
    with nc.Block() as block:
        @block.sync
        def _(sp):
            sp.dma_start(k.out_dram, k.x[:, :, :]).then_inc(stored, 16)
            sp.wait_ge(stored, 16)


def expert_layer(k):
    with ExitStack() as local:
        total = local.enter_context(k.nc.sbuf_tensor("ex_total", [P, KC, T], F32))
        weights = local.enter_context(k.nc.sbuf_tensor("ex_weights", [N_EXPERTS, T], F32))
        stage_norm(k, "e_norm", [(lambda c: k.x[:, c, :], 7, lambda c: k.h[:, c, 0:T])])
        stage_router(k, weights)
        stage_experts(k, weights, total)
        stage_add(k, total)
    stage_norm(k, "final1", [(lambda c: k.x[:, c, :], None, lambda c: k.x[:, c, :])], KC, k.s("norm_g")[:, 7 * KC:8 * KC])


def build(nc, dram, out, stop=None):
    k = Core()
    k.nc, k.dram, k.out_dram = nc, dram, out
    k.stream_dram, k.small_dram, k.x_dram = dram["stream"], dram["small"], dram["tokens"]
    layout, columns = small_layout()
    k.norms = [(0, 1, 0), (0, 1, 1), (1, 1, 0), (0, 4, 0), (2, 1, 2), (2, 1, 3), (1, 4, 0), (2, 4, 2)]
    k.norm_of = [0, 0, 1, 2, 5, 5, 3, 6]
    with ExitStack() as stack:
        k.sems, k.sem_stack = [], stack
        k.ring = stack.enter_context(nc.sbuf_tensor("ring", [P, RING, KC * P], F32))
        k.small = stack.enter_context(nc.sbuf_tensor("small", [P, columns], F32))
        k.x = stack.enter_context(nc.sbuf_tensor("x", [P, KC, T], F32))
        k.h = stack.enter_context(nc.sbuf_tensor("h", [P, KC, T2], F32))
        k.mod = stack.enter_context(nc.sbuf_tensor("mod", [P, 4, 3 * MOD_CHUNKS], F32))
        k.gain = stack.enter_context(nc.sbuf_tensor("gain", [P, 8, KC], F32))
        k.ps = stack.enter_context(nc.psum_tensor("ps", [P, 8, BANK], F32))
        k.s = lambda name: k.small[:, layout[name][0]:layout[name][0] + layout[name][1]]
        k.slab_filled = [sem(k, f"slab_filled{i}") for i in range(RING)]
        k.dve_steps, k.act_steps = Steps(sem(k, "dve_steps")), Steps(sem(k, "act_steps"))
        k.norm_sems = [sem(k, f"norm_{n}") for n in ("squares", "total", "root", "scaled", "inverse")]
        k.norm_chunks = k.norm_parts = 0
        k.slab_used, k.small_loaded, k.x_loaded = (sem(k, n) for n in ("slab_used", "small_loaded", "x_loaded"))
        for name, stage in [("load", stage_load), ("modulation", stage_modulation), ("attention", attention_layer),
                            ("mlp0", lambda k: mlp_layer(k, 0, 3)), ("hyena", hyena_layer), ("mlp1", lambda k: mlp_layer(k, 1, 6)),
                            ("delta", delta_layer), ("experts", expert_layer)]:
            with_own_semaphores(k, stage)
            if name == stop:
                break
        with_own_semaphores(k, stage_store)


def mlp_layer(k, layer, norm):
    stage_norm(k, f"m{layer}_norm", [(lambda c: k.x[:, c, :], norm, lambda c: k.h[:, c, 0:T])])
    stage_mlp(k, layer)


def slabs_of(w, chunks=KC):
    n = w.shape[1] // P
    return w.reshape(chunks, P, n, P).transpose(2, 1, 0, 3).reshape(n, P, chunks * P)


def padded_slab(w):
    out = np.zeros((1, P, KC * P), np.float32)
    out[0, :, :w.shape[1]] = w
    return out


def weight_stream(i):
    def columns(w, cols):
        out = np.zeros((D, P), np.float32)
        out[:, cols[0]:cols[0] + w.shape[1]] = w
        return slabs_of(out)
    a = i["a_w_in"][0]
    cq, ckv, kr, gq, gk, gv = np.split(a, np.cumsum([384, 256, 32, 512, 128]), axis=1)
    gq = gq.reshape(D, GQA_KV, 4, HEAD).transpose(0, 2, 1, 3).reshape(D, GQA_HEADS * HEAD)
    qb = i["a_w_q_b"][0].reshape(Q_CHUNKS, P, MLA_HEADS, QK_MLA).transpose(1, 0, 2, 3)
    kvb = i["a_w_kv_b"][0].reshape(KV_CHUNKS, P, MLA_HEADS, NOPE + DV).transpose(1, 0, 2, 3)
    out = i["a_w_out"][0]
    low = out[512:].reshape(GQA_KV, 4, HEAD, D).transpose(1, 0, 2, 3).reshape(512, D)
    parts = [slabs_of(i["w_mod"][0]), slabs_of(i["w_mod"][1]), slabs_of(i["w_mod_2"][0]),
             slabs_of(cq), slabs_of(gq), slabs_of(ckv), slabs_of(gk), columns(kr, (NOPE,)), slabs_of(gv)]
    for h, n in ((0, 3), (3, 3), (6, 2)):
        wide = np.zeros((P, Q_CHUNKS, 3 * QK_MLA), np.float32)
        wide[:, :, :n * QK_MLA] = qb[:, :, h:h + n].reshape(P, Q_CHUNKS, n * QK_MLA)
        parts.append(padded_slab(wide.reshape(P, -1)))
    parts += [padded_slab(kvb[..., :NOPE].reshape(P, -1)), padded_slab(kvb[..., NOPE:].reshape(P, -1)),
              slabs_of(np.concatenate([out[:512], low]))]

    def mlp(n):
        w2 = i["mlp_w2"][n].reshape(4, KC, P, KC, P).transpose(3, 0, 2, 1, 4).reshape(4 * KC, P, KC * P)
        return [slabs_of(i["mlp_w1"][n]), w2]
    g = i["w_in_2"][0]
    qkv, ba, z, f, ga, gb = np.split(g, np.cumsum([2048, 32, 1024, 512, 1024]), axis=1)
    fout = i["w_fourier_out_2"][0].reshape(F_GROUPS, P, 4, 2 * P).transpose(2, 1, 0, 3).reshape(4, P, KC * P)
    parts += mlp(0) + [slabs_of(i["h_w_in"][0]), slabs_of(i["h_w_out"][0])] + mlp(1)
    parts += [slabs_of(qkv), columns(ba, (0,)), slabs_of(f), fout, slabs_of(z), slabs_of(i["w_gdn_out_2"][0]),
              slabs_of(ga), slabs_of(gb), slabs_of(i["w_merge_out_2"][0]), columns(i["w_router_2"][0], (0,))]
    out = np.empty((SLABS, P, KC * P), np.float32)
    at = 0
    for p in parts:
        out[at:at + len(p)] = p
        at += len(p)
    assert at == START["moe"]
    for e in range(N_EXPERTS):
        out[at:at + 2 * KC:2] = slabs_of(i["w_gate_2"][0, e])
        out[at + 1:at + 2 * KC:2] = slabs_of(i["w_up_2"][0, e])
        out[at + 2 * KC:at + 3 * KC] = slabs_of(i["w_down_2"][0, e])
        at += 3 * KC
    return out


def by_feature(v):
    v = np.asarray(v, np.float32).reshape(-1, P)
    return np.ascontiguousarray(v.T)


def rope_tables(half_dim):
    nf = half_dim // 2
    inv = (10000.0 ** (-np.arange(nf, dtype=np.float32) / np.float32(nf))).astype(np.float32)
    t = np.arange(T)
    ang = np.concatenate([(t // GRID_W)[None] * inv[:, None]] * 2 + [(t % GRID_W)[None] * inv[:, None]] * 2).astype(np.float32)
    turn = np.zeros((2 * half_dim, 2 * half_dim), np.float32)
    for half in (0, half_dim):
        for j in range(nf):
            turn[half + nf + j, half + j] = -1.0
            turn[half + j, half + nf + j] = 1.0
    return np.cos(ang), np.sin(ang), turn


def small_columns(i):
    layout, width = small_layout()
    out = np.zeros((P, width), np.float32)

    def put(name, a, row=0):
        a = np.asarray(a, np.float32)
        at, w = layout[name]
        assert a.shape[1] == w, (name, a.shape, w)
        out[row:row + a.shape[0], at:at + w] = a

    def rows(v):
        return np.broadcast_to(np.asarray(v, np.float32).reshape(1, -1), (P, np.size(v)))
    c4 = np.stack([i["c"][0], i["c_ctx"], i["c_2"][0], i["c_ctx_2"]])
    put("c4", c4.reshape(4, KC, P).transpose(2, 1, 0).reshape(P, -1))
    put("b_mod", np.concatenate([by_feature(i["b_mod"]), by_feature(i["b_mod_2"])], 1))
    put("norm_g", np.concatenate([by_feature(i[n]) for n in ("norm1_g", "norm2_g", "final_g", "norm1_g_2", "norm2_g_2", "final_norm_g_2")], 1))
    put("q_a_g", by_feature(i["a_q_a_g"]))
    put("kv_a_g", by_feature(i["a_kv_a_g"]))
    put("q_norm_g", np.tile(i["a_q_norm_g"][0], 2)[:, None])
    put("k_norm_g", np.tile(i["a_k_norm_g"][0], 2)[:, None])
    put("h_conv_w", by_feature(i["h_conv_w"]))
    put("h_conv_b", by_feature(i["h_conv_b"]))
    put("f_b", np.stack([i["h_f_b1"][0], i["h_f_b2"][0], i["h_f_b3"][0]], 1))
    put("f_freq", i["h_f_freq"][0].T)
    put("h_skip", by_feature(i["h_skip"]))
    put("g_conv_w", by_feature(i["conv_w_2"]))
    put("dt_bias", rows(i["dt_bias_2"]))
    put("a_log", rows(i["a_log_2"]))
    put("gdn_g", by_feature(i["gdn_norm_g_2"]))
    put("b_router", rows(i["b_router_2"]))
    for n in ("b_gate", "b_up", "b_down"):
        put(n, by_feature(i[n + "_2"]))
    put("f_w1", i["h_f_w1"][0])
    put("f_w2", i["h_f_w2"][0])
    put("f_w3", i["h_f_w3"][0])
    put("ident", np.eye(P))
    put("ones", np.ones((P, P)))
    put("blocks64", np.kron(np.eye(2), np.ones((HEAD, HEAD))))
    put("eps", np.full((P, 1), EPS))
    put("one", np.ones((P, 1)))
    cos, sin, turn = rope_tables(HEAD // 2)
    put("rope_cos", np.tile(cos, (2, 1)))
    put("rope_sin", np.tile(sin, (2, 1)))
    put("rope_turn", np.kron(np.eye(2), turn))
    cos, sin, turn = rope_tables(ROPE // 2)
    put("kr_cos", cos, NOPE)
    put("kr_sin", sin, NOPE)
    put("kr_turn", np.concatenate([np.zeros((ROPE, NOPE)), turn], 1), NOPE)
    p, f = np.arange(P)[:, None], np.arange(P)[None]
    put("tri", np.concatenate([p <= f, p >= f], 1))
    put("strict", np.concatenate([p > f, p < f], 1))
    up = [(p // (2 << n) == f // (2 << n)) & ((p >> n) % 2 == 0) & ((f >> n) % 2 == 1) for n in range(LEVELS)]
    put("level", np.concatenate(up + [m.T for m in up], 1))
    norm = 1.0 / math.sqrt(T * P)
    ang = 2 * np.pi * (np.outer(np.arange(P), np.arange(P)) % P) / P
    put("four_g", np.concatenate([np.cos(ang), -np.sin(ang)], 1) * norm)
    ang = 2 * np.pi * (np.outer(np.arange(T), np.arange(T)) % T) / T
    tab = np.stack([np.cos(ang), np.sin(ang)]).reshape(2, 2, P, T).transpose(2, 0, 1, 3)
    put("four_t", tab.reshape(P, -1))
    return out


def filter_constants():
    f32 = np.float32
    t = np.arange(T, dtype=f32)
    t_norm = t / f32(T)
    w = f32(2.0 * math.pi) * t / f32(T)
    bands = np.linspace(1e-4, BANDS - 1, BANDS, dtype=f32)
    fw = w[:, None] * bands[None]
    feats = np.concatenate([t_norm[:, None], np.cos(fw), -np.sin(fw)], 1).astype(f32)
    low, high = math.log(1e-2) / 1.5, math.log(1e-2) / 0.3
    deltas = np.abs(np.linspace(low, high, D, dtype=f32))
    window = np.exp(-t_norm[:, None] * deltas[None]).astype(f32)
    k = (np.outer(np.arange(T), 2 * np.arange(T) + 1) % (4 * T)) * (np.pi / (2 * T))
    by_token = lambda a: np.ascontiguousarray(a.reshape(2, P, -1).transpose(1, 0, 2).astype(f32))
    first = np.ones((P, 2), f32)
    first[0, 0] = 0.0
    return {"feats": np.ascontiguousarray(feats.T), "window": by_token(window), "fc": by_token(np.cos(k)), "fs": by_token(-np.sin(k)),
            "gc": by_token(np.cos(k).T / T), "gs": by_token(-np.sin(k).T / T), "first": first}


def kernel(**inputs):
    import concourse.bacc as bacc
    from concourse.bass_utils import run_bass_kernel_spmd

    i = {n: np.asarray(a) for n, a in inputs.items()}
    tokens = np.concatenate([i["x"], i["ctx"], i["ctx_2"]])
    arrays = {"stream": weight_stream(i), "small": small_columns(i),
              "tokens": np.ascontiguousarray(tokens.reshape(3, T, KC, P).transpose(0, 3, 2, 1)),
              "w4": np.ascontiguousarray(i["h_f_w4"][0]), **filter_constants()}
    nc = bacc.Bacc("TRN2", target_bir_lowering=False, num_devices=1)
    dram = {n: nc.dram_tensor(f"in_{n}", a.shape, mybir.dt.from_np(a.dtype), kind="ExternalInput").ap() for n, a in arrays.items()}
    out = nc.dram_tensor("out", (P, KC, T), F32, kind="ExternalOutput").ap()
    build(nc, dram, out)
    got = run_bass_kernel_spmd(nc, [{f"in_{n}": a for n, a in arrays.items()}], core_ids=[0]).results[0]["out"]
    return np.ascontiguousarray(np.asarray(got).transpose(2, 1, 0).reshape(1, T, D))
```

```python
import math
from contextlib import ExitStack

import numpy as np
import concourse.bass as bass
from concourse import mybir

P = 128
D = 1024
KC = D // P
T = 256
T2 = 2 * T
BANK = 512
F32 = mybir.dt.float32
BF16 = mybir.dt.bfloat16
ALU = mybir.AluOpType
ACT = mybir.ActivationFunctionType
AX_X = mybir.AxisListType.X
EPS = 1e-6

N_MOD = 6
MOD_CHUNKS = N_MOD * KC
MLP_CHUNKS = 4 * KC
MLA_HEADS, NOPE, ROPE, DV = 8, 64, 32, 64
QK_MLA = NOPE + ROPE
Q_CHUNKS, KV_CHUNKS = 3, 2
GQA_HEADS, GQA_KV = 8, 2
HEAD = 64
GRID_W = 64
ROWS = T // GRID_W
F_HIDDEN, F_EMB, BANDS, ORDERS = 64, 17, 8, 2
NQK, NV = 4, 8
QKV_CHUNKS = 2 * NQK + NV
F_GROUPS = 4
N_EXPERTS, TOP_K = 32, 4
ALPHA, LIMIT = 1.702, 7.0
BLOCK_SLOTS = P // 2
MAX_BLOCKS = 48
FAR = 1024.0
LEVELS = 7

RING = 8
GROUP = 2 * RING
STREAM = [("mod", MOD_CHUNKS),
          ("a_in", 12), ("a_qb", 3), ("a_kvb", 2), ("a_out", KC),
          ("mlp0_up", MLP_CHUNKS), ("mlp0_down", MLP_CHUNKS),
          ("h_in", 3 * KC), ("h_out", KC),
          ("mlp1_up", MLP_CHUNKS), ("mlp1_down", MLP_CHUNKS),
          ("g_qkv", QKV_CHUNKS), ("g_ba", 1), ("g_f", F_GROUPS), ("g_fout", 4), ("g_z", KC), ("g_out", KC),
          ("g_ga", KC), ("g_gb", KC), ("g_merge", KC), ("router", 1),
          ("moe", N_EXPERTS * 3 * KC)]
START = {name: sum(n for _, n in STREAM[:i]) for i, (name, _) in enumerate(STREAM)}
SLABS = sum(n for _, n in STREAM)


class Steps:

    def __init__(self, sem):
        self.sem, self.n, self.turn, self.per = sem, 0, None, 0

    def on(self, eng):
        self.eng = eng
        return self

    def done(self, ins):
        ins.then_inc(self.sem, 1)
        self.n += 1
        return self.n

    def wait(self, n=None):
        n = self.n if n is None else n
        self.eng.wait_ge(self.sem, n if self.turn is None else self.turn * self.per + n)

    def then(self, ins):
        self.done(ins)
        self.wait()

    def loop(self, turn, per):
        self.turn, self.per, self.first = turn, per, self.n

    def end(self, turns):
        assert self.n - self.first == self.per, (self.n - self.first, self.per)
        self.n += (turns - 1) * self.per
        self.turn = None


def small_layout():
    out, at = {}, 0
    for name, width in [
            ("b_mod", 3 * MOD_CHUNKS), ("norm_g", 8 * KC), ("q_a_g", Q_CHUNKS),
            ("kv_a_g", KV_CHUNKS), ("q_norm_g", 1), ("k_norm_g", 1), ("h_conv_w", 3 * 3 * KC),
            ("h_conv_b", 3 * KC), ("f_b", 3), ("f_freq", 3), ("h_skip", ORDERS * KC),
            ("g_conv_w", 9 * QKV_CHUNKS), ("dt_bias", 2 * NV), ("a_log", 2 * NV), ("gdn_g", 1),
            ("b_router", N_EXPERTS), ("f_w1", F_HIDDEN), ("f_w2", F_HIDDEN), ("f_w3", F_HIDDEN),
            ("ident", P), ("ones", P), ("iota", P), ("slots", P), ("tri3", 3 * N_EXPERTS), ("blocks64", P), ("eps", 1), ("one", 1),
            ("rope_cos", T), ("rope_sin", T), ("rope_turn", P),
            ("kr_cos", T), ("kr_sin", T), ("kr_turn", QK_MLA),
            ("tri", 2 * P), ("strict", 2 * P), ("level", 2 * LEVELS * P),
            ("four_g", 2 * P), ("four_t", 4 * T)]:
        out[name] = (at, width)
        at += width
    return out, at


class Core:
    pass


def sem(k, name):
    k.sems.append(k.sem_stack.enter_context(k.nc.semaphore(name)))
    return k.sems[-1]


def with_own_semaphores(k, layer):
    nc = k.nc
    k.sems = []
    with ExitStack() as k.sem_stack:
        layer(k)
        with nc.Block() as block:
            @block.sync
            def _(sp):
                for s in k.sems:
                    sp.sem_clear(s)


def take_slab(k, pe, j, turn=None, count=RING):
    value = 16 * (j // RING + 1)
    pe.wait_ge(k.slab_filled[j % RING], value if turn is None else turn * (16 * count // RING) + value)
    return k.ring[:, j % RING, :]


def refill(k, sp, first, count, turns=1):
    def one(j, turn=None):
        n = j + RING
        if turn is None:
            if n >= START["moe"]:
                return
            sp.wait_ge(k.slab_used, j + 1)
            src = k.stream_dram[n, :, :]
        else:
            sp.wait_ge(k.slab_used, turn * count + j + 1)
            src = k.stream_dram[bass.ds(turn * count + n, 1), :, :].rearrange("a p n -> (a p) n")
        sp.dma_start(k.ring[:, j % RING, :], src).then_inc(k.slab_filled[j % RING], 16)

    whole = turns if first + count * turns + RING <= START["moe"] else turns - 1
    if turns > 1:
        with sp.Fori(0, whole) as turn:
            for j in range(count):
                one(first + j, turn)
    for j in range(whole * count if turns > 1 else 0, count * turns):
        one(first + j)


def slab_product(k, slab, rhs, out, width=P, chunks=KC, start=True, stop=True, used=True):
    w = slab.rearrange("p (k c) -> p k c", k=chunks)
    for c in range(chunks):
        last = k.nc.tensor.matmul(out, w[:, c, 0:width], rhs(c), start=start and c == 0, stop=stop and c == chunks - 1)
    if used:
        last.then_inc(k.slab_used, 1)
    return last


def stage_load(k):
    nc = k.nc
    with nc.Block() as block:
        @block.sync
        def _(sp):
            for j in range(RING):
                sp.dma_start(k.ring[:, j, :], k.stream_dram[j, :, :]).then_inc(k.slab_filled[j], 16)

        @block.scalar
        def _(act):
            act.dma_start(k.small[:, :], k.small_dram).then_inc(k.small_loaded, 16)
            act.dma_start(k.x[:, :, :], k.x_dram[0]).then_inc(k.x_loaded, 16)
            act.wait_ge(k.small_loaded, 16)
            act.wait_ge(k.x_loaded, 16)


def set_gains(k, layer):
    for n, (of, part, v) in enumerate(k.norms):
        a = of * MOD_CHUNKS + part * KC
        if of == layer:
            k.nc.vector.scalar_tensor_tensor(k.gain[:, n, :], k.mod[:, v, a:a + KC], 1.0,
                                             k.s("norm_g")[:, k.norm_of[n] * KC:(k.norm_of[n] + 1) * KC], ALU.add, ALU.mult)


def stage_modulation(k):
    nc = k.nc
    loaded, silu_ready, turn_taken = (sem(k, f"mod_{n}") for n in ("loaded", "silu_ready", "turn_taken"))
    OWN = 2 * KC
    segments = [(0, OWN, (0, 1)), (OWN, MOD_CHUNKS - OWN, (0,))]
    SPARE = 4
    with ExitStack() as local:
        c4 = local.enter_context(nc.sbuf_tensor("mod_c4", [P, 4, D], F32))
        waste = local.enter_context(nc.sbuf_tensor("mod_waste", [P, SPARE, 2, D], F32))
        sums = local.enter_context(nc.sbuf_tensor("mod_sums", [P, 2, RING], F32))
        with nc.Block() as block:
            @block.sync
            def _(sp):
                refill(k, sp, START["mod"], GROUP, MOD_CHUNKS // GROUP)

            @block.scalar
            def _(act):
                act.dma_start(c4[:, :, :], k.dram["c4"]).then_inc(loaded, 16)
                act.wait_ge(loaded, 16)
                nc.scalar.activation(c4[:, :, :], c4[:, :, :], ACT.Silu).then_inc(silu_ready, 1)

            @block.vector
            def _(dve):
                dve.wait_ge(silu_ready, 1)
                b = k.s("b_mod")
                turns = 0
                for first, count, vectors in segments:
                    with dve.Fori(0, count // RING) as turn:
                        for s in range(RING):
                            j = first + s
                            dve.wait_ge(k.slab_filled[s], turn * 16 + 16 * (j // RING + 1))
                            if s >= SPARE:
                                dve.wait_ge(k.slab_used, turn * RING + j - SPARE + 1)
                            for n, v in enumerate(vectors):
                                last = nc.vector.scalar_tensor_tensor(waste[:, s % SPARE, n, :], k.ring[:, s, :], 1.0, c4[:, v, :], ALU.mult, ALU.mult,
                                                                      accum_out=sums[:, n, s:s + 1])
                            last.then_inc(k.slab_used, 1)
                        dve.wait_ge(k.slab_used, turn * RING + first + RING)
                        for n, v in enumerate(vectors):
                            at = turn * RING + first
                            last = nc.vector.tensor_tensor(k.mod[:, v, bass.ds(at, RING)], sums[:, n, :], b[:, bass.ds(at, RING)], ALU.add)
                        last.then_inc(turn_taken, 1)
                        dve.wait_ge(turn_taken, turn + turns + 1)
                    turns += count // RING
                set_gains(k, 0)


def shift_of(k, n, c):
    layer, part, v = k.norms[n]
    at = layer * MOD_CHUNKS + (part - 1) * KC + c
    return k.mod[:, v, at:at + 1]


def gate_of(k, layer, part, c):
    v = 2 if layer == 2 else 0
    at = layer * MOD_CHUNKS + part * KC + c
    return k.mod[:, v, at:at + 1]


def stage_norm(k, name, parts, chunks=KC, gains=None):
    nc = k.nc
    squares, total, root, scaled, inverse = k.norm_sems
    chunk0, part0 = k.norm_chunks, k.norm_parts
    k.norm_chunks, k.norm_parts = chunk0 + len(parts) * chunks, part0 + len(parts)
    with ExitStack() as local:
        sq = local.enter_context(nc.sbuf_tensor(f"{name}_sq", [P, chunks, T2], F32))
        std = local.enter_context(nc.sbuf_tensor(f"{name}_std", [P, len(parts), T], F32))
        rstd = local.enter_context(nc.sbuf_tensor(f"{name}_rstd", [P, len(parts), T], F32))
        with nc.Block() as block:
            @block.scalar
            def _(act):
                for i, (src, _, _) in enumerate(parts):
                    for c in range(chunks):
                        nc.scalar.activation(sq[:, c, i * T:(i + 1) * T], src(c), ACT.Square).then_inc(squares, 1)
                for i in range(len(parts)):
                    act.wait_ge(total, part0 + i + 1)
                    nc.scalar.activation(std[:, i, :], k.ps[:, i, 0:T], ACT.Sqrt, scale=1.0 / (chunks * P), bias=k.s("eps")).then_inc(root, 1)
                for i, (_, n, dst) in enumerate(parts):
                    for c in range(chunks):
                        act.wait_ge(scaled, chunk0 + i * chunks + c + 1)
                        if n is None:
                            nc.scalar.activation(dst(c), sq[:, c, i * T:(i + 1) * T], ACT.Identity, scale=gains[:, c:c + 1])
                        else:
                            nc.scalar.activation(dst(c), sq[:, c, i * T:(i + 1) * T], ACT.Identity,
                                                 scale=k.gain[:, n, c:c + 1], bias=shift_of(k, n, c))

            @block.tensor
            def _(pe):
                for i in range(len(parts)):
                    for c in range(chunks):
                        pe.wait_ge(squares, chunk0 + i * chunks + c + 1)
                        last = nc.tensor.matmul(k.ps[:, i, 0:T], k.s("ones"), sq[:, c, i * T:(i + 1) * T], start=c == 0, stop=c == chunks - 1)
                    last.then_inc(total, 1)

            @block.vector
            def _(dve):
                for i, (src, _, _) in enumerate(parts):
                    dve.wait_ge(root, part0 + i + 1)
                    nc.vector.reciprocal(rstd[:, i, :], std[:, i, :]).then_inc(inverse, 1)
                    dve.wait_ge(inverse, part0 + i + 1)
                    for c in range(chunks):
                        nc.vector.tensor_tensor(sq[:, c, i * T:(i + 1) * T], src(c), rstd[:, i, :], ALU.mult).then_inc(scaled, 1)


def stage_mlp(k, layer):
    nc = k.nc
    name = f"mlp{layer}"
    bank_free, hidden_ready, sum_free, loaded, silu_ready, mod_used, mod_taken = (
        sem(k, f"{name}_{n}") for n in ("bank_free", "hidden_ready", "sum_free", "loaded", "silu_ready", "mod_used", "mod_taken"))
    mod_filled = [sem(k, f"{name}_mod_filled{i}") for i in range(4)]
    vectors = [(0,), (2, 3)][layer]
    SLOTS, SPARE = 4, 2
    LATE = GROUP // 2
    up, down = START[f"{name}_up"], START[f"{name}_down"]
    turns = MLP_CHUNKS // GROUP
    BANKS = 4
    SUMS = GROUP // 4
    with ExitStack() as local:
        hidden = local.enter_context(nc.sbuf_tensor(f"{name}_hidden", [P, MLP_CHUNKS, T], F32))
        c4 = local.enter_context(nc.sbuf_tensor(f"{name}_c4", [P, 4, D], F32))
        mod_ring = local.enter_context(nc.sbuf_tensor(f"{name}_mod_ring", [P, SLOTS, D], F32))
        waste = local.enter_context(nc.sbuf_tensor(f"{name}_waste", [P, SPARE, 2, D], F32))
        sums = local.enter_context(nc.sbuf_tensor(f"{name}_sums", [P, 2, GROUP], F32))
        with nc.Block() as block:
            @block.scalar
            def _(act):
                act.dma_start(c4[:, :, :], k.dram["c4"]).then_inc(loaded, 16)
                act.wait_ge(loaded, 16)
                nc.scalar.activation(c4[:, :, :], c4[:, :, :], ACT.Silu).then_inc(silu_ready, 1)
                act.sem_inc(mod_used, SLOTS)

                def load(at, s):
                    act.wait_ge(mod_used, at + s + 1)
                    src = k.dram["mod_later"][bass.ds(at + layer * MOD_CHUNKS + s, 1), :, :].rearrange("a p n -> (a p) n")
                    act.dma_start(mod_ring[:, s % SLOTS, :], src).then_inc(mod_filled[s % SLOTS], 16)

                with act.Fori(0, turns) as turn:
                    for s in range(GROUP):
                        load(turn * GROUP, s)
                with act.Fori(0, turns) as turn:
                    for s in range(LATE):
                        load(turn * LATE + MLP_CHUNKS, s)

            @block.sync
            def _(sp):
                refill(k, sp, up, GROUP, 2 * turns)

            @block.tensor
            def _(pe):
                with pe.Fori(0, turns) as turn:
                    for s in range(GROUP):
                        slab = take_slab(k, pe, up + s, turn, GROUP)
                        pe.wait_ge(bank_free, turn * GROUP + s + 1)
                        slab_product(k, slab, lambda c: k.h[:, c, 0:T], k.ps[:, s % BANKS, 0:T])
                pe.wait_ge(hidden_ready, MLP_CHUNKS)
                with pe.Fori(0, turns) as turn:
                    for m in range(SUMS):
                        pe.wait_ge(sum_free, turn * SUMS + m + 1)
                        for q in range(4):
                            slab = take_slab(k, pe, down + 4 * m + q, turn, GROUP)
                            slab_product(k, slab, lambda c: hidden[:, q * KC + c, :], k.ps[:, BANKS + m, 0:T],
                                         start=q == 0, stop=q == 3)

            @block.vector
            def _(dve):
                dve.sem_inc(bank_free, BANKS)
                dve.sem_inc(sum_free, SUMS)
                dve.wait_ge(silu_ready, 1)

                def modulation(at, s, vs):
                    dve.wait_ge(mod_filled[s % SLOTS], at * (16 // SLOTS) + 16 * (s // SLOTS + 1))
                    dve.wait_ge(mod_used, at + s + SLOTS - SPARE + 1)
                    for n, v in enumerate(vs):
                        last = nc.vector.scalar_tensor_tensor(waste[:, s % SPARE, n, :], mod_ring[:, s % SLOTS, :], 1.0, c4[:, v, :], ALU.mult, ALU.mult,
                                                              accum_out=sums[:, n, s:s + 1])
                    last.then_inc(mod_used, 1)

                def modulation_done(at, count, vs, taken):
                    dve.wait_ge(mod_used, at + count + SLOTS)
                    cols = bass.ds(at + (layer + 1) * MOD_CHUNKS, count)
                    for n, v in enumerate(vs):
                        last = nc.vector.tensor_tensor(k.mod[:, v, cols], sums[:, n, 0:count], k.s("b_mod")[:, cols], ALU.add)
                    last.then_inc(mod_taken, 1)
                    dve.wait_ge(mod_taken, taken)

                with dve.Fori(0, turns) as turn:
                    for s in range(GROUP):
                        out = hidden[:, bass.ds(turn * GROUP + s, 1), :].rearrange("p a t -> p (a t)")
                        dve.wait_ge(k.slab_used, turn * GROUP + up + s + 1)
                        nc.vector.tensor_scalar(out, k.ps[:, s % BANKS, 0:T], 0.0, None, ALU.max).then_inc(bank_free, 1)
                        dve.wait_ge(bank_free, turn * GROUP + BANKS + s + 1)
                        nc.vector.tensor_tensor(out, out, out, ALU.mult).then_inc(hidden_ready, 1)
                        modulation(turn * GROUP, s, vectors)
                    modulation_done(turn * GROUP, GROUP, vectors, turn + 1)
                with dve.Fori(0, turns) as turn:
                    for m in range(SUMS):
                        x = k.x[:, bass.ds(turn * SUMS + m, 1), :].rearrange("p a t -> p (a t)")
                        gate = k.mod[:, 0, bass.ds(layer * MOD_CHUNKS + (N_MOD - 1) * KC + turn * SUMS + m, 1)]
                        dve.wait_ge(k.slab_used, turn * GROUP + down + 4 * (m + 1))
                        nc.vector.scalar_tensor_tensor(x, k.ps[:, BANKS + m, 0:T], gate, x, ALU.mult, ALU.add).then_inc(sum_free, 1)
                        for s in range(m * LATE // SUMS, (m + 1) * LATE // SUMS):
                            modulation(turn * LATE + MLP_CHUNKS, s, vectors[:1])
                    modulation_done(turn * LATE + MLP_CHUNKS, LATE, vectors[:1], turn + turns + 1)
                set_gains(k, layer + 1)


def stage_attention_in(k, a):
    nc = k.nc
    taken = sem(k, "a_in_taken")
    first = START["a_in"]
    order = [0, 1, 2, 5, 6, 7, 8, 3, 4, 9, 11, 10]
    with nc.Block() as block:
        @block.sync
        def _(sp):
            refill(k, sp, first, 12)

        @block.tensor
        def _(pe):
            for i, m in enumerate(order):
                slab = take_slab(k, pe, first + i)
                if i >= 8:
                    pe.wait_ge(taken, i - 7)
                bank = k.ps[:, i % 8, :]
                if m == 10:
                    w = slab.rearrange("p (k c) -> p k c", k=KC)
                    for b in range(4):
                        for c in range(KC):
                            last = nc.tensor.matmul(bank[:, b * P:(b + 1) * P], k.h[:, c, b * P:(b + 1) * P], w[:, c, :],
                                                    start=c == 0, stop=c == KC - 1)
                    last.then_inc(k.slab_used, 1)
                else:
                    n = T if m in (0, 1, 2, 5, 6, 7, 8) else T2
                    slab_product(k, slab, lambda c: k.h[:, c, 0:n], bank[:, 0:n])

        @block.vector
        def _(dve):
            for i, m in enumerate(order):
                bank = k.ps[:, i % 8, :]
                if m < 3:
                    dst, src = a.cq[:, m, :], bank[:, 0:T]
                elif m < 5:
                    dst, src = a.ckv[:, m - 3, :], bank
                elif m < 9:
                    dst, src = a.gqk[:, (m - 5) * T:(m - 4) * T], bank[:, 0:T]
                elif m == 9:
                    dst, src = a.gqk[:, 4 * T:4 * T + T2], bank
                elif m == 10:
                    dst, src = a.v[:, :, 4 * P:5 * P], bank.rearrange("p (b c) -> p b c", b=4)
                else:
                    dst, src = a.kr[NOPE:QK_MLA, :], bank[NOPE:QK_MLA, :]
                dve.wait_ge(k.slab_used, first + i + 1)
                nc.vector.tensor_copy(dst, src).then_inc(taken, 1)


def stage_grouped_heads(k, a):
    nc = k.nc
    squared, total, root, gained, turned = (sem(k, f"gqa_{n}") for n in ("squared", "total", "root", "gained", "turned"))
    W = 3 * BANK
    R = 5 * T
    turns = [(0, BANK), (BANK, 2 * BANK), (2 * BANK, R)]
    with ExitStack() as local:
        tmp = local.enter_context(nc.sbuf_tensor("gqa_tmp", [P, W], F32))
        std = local.enter_context(nc.sbuf_tensor("gqa_std", [P, W], F32))
        with nc.Block() as block:
            @block.sync
            def _(sp):
                pass

            @block.scalar
            def _(act):
                nc.scalar.activation(tmp[:, :], a.gqk[:, :], ACT.Square).then_inc(squared, 1)
                act.wait_ge(total, 3)
                nc.scalar.activation(std[:, :], k.ps[:, 0:3, :].rearrange("p b n -> p (b n)"), ACT.Sqrt, scale=1.0 / HEAD, bias=k.s("eps")).then_inc(root, 1)

            @block.tensor
            def _(pe):
                pe.wait_ge(squared, 1)
                for i in range(3):
                    nc.tensor.matmul(k.ps[:, i, :], k.s("blocks64"), tmp[:, i * BANK:(i + 1) * BANK], start=True, stop=True).then_inc(total, 1)
                pe.wait_ge(gained, 1)
                for i, (lo, hi) in enumerate(turns):
                    nc.tensor.matmul(k.ps[:, 4 + i, 0:hi - lo], k.s("rope_turn"), a.gqk[:, lo:hi], start=True, stop=True).then_inc(turned, 1)

            @block.vector
            def _(dve):
                steps = k.dve_steps.on(dve)
                dve.wait_ge(root, 1)
                steps.then(nc.vector.reciprocal(std[:, :], std[:, :]))
                steps.then(nc.vector.tensor_tensor(a.gqk[:, :], a.gqk[:, :], std[:, :], ALU.mult))
                nc.vector.tensor_scalar(a.gqk[:, 0:4 * T], a.gqk[:, 0:4 * T], k.s("q_norm_g"), None, ALU.mult)
                nc.vector.tensor_scalar(a.gqk[:, 4 * T:W], a.gqk[:, 4 * T:W], k.s("k_norm_g"), None, ALU.mult).then_inc(gained, 1)
                dve.wait_ge(turned, 3)
                for i in range(5):
                    bank = k.ps[:, 4 + i // 2, (i % 2) * T:(i % 2 + 1) * T]
                    steps.done(nc.vector.tensor_tensor(tmp[:, i * T:(i + 1) * T], bank, k.s("rope_sin"), ALU.mult))
                for i in range(5):
                    steps.done(nc.vector.tensor_tensor(a.gqk[:, i * T:(i + 1) * T], a.gqk[:, i * T:(i + 1) * T], k.s("rope_cos"), ALU.mult))
                steps.wait()
                nc.vector.tensor_tensor(a.gqk[:, 0:R], a.gqk[:, 0:R], tmp[:, 0:R], ALU.add)


def stage_latent_heads(k, a):
    nc = k.nc
    done, taken, turned, kr_done = (sem(k, f"mla_{n}") for n in ("done", "taken", "turned", "kr_done"))
    qb, kvb = START["a_qb"], START["a_kvb"]
    PER = [3, 3, 2]
    rope = slice(NOPE, QK_MLA)
    with ExitStack() as local:
        tmp = local.enter_context(nc.sbuf_tensor("mla_tmp", [P, 2, T], F32))
        with nc.Block() as block:
            @block.sync
            def _(sp):
                refill(k, sp, qb, 5)

            @block.tensor
            def _(pe):
                for s in range(3):
                    w = take_slab(k, pe, qb + s)[:, 0:Q_CHUNKS * 3 * QK_MLA].rearrange("p (k c) -> p k c", k=Q_CHUNKS)
                    for i in range(PER[s]):
                        h = 3 * s + i
                        for c in range(Q_CHUNKS):
                            last = nc.tensor.matmul(k.ps[0:QK_MLA, h // 2, (h % 2) * T:(h % 2 + 1) * T], w[:, c, i * QK_MLA:(i + 1) * QK_MLA],
                                                    a.cq[:, c, :], start=c == 0, stop=c == Q_CHUNKS - 1)
                    last.then_inc(k.slab_used, 1)
                w = take_slab(k, pe, kvb).rearrange("p (k c) -> p k c", k=KV_CHUNKS)
                for h in range(MLA_HEADS):
                    if h >= 4:
                        pe.wait_ge(taken, h - 3)
                    for c in range(KV_CHUNKS):
                        last = nc.tensor.matmul(k.ps[0:NOPE, 4 + h if h < 4 else h - 4, :], w[:, c, h * NOPE:(h + 1) * NOPE], a.ckv[:, c, :],
                                                start=c == 0, stop=c == KV_CHUNKS - 1)
                    if h < MLA_HEADS - 1:
                        last.then_inc(done, 1)
                    else:
                        last.then_inc(k.slab_used, 1)
                w = take_slab(k, pe, kvb + 1).rearrange("p (k c) -> p k c", k=KV_CHUNKS)
                for b in range(4):
                    pe.wait_ge(taken, 5 + b)
                    for c in range(KV_CHUNKS):
                        last = nc.tensor.matmul(k.ps[:, 4 + b, :], a.ckv[:, c, b * P:(b + 1) * P], w[:, c, :], start=c == 0, stop=c == KV_CHUNKS - 1)
                    if b < 3:
                        last.then_inc(done, 1)
                    else:
                        last.then_inc(k.slab_used, 1)
                turn = k.s("kr_turn")[rope, :]
                for i in range(4):
                    pe.wait_ge(taken, 9 + i)
                    nc.tensor.matmul(k.ps[0:QK_MLA, i, :], turn, a.q[rope, 2 * i:2 * i + 2, :], start=True, stop=True).then_inc(turned, 1)
                pe.wait_ge(taken, 13)
                nc.tensor.matmul(k.ps[0:QK_MLA, 4, 0:T], turn, a.kr[rope, 0:T], start=True, stop=True).then_inc(turned, 1)

            @block.vector
            def _(dve):
                steps = k.dve_steps.on(dve)
                for i in range(4):
                    dve.wait_ge(k.slab_used, qb + min(2, (2 * i + 1) // 3) + 1)
                    nc.vector.tensor_copy(a.q[0:QK_MLA, 2 * i:2 * i + 2, :].rearrange("p h t -> p (h t)"), k.ps[0:QK_MLA, i, :]).then_inc(taken, 1)
                for h in range(MLA_HEADS):
                    if h < MLA_HEADS - 1:
                        dve.wait_ge(done, h + 1)
                    else:
                        dve.wait_ge(k.slab_used, kvb + 1)
                    nc.vector.tensor_copy(a.k[0:NOPE, h, :], k.ps[0:NOPE, 4 + h if h < 4 else h - 4, :]).then_inc(taken, 1)
                for b in range(4):
                    if b < 3:
                        dve.wait_ge(done, MLA_HEADS + b)
                    else:
                        dve.wait_ge(k.slab_used, kvb + 2)
                    nc.vector.tensor_copy(a.v[:, b, 0:4 * P], k.ps[:, 4 + b, :]).then_inc(taken, 1)
                sin, cos = k.s("kr_sin")[rope, :], k.s("kr_cos")[rope, :]
                for i in range(4):
                    dve.wait_ge(turned, i + 1)
                    for j in range(2):
                        nc.vector.tensor_tensor(tmp[rope, j, :], k.ps[rope, i, j * T:(j + 1) * T], sin, ALU.mult)
                        last = nc.vector.tensor_tensor(a.q[rope, 2 * i + j, :], a.q[rope, 2 * i + j, :], cos, ALU.mult)
                    steps.then(last)
                    steps.then(nc.vector.tensor_tensor(a.q[rope, 2 * i:2 * i + 2, :], a.q[rope, 2 * i:2 * i + 2, :], tmp[rope, :, :], ALU.add))
                dve.wait_ge(turned, 5)
                nc.vector.tensor_tensor(tmp[rope, 0, :], k.ps[rope, 4, 0:T], sin, ALU.mult)
                steps.then(nc.vector.tensor_tensor(a.kr[rope, 0:T], a.kr[rope, 0:T], cos, ALU.mult))
                steps.then(nc.vector.tensor_tensor(a.kr[rope, 0:T], a.kr[rope, 0:T], tmp[rope, 0, :], ALU.add))
                for h in range(MLA_HEADS):
                    nc.vector.tensor_copy(a.k[rope, h, :], a.kr[rope, :])


def stage_attention(k, a):
    nc = k.nc
    scores, maxed, exped, normed, flipped, copied, mixed, stored = (sem(k, f"attn_{n}") for n in ("scores", "maxed", "exped", "normed", "flipped", "copied", "mixed", "stored"))
    heads = [("mla", h) for h in range(MLA_HEADS)] + [("gqa", h) for h in range(GQA_HEADS)]
    BLOCKS = T // P
    DEEP = 3
    units = [(n, b) for n in range(len(heads)) for b in range(BLOCKS)]

    def operands(n, b):
        kind, h = heads[n]
        if kind == "mla":
            return a.q[0:QK_MLA, h, b * P:(b + 1) * P], a.k[0:QK_MLA, h, :], 1.0 / math.sqrt(QK_MLA)
        group, c = h % 2, h // 2
        rows = slice(group * HEAD, (group + 1) * HEAD)
        return a.gqk[rows, c * T + b * P:c * T + (b + 1) * P], a.gqk[rows, 4 * T:4 * T + T2], 1.0 / math.sqrt(HEAD)

    with ExitStack() as local:
        probs = local.enter_context(nc.sbuf_tensor("attn_probs", [P, DEEP, T2], F32))
        turned = local.enter_context(nc.sbuf_tensor("attn_turned", [P, 2, 4, T], F32))
        stat = local.enter_context(nc.sbuf_tensor("attn_stat", [P, 4, len(units)], F32))
        with nc.Block() as block:
            @block.sync
            def _(sp):
                pass

            @block.tensor
            def _(pe):
                def score(i):
                    q, kk, _ = operands(*units[i])
                    if i >= DEEP:
                        pe.wait_ge(exped, i - DEEP + 1)
                    nc.tensor.matmul(k.ps[:, i % DEEP, :], q, kk, start=True, stop=True).then_inc(scores, 1)

                for i in range(DEEP - 1):
                    score(i)
                for i, (n, b) in enumerate(units):
                    if i + DEEP - 1 < len(units):
                        score(i + DEEP - 1)
                    pe.wait_ge(normed, i + 1)
                    if i >= 2:
                        pe.wait_ge(copied, i - 1)
                    for c in range(4):
                        last = nc.tensor.transpose(k.ps[:, DEEP + i % 2, c * P:(c + 1) * P], probs[:, i % DEEP, c * P:(c + 1) * P], k.s("ident"))
                    last.then_inc(flipped, 1)
                    if b == BLOCKS - 1:
                        pe.wait_ge(copied, i + 1)
                        if n >= 2:
                            pe.wait_ge(stored, n - 1)
                        pair = n // 2 if n < MLA_HEADS else 4
                        for c in range(4):
                            last = nc.tensor.matmul(k.ps[:, DEEP + 2 + n % 2, 0:T], a.v[:, c, pair * P:(pair + 1) * P], turned[:, n % 2, c, :],
                                                    start=c == 0, stop=c == 3)
                        last.then_inc(mixed, 1)

            @block.vector
            def _(dve):
                steps = k.dve_steps.on(dve)

                def store(n):
                    rows = slice((n % 2) * HEAD, (n % 2 + 1) * HEAD)
                    dve.wait_ge(mixed, n + 1)
                    nc.vector.tensor_copy(a.o[rows, n // 2, :], k.ps[rows, DEEP + 2 + n % 2, 0:T]).then_inc(stored, 1)

                def largest(i):
                    scale = operands(*units[i])[2]
                    dve.wait_ge(scores, i + 1)
                    steps.then(nc.vector.reduce_max(stat[:, 0, i:i + 1], k.ps[:, i % DEEP, :], AX_X))
                    nc.vector.tensor_scalar(stat[:, 1, i:i + 1], stat[:, 0, i:i + 1], -scale, None, ALU.mult).then_inc(maxed, 1)

                for i in range(DEEP - 1):
                    largest(i)
                for i, (n, b) in enumerate(units):
                    dve.wait_ge(exped, i + 1)
                    steps.then(nc.vector.reciprocal(stat[:, 3, i:i + 1], stat[:, 2, i:i + 1]))
                    nc.vector.tensor_scalar(probs[:, i % DEEP, :], probs[:, i % DEEP, :], stat[:, 3, i:i + 1], None, ALU.mult).then_inc(normed, 1)
                    if i + DEEP - 1 < len(units):
                        largest(i + DEEP - 1)
                    if b == 0 and n >= 1:
                        store(n - 1)
                store(len(heads) - 1)

            @block.scalar
            def _(act):
                def copy(i):
                    n, b = units[i]
                    act.wait_ge(flipped, i + 1)
                    if n >= 2:
                        act.wait_ge(mixed, n - 1)
                    nc.scalar.activation(turned[:, n % 2, :, b * P:(b + 1) * P], k.ps[:, DEEP + i % 2, :].rearrange("p (c q) -> p c q", c=4),
                                         ACT.Identity).then_inc(copied, 1)

                for i in range(len(units)):
                    act.wait_ge(maxed, i + 1)
                    if i >= DEEP:
                        act.wait_ge(flipped, i - DEEP + 1)
                    nc.scalar.activation(probs[:, i % DEEP, :], k.ps[:, i % DEEP, :], ACT.Exp, scale=operands(*units[i])[2], bias=stat[:, 1, i:i + 1],
                                         accum_out=stat[:, 2, i:i + 1]).then_inc(exped, 1)
                    if i >= DEEP - 1:
                        copy(i - DEEP + 1)
                for i in range(len(units) - DEEP + 1, len(units)):
                    copy(i)


def stage_add_product(k, name, slabs, src, layer, part):
    nc = k.nc
    taken = sem(k, f"{name}_taken")
    first = START[slabs]
    with nc.Block() as block:
        @block.sync
        def _(sp):
            refill(k, sp, first, KC)

        @block.tensor
        def _(pe):
            for m in range(KC):
                slab = take_slab(k, pe, first + m)
                slab_product(k, slab, lambda c: src[:, c, :], k.ps[:, m, 0:T])

        @block.vector
        def _(dve):
            for m in range(KC):
                dve.wait_ge(k.slab_used, first + m + 1)
                nc.vector.scalar_tensor_tensor(k.x[:, m, :], k.ps[:, m, 0:T], gate_of(k, layer, part, m), k.x[:, m, :], ALU.mult, ALU.add)


def attention_layer(k):
    nc = k.nc
    with ExitStack() as local:
        a = Core()
        def sb(name, shape):
            return local.enter_context(nc.sbuf_tensor(f"a_{name}", shape, F32))
        a.cq, a.ckv, a.gqk = sb("cq", [P, Q_CHUNKS, T]), sb("ckv", [P, KV_CHUNKS, T2]), sb("gqk", [P, 3 * BANK])
        a.kr, a.q, a.k = sb("kr", [P, T2]), sb("q", [P, MLA_HEADS, T]), sb("k", [P, MLA_HEADS, T2])
        a.v, a.o = sb("v", [P, 4, 5 * P]), sb("o", [P, KC, T])
        ctx = sb("ctx", [P, KC, T])
        loaded = sem(k, "a_ctx_loaded")
        with nc.Block() as block:
            @block.scalar
            def _(act):
                act.dma_start(ctx[:, :, :], k.x_dram[1]).then_inc(loaded, 16)
                act.wait_ge(loaded, 16)
        stage_norm(k, "a_norm", [(lambda c: k.x[:, c, :], 0, lambda c: k.h[:, c, 0:T]),
                                 (lambda c: ctx[:, c, :], 1, lambda c: k.h[:, c, T:T2])])
        stage_attention_in(k, a)
        stage_norm(k, "cq_norm", [(lambda c: a.cq[:, c, :], None, lambda c: a.cq[:, c, :])], Q_CHUNKS, k.s("q_a_g"))
        stage_norm(k, "ckv_norm", [(lambda c, i=i: a.ckv[:, c, i * T:(i + 1) * T], None, lambda c, i=i: a.ckv[:, c, i * T:(i + 1) * T])
                                   for i in range(2)], KV_CHUNKS, k.s("kv_a_g"))
        stage_grouped_heads(k, a)
        stage_latent_heads(k, a)
        stage_attention(k, a)
        stage_add_product(k, "a_out", "a_out", a.o, 0, 2)


def stage_filters(k, spectra, rstd):
    nc = k.nc
    loaded, layer_done, reduced, sine_ready, filt_done, filt_taken, squares, norm_done, parts_ready, spec_done, spec_taken, normed = (sem(k, f"filt_{n}") for n in ("loaded", "layer_done", "reduced", "sine_ready", "done", "taken", "squares", "norm_done", "parts_ready", "spec_done", "spec_taken", "normed"))
    H, C2PI, MAGIC = F_HIDDEN, 6.28125, 1.5 * 2.0 ** 23
    with ExitStack() as local:
        def sb(name, shape):
            return local.enter_context(nc.sbuf_tensor(f"filt_{name}", shape, F32))
        feats, hid, y, turns_ = sb("feats", [F_EMB, T]), sb("hid", [H, T]), sb("y", [H, T]), sb("turns", [H, T])
        w4, window = sb("w4", [H, 4 * D]), sb("window", [P, 2, D])
        fc, fs, first = sb("fc", [P, 2, T]), sb("fs", [P, 2, T]), sb("first", [P, 2])
        power, sq, even = sb("power", [P, ORDERS, D]), sb("sq", [P, D]), sb("even", [P, 2, D])
        root = sb("root", [P, ORDERS * KC])
        with nc.Block() as block:
            @block.scalar
            def _(act):
                for dst, src in [(feats, "feats"), (w4, "w4"), (window, "window"), (fc, "fc"), (fs, "fs"), (first, "first")]:
                    act.dma_start(dst[:], k.dram[src]).then_inc(loaded, 16)
                act.wait_ge(loaded, 6 * 16)
                for n in range(3):
                    act.wait_ge(reduced, n + 1)
                    nc.scalar.activation(hid[:, :], y[:, :], ACT.Sin).then_inc(sine_ready, 1)
                act.wait_ge(norm_done, 1)
                nc.scalar.activation(root[:, :], k.ps[:, 0, 0:ORDERS * KC], ACT.Sqrt, bias=k.s("eps")).then_inc(normed, 1)
                for o in range(ORDERS):
                    for n in range(8):
                        act.wait_ge(spec_done, o * 8 + n + 1)
                        if n == 0:
                            act.wait_ge(spec_done, o * 8 + 8)
                        nc.scalar.activation(spectra[:, o, n // 2, (n % 2) * BANK:(n % 2 + 1) * BANK], k.ps[:, n, :], ACT.Identity).then_inc(spec_taken, 1)

            @block.tensor
            def _(pe):
                pe.wait_ge(loaded, 6 * 16)
                for n, w in enumerate(("f_w1", "f_w2", "f_w3")):
                    if n:
                        pe.wait_ge(sine_ready, n)
                    rows = F_EMB if n == 0 else H
                    nc.tensor.matmul(k.ps[0:H, n, 0:T], k.s(w)[0:rows, :], (feats if n == 0 else hid)[:, :], start=True, stop=True).then_inc(layer_done, 1)
                pe.wait_ge(sine_ready, 3)
                for t in range(2):
                    for n in range(8):
                        if t:
                            pe.wait_ge(filt_taken, n + 1)
                        nc.tensor.matmul(k.ps[:, n, :], hid[:, t * P:(t + 1) * P], w4[:, n * BANK:(n + 1) * BANK], start=True, stop=True).then_inc(filt_done, 1)
                pe.wait_ge(squares, 1)
                pe.wait_ge(filt_taken, 16)
                for n in range(ORDERS * KC):
                    last = nc.tensor.matmul(k.ps[:, 0, n:n + 1], power[:, n // KC, (n % KC) * P:(n % KC + 1) * P], k.s("ones")[:, 0:1], start=True, stop=True)
                last.then_inc(norm_done, 1)
                pe.wait_ge(normed, 1)
                for o in range(ORDERS):
                    pe.wait_ge(parts_ready, o + 1)
                    for n in range(8):
                        part, f, half = n // 4, n // 2 % 2, n % 2
                        if o:
                            pe.wait_ge(spec_taken, n + 1)
                        for t in range(2):
                            src = even[:, t, :] if part == 0 else spectra[:, o, 2 + t, :]
                            last = nc.tensor.matmul(k.ps[:, n, :], (fc if part == 0 else fs)[:, t, f * P:(f + 1) * P],
                                                    src[:, half * BANK:(half + 1) * BANK], start=t == 0, stop=t == 1)
                        last.then_inc(spec_done, 1)

            @block.vector
            def _(dve):
                steps = k.dve_steps.on(dve)
                for n in range(3):
                    dve.wait_ge(layer_done, n + 1)
                    if n:
                        dve.wait_ge(sine_ready, n)
                    b, f = k.s("f_b")[0:H, n:n + 1], k.s("f_freq")[0:H, n:n + 1]
                    steps.then(nc.vector.tensor_scalar(y[:, :], k.ps[0:H, n, 0:T], b, f, ALU.add, ALU.mult))
                    steps.then(nc.vector.tensor_scalar(turns_[:, :], y[:, :], 1.0 / (2.0 * math.pi), MAGIC, ALU.mult, ALU.add))
                    steps.then(nc.vector.tensor_scalar(turns_[:, :], turns_[:, :], MAGIC, None, ALU.subtract))
                    steps.then(nc.vector.scalar_tensor_tensor(y[:, :], turns_[:, :], -C2PI, y[:, :], ALU.mult, ALU.add))
                    steps.then(nc.vector.scalar_tensor_tensor(y[:, :], turns_[:, :], C2PI - 2.0 * math.pi, y[:, :], ALU.mult, ALU.add))
                    nc.vector.tensor_scalar(y[:, :], y[:, :], 3.1415925, -3.1415925, ALU.min, ALU.max).then_inc(reduced, 1)
                for t in range(2):
                    for n in range(8):
                        d, o, half = n // 4, n // 2 % 2, n % 2
                        cols = slice(half * BANK, (half + 1) * BANK)
                        dve.wait_ge(filt_done, 8 * t + n + 1)
                        nc.vector.tensor_tensor(spectra[:, o, 2 * d + t, cols], k.ps[:, n, :], window[:, t, cols], ALU.mult).then_inc(filt_taken, 1)
                dve.wait_ge(filt_taken, 16)
                for o in range(ORDERS):
                    steps.then(nc.vector.tensor_tensor(power[:, o, :], spectra[:, o, 0, :], spectra[:, o, 0, :], ALU.mult))
                    for n in range(1, 4):
                        steps.then(nc.vector.tensor_tensor(sq[:, :], spectra[:, o, n, :], spectra[:, o, n, :], ALU.mult))
                        steps.then(nc.vector.tensor_tensor(power[:, o, :], power[:, o, :], sq[:, :], ALU.add))
                nc.vector.tensor_copy(sq[:, 0:1], power[:, 0, 0:1]).then_inc(squares, 1)
                dve.wait_ge(normed, 1)
                nc.vector.reciprocal(rstd[:, :], root[:, :])
                for o in range(ORDERS):
                    if o:
                        dve.wait_ge(spec_done, 8)
                    for t in range(2):
                        steps.done(nc.vector.scalar_tensor_tensor(even[:, t, :], spectra[:, o, 2 + t, :], first[:, t:t + 1], spectra[:, o, t, :], ALU.mult, ALU.add))
                    for t in range(2):
                        steps.then(nc.vector.tensor_scalar(spectra[:, o, 2 + t, :], spectra[:, o, 2 + t, :], first[:, t:t + 1], None, ALU.mult))
                        last = nc.vector.tensor_tensor(spectra[:, o, 2 + t, :], spectra[:, o, t, :], spectra[:, o, 2 + t, :], ALU.subtract)
                        steps.done(last) if t == 0 else last.then_inc(parts_ready, 1)


def stage_hyena_in(k, z):
    nc = k.nc
    taken, cleared, convolved = (sem(k, f"h_in_{n}") for n in ("taken", "cleared", "convolved"))
    first = START["h_in"]
    with ExitStack() as local:
        padded = local.enter_context(nc.sbuf_tensor("h_padded", [P, KC, T + 2], F32))
        with nc.Block() as block:
            @block.sync
            def _(sp):
                refill(k, sp, first, 3 * KC)

            @block.gpsimd
            def _(pool):
                nc.gpsimd.memset(padded[:, :, :], 0.0).then_inc(cleared, 1)

            @block.tensor
            def _(pe):
                for m in range(3 * KC):
                    slab = take_slab(k, pe, first + m)
                    if m >= 8:
                        pe.wait_ge(taken, m - 7)
                    slab_product(k, slab, lambda c: k.h[:, c, 0:T], k.ps[:, m % 8, 0:T])

            @block.scalar
            def _(act):
                act.wait_ge(cleared, 1)
                for m in range(3 * KC):
                    act.wait_ge(k.slab_used, first + m + 1)
                    if m >= KC:
                        act.wait_ge(convolved, m - KC + 1)
                    nc.scalar.activation(padded[:, m % KC, 1:T + 1], k.ps[:, m % 8, 0:T], ACT.Identity).then_inc(taken, 1)

            @block.vector
            def _(dve):
                steps = k.dve_steps.on(dve)
                w, b = k.s("h_conv_w"), k.s("h_conv_b")
                for m in range(3 * KC):
                    dve.wait_ge(taken, m + 1)
                    tap = lambda j: (padded[:, m % KC, j:j + T], w[:, j * 3 * KC + m:j * 3 * KC + m + 1])
                    steps.then(nc.vector.tensor_scalar(z[:, m, :], *tap(0), b[:, m:m + 1], ALU.mult, ALU.add))
                    steps.then(nc.vector.scalar_tensor_tensor(z[:, m, :], *tap(1), z[:, m, :], ALU.mult, ALU.add))
                    nc.vector.scalar_tensor_tensor(z[:, m, :], *tap(2), z[:, m, :], ALU.mult, ALU.add).then_inc(convolved, 1)


def stage_long_conv(k, o, spectra, rstd, z):
    nc = k.nc
    loaded, flipped, copied, spec_done, prod_ready, back_done, back_taken = (sem(k, f"conv{o}_{n}") for n in ("loaded", "flipped", "copied", "spec_done", "prod_ready", "back_done", "back_taken"))
    work = k.h[:, :, :].rearrange("p a b -> p (a b)")
    vt, ta, tb = work[:, 0:2 * D].rearrange("p (t d) -> p t d", t=2), work[:, 2 * D:3 * D], work[:, 3 * D:4 * D]
    v = z[:, 2 * KC:3 * KC, :]
    with ExitStack() as local:
        fc, fs, gc, gs = (local.enter_context(nc.sbuf_tensor(f"conv{o}_{n}", [P, 2, T], F32)) for n in ("fc", "fs", "gc", "gs"))
        prod = local.enter_context(nc.sbuf_tensor(f"conv{o}_prod", [P, 4, D], F32))
        tmp = local.enter_context(nc.sbuf_tensor(f"conv{o}_tmp", [P, 2, T], F32))
        with nc.Block() as block:
            @block.scalar
            def _(act):
                for dst, src in [(fc, "fc"), (fs, "fs"), (gc, "gc"), (gs, "gs")]:
                    act.dma_start(dst[:], k.dram[src]).then_inc(loaded, 16)
                for n in range(4):
                    act.wait_ge(flipped, n + 1)
                    nc.scalar.activation(vt[:, n // 2, (n % 2) * BANK:(n % 2 + 1) * BANK], k.ps[:, n, :], ACT.Identity).then_inc(copied, 1)
                act.wait_ge(loaded, 4 * 16)

            @block.tensor
            def _(pe):
                for n in range(4):
                    for c in range(4):
                        last = nc.tensor.transpose(k.ps[:, n, c * P:(c + 1) * P], v[:, (n % 2) * 4 + c, (n // 2) * P:(n // 2 + 1) * P], k.s("ident"))
                    last.then_inc(flipped, 1)
                pe.wait_ge(loaded, 4 * 16)
                pe.wait_ge(copied, 4)
                for f in range(2):
                    for part in range(2):
                        for half in range(2):
                            for t in range(2):
                                last = nc.tensor.matmul(k.ps[:, 4 * part + 2 * f + half, :], (fs if part else fc)[:, t, f * P:(f + 1) * P],
                                                        vt[:, t, half * BANK:(half + 1) * BANK], start=t == 0, stop=t == 1)
                    last.then_inc(spec_done, 1)
                pe.wait_ge(prod_ready, 2)
                for m in range(KC):
                    for n in range(4):
                        last = nc.tensor.matmul(k.ps[:, m, 0:T], prod[:, n, m * P:(m + 1) * P], (gs if n // 2 else gc)[:, n % 2, :], start=n == 0, stop=n == 3)
                    last.then_inc(back_done, 1)

            @block.vector
            def _(dve):
                steps = k.dve_steps.on(dve)
                for f in range(2):
                    dve.wait_ge(spec_done, f + 1)
                    re = k.ps[:, 2 * f:2 * f + 2, :].rearrange("p b n -> p (b n)")
                    im = k.ps[:, 4 + 2 * f:6 + 2 * f, :].rearrange("p b n -> p (b n)")
                    kre, kim = spectra[:, o, f, :], spectra[:, o, 2 + f, :]
                    steps.done(nc.vector.tensor_tensor(ta, re, kre, ALU.mult))
                    steps.then(nc.vector.tensor_tensor(tb, im, kim, ALU.mult))
                    steps.then(nc.vector.tensor_tensor(prod[:, f, :], ta, tb, ALU.subtract))
                    steps.done(nc.vector.tensor_tensor(ta, re, kim, ALU.mult))
                    steps.then(nc.vector.tensor_tensor(tb, im, kre, ALU.mult))
                    nc.vector.tensor_tensor(prod[:, 2 + f, :], ta, tb, ALU.add).then_inc(prod_ready, 1)
                    dve.wait_ge(prod_ready, f + 1)
                for m in range(KC):
                    n = o * KC + m
                    dve.wait_ge(back_done, m + 1)
                    steps.then(nc.vector.tensor_scalar(tmp[:, m % 2, :], k.ps[:, m, 0:T], rstd[:, n:n + 1], None, ALU.mult))
                    steps.then(nc.vector.scalar_tensor_tensor(tmp[:, m % 2, :], v[:, m, :], k.s("h_skip")[:, n:n + 1], tmp[:, m % 2, :], ALU.mult, ALU.add))
                    steps.then(nc.vector.tensor_tensor(v[:, m, :], tmp[:, m % 2, :], z[:, o * KC + m, :], ALU.mult))


def hyena_layer(k):
    nc = k.nc
    with ExitStack() as local:
        spectra = local.enter_context(nc.sbuf_tensor("h_spectra", [P, ORDERS, 4, D], F32))
        rstd = local.enter_context(nc.sbuf_tensor("h_rstd", [P, ORDERS * KC], F32))
        stage_filters(k, spectra, rstd)
        z = local.enter_context(nc.sbuf_tensor("h_z", [P, 3 * KC, T], F32))
        stage_norm(k, "h_norm", [(lambda c: k.x[:, c, :], 2, lambda c: k.h[:, c, 0:T])])
        stage_hyena_in(k, z)
        for o in range(ORDERS):
            stage_long_conv(k, o, spectra, rstd, z)
        stage_add_product(k, "h_out", "h_out", z[:, 2 * KC:3 * KC, :], 1, 2)


def stage_delta_qkv(k, qkv, gates):
    nc = k.nc
    cleared, taken, convolved, ba_done, silu_done = (sem(k, f"gq_{n}") for n in ("cleared", "taken", "convolved", "ba_done", "silu_done"))
    first, ba = START["g_qkv"], START["g_ba"]
    SLOTS = 4
    with ExitStack() as local:
        grid = local.enter_context(nc.sbuf_tensor("g_grid", [P, SLOTS, ROWS + 2, GRID_W + 2], F32))
        line = local.enter_context(nc.sbuf_tensor("g_line", [P, SLOTS, T + 2], F32))
        with nc.Block() as block:
            @block.sync
            def _(sp):
                refill(k, sp, first, QKV_CHUNKS + 1)

            @block.gpsimd
            def _(pool):
                nc.gpsimd.memset(grid[:, :, :, :], 0.0).then_inc(cleared, 1)
                nc.gpsimd.memset(line[:, :, :], 0.0).then_inc(cleared, 1)

            @block.tensor
            def _(pe):
                for m in range(QKV_CHUNKS):
                    slab = take_slab(k, pe, first + m)
                    if m >= 7:
                        pe.wait_ge(taken, m - 6)
                    slab_product(k, slab, lambda c: k.h[:, c, :], k.ps[:, m % 7, :])
                w = take_slab(k, pe, ba).rearrange("p (k c) -> p k c", k=KC)
                for b in range(4):
                    for c in range(KC):
                        last = nc.tensor.matmul(k.ps[:, 7, b * 32:(b + 1) * 32], k.h[:, c, b * P:(b + 1) * P], w[:, c, 0:32], start=c == 0, stop=c == KC - 1)
                last.then_inc(k.slab_used, 1)

            @block.scalar
            def _(act):
                act.wait_ge(cleared, 2)

                def silu(m):
                    act.wait_ge(convolved, m + 1)
                    nc.scalar.activation(qkv[:, m, :], qkv[:, m, :], ACT.Silu).then_inc(silu_done, 1)

                for m in range(QKV_CHUNKS):
                    act.wait_ge(k.slab_used, first + m + 1)
                    if m >= SLOTS:
                        act.wait_ge(convolved, m - SLOTS + 1)
                    nc.scalar.activation(grid[:, m % SLOTS, 1:ROWS + 1, 1:GRID_W + 1],
                                         k.ps[:, m % 7, 0:T].rearrange("p (r c) -> p r c", r=ROWS), ACT.Identity)
                    nc.scalar.activation(line[:, m % SLOTS, 1:T + 1], k.ps[:, m % 7, T:T2], ACT.Identity).then_inc(taken, 1)
                    if m >= 2:
                        silu(m - 2)
                silu(QKV_CHUNKS - 2)
                silu(QKV_CHUNKS - 1)

            @block.vector
            def _(dve):
                steps = k.dve_steps.on(dve)
                w = k.s("g_conv_w")
                for m in range(QKV_CHUNKS):
                    lat = qkv[:, m, 0:T].rearrange("p (r c) -> p r c", r=ROWS)
                    ctx = qkv[:, m, T:T2]
                    tap = lambda dy, dx: w[:, (3 * dy + dx) * QKV_CHUNKS + m:(3 * dy + dx) * QKV_CHUNKS + m + 1]
                    dve.wait_ge(taken, m + 1)
                    for n in range(9):
                        dy, dx = n // 3, n % 3
                        src = grid[:, m % SLOTS, dy:dy + ROWS, dx:dx + GRID_W]
                        if n == 0:
                            steps.done(nc.vector.tensor_scalar(lat, src, tap(dy, dx), None, ALU.mult))
                            steps.then(nc.vector.tensor_scalar(ctx, line[:, m % SLOTS, 0:T], tap(1, 0), None, ALU.mult))
                        else:
                            last = nc.vector.scalar_tensor_tensor(lat, src, tap(dy, dx), lat, ALU.mult, ALU.add)
                            if n in (4, 6):
                                steps.done(last)
                                j = n // 2 - 1
                                steps.then(nc.vector.scalar_tensor_tensor(ctx, line[:, m % SLOTS, j:j + T], tap(1, j), ctx, ALU.mult, ALU.add))
                            elif n < 8:
                                steps.then(last)
                            else:
                                last.then_inc(convolved, 1)
                dve.wait_ge(k.slab_used, ba + 1)
                nc.vector.tensor_copy(gates[:, :, :], k.ps[:, 7, 0:P].rearrange("p (b n) -> p b n", b=4))


def stage_delta_norm(k, qkv):
    nc = k.nc
    squared, total, root = (sem(k, f"gl_{n}") for n in ("squared", "total", "root"))
    heads = 2 * NQK
    with ExitStack() as local:
        sq = local.enter_context(nc.sbuf_tensor("gl_sq", [P, heads, T2], F32))
        with nc.Block() as block:
            @block.scalar
            def _(act):
                for c in range(heads):
                    nc.scalar.activation(sq[:, c, :], qkv[:, c, :], ACT.Square).then_inc(squared, 1)
                for c in range(heads):
                    act.wait_ge(total, c + 1)
                    nc.scalar.activation(sq[:, c, :], k.ps[:, c, :], ACT.Sqrt, bias=k.s("eps")).then_inc(root, 1)

            @block.tensor
            def _(pe):
                for c in range(heads):
                    pe.wait_ge(squared, c + 1)
                    nc.tensor.matmul(k.ps[:, c, :], k.s("ones"), sq[:, c, :], start=True, stop=True).then_inc(total, 1)

            @block.vector
            def _(dve):
                steps = k.dve_steps.on(dve)
                for c in range(heads):
                    dve.wait_ge(root, c + 1)
                    steps.then(nc.vector.reciprocal(sq[:, c, :], sq[:, c, :]))
                    nc.vector.scalar_tensor_tensor(qkv[:, c, :], qkv[:, c, :], P ** -0.5 if c < NQK else 1.0, sq[:, c, :], ALU.mult, ALU.mult)


def stage_delta_turn(k, qkv, g):
    nc = k.nc
    flipped, copied, logs_ready, sums_done = (sem(k, f"gt_{n}") for n in ("flipped", "copied", "logs_ready", "sums_done"))
    chunks = list(range(NQK, QKV_CHUNKS))
    banks = [(b, c) for b in range(4) for c in range(0, len(chunks), 4)]
    with ExitStack() as local:
        def sb(name, shape):
            return local.enter_context(nc.sbuf_tensor(f"gt_{name}", shape, F32))
        raw, soft, rate = sb("raw", [P, 4, 2 * NV]), sb("soft", [P, 4, 2 * NV]), sb("rate", [P, 2 * NV])
        with nc.Block() as block:
            @block.tensor
            def _(pe):
                for n, (b, c) in enumerate(banks):
                    if n >= 6:
                        pe.wait_ge(copied, n - 5)
                    for i in range(4):
                        last = nc.tensor.transpose(k.ps[:, n % 6, i * P:(i + 1) * P], qkv[:, chunks[c + i], b * P:(b + 1) * P], k.s("ident"))
                    last.then_inc(flipped, 1)
                pe.wait_ge(logs_ready, 1)
                for d in range(2):
                    src = g.log[:, d, :]
                    nc.tensor.matmul(k.ps[:, 6, d * 32:(d + 1) * 32], k.s("tri")[:, d * P:(d + 1) * P], src, start=True, stop=True)
                    last = nc.tensor.matmul(k.ps[:, 7, d * 32:(d + 1) * 32], k.s("ones"), src, start=True, stop=True)
                last.then_inc(sums_done, 1)

            @block.scalar
            def _(act):
                steps = k.act_steps.on(act)
                for n, (b, c) in enumerate(banks):
                    dst = g.k_tok[:, b, :] if c == 0 else g.v_tok[:, b, (c // 4 - 1) * BANK:c // 4 * BANK]
                    act.wait_ge(flipped, n + 1)
                    nc.scalar.activation(dst, k.ps[:, n % 6, :], ACT.Identity).then_inc(copied, 1)
                steps.done(nc.scalar.activation(rate[:, :], k.s("a_log"), ACT.Exp))
                act.wait_ge(g.raw_ready, 1)
                steps.then(nc.scalar.activation(soft[:, :, :], raw[:, :, :], ACT.Abs))
                steps.then(nc.scalar.activation(soft[:, :, :], soft[:, :, :], ACT.Exp, scale=-1.0))
                nc.scalar.activation(soft[:, :, :], soft[:, :, :], ACT.Ln, bias=k.s("one")).then_inc(g.soft_ready, 1)
                for d in range(2):
                    last = nc.scalar.activation(g.beta[:, d, :].rearrange("p (b h) -> p b h", b=4), g.gates[:, :, d * NV:(d + 1) * NV], ACT.Sigmoid)
                last.then_inc(g.beta_ready, 1)
                act.wait_ge(g.cum_ready, 1)
                nc.scalar.activation(g.from_start[:, :, :], g.cum[:, :, :], ACT.Exp).then_inc(g.start_ready, 1)
                act.wait_ge(g.cum_ready, 2)
                nc.scalar.activation(g.end[:, :, :], g.end[:, :, :], ACT.Exp)
                steps.then(nc.scalar.activation(g.to_end[:, :, :], g.to_end[:, :, :], ACT.Exp))

            @block.vector
            def _(dve):
                steps = k.dve_steps.on(dve)
                for b in range(4):
                    last = nc.vector.tensor_tensor(raw[:, b, :], g.gates[:, b, 2 * NV:4 * NV], k.s("dt_bias"), ALU.add)
                last.then_inc(g.raw_ready, 1)
                dve.wait_ge(g.soft_ready, 1)
                steps.then(nc.vector.scalar_tensor_tensor(soft[:, :, :], raw[:, :, :], 0.0, soft[:, :, :], ALU.max, ALU.add))
                for d in range(2):
                    for b in range(4):
                        last = nc.vector.scalar_tensor_tensor(g.log[:, d, b * NV:(b + 1) * NV], soft[:, b, d * NV:(d + 1) * NV], -1.0,
                                                              rate[:, d * NV:(d + 1) * NV], ALU.mult, ALU.mult)
                last.then_inc(logs_ready, 1)
                dve.wait_ge(sums_done, 1)
                nc.vector.tensor_copy(g.end[:, :, :].rearrange("p d n -> p (d n)"), k.ps[:, 7, 0:64])
                nc.vector.tensor_copy(g.cum[:, :, :].rearrange("p d n -> p (d n)"), k.ps[:, 6, 0:64]).then_inc(g.cum_ready, 1)
                dve.wait_ge(g.cum_ready, 1)
                nc.vector.tensor_tensor(g.to_end[:, :, :], g.end[:, :, :], g.cum[:, :, :], ALU.subtract).then_inc(g.cum_ready, 1)
                dve.wait_ge(g.start_ready, 1)
                dve.wait_ge(g.beta_ready, 1)
                nc.vector.scalar_tensor_tensor(g.erase[:, :, :], g.beta[:, :, :], -1.0, g.from_start[:, :, :], ALU.mult, ALU.mult)


def stage_delta_solve(k, d, qkv, g):
    nc = k.nc
    gram_done, gram_taken, rows_ready, sums_done, gaps_ready, decay_ready, lower_ready, prod_done, prod_ready, step_done, step_ready, pairs_ready = (
        sem(k, f"gs{d}_{n}") for n in ("gram_done", "gram_taken", "rows_ready", "sums_done", "gaps_ready", "decay_ready", "lower_ready",
                                       "prod_done", "prod_ready", "step_done", "step_ready", "pairs_ready"))
    S, U = 2, 4
    tri, strict = k.s("tri")[:, d * P:(d + 1) * P], k.s("strict")[:, d * P:(d + 1) * P]
    level = lambda dd, n: k.s("level")[:, (dd * LEVELS + n) * P:(dd * LEVELS + n + 1) * P]
    wide = lambda m: m.unsqueeze(1).broadcast_to([P, U, P])
    with ExitStack() as local:
        def sb(name, shape):
            return local.enter_context(nc.sbuf_tensor(f"gs{d}_{name}", shape, F32))
        gram, mixed = sb("gram", [P, 4 * NQK, P]), sb("mixed", [P, 2 * NQK, P])
        rows, fall, rise = sb("rows", [P, S, U, P]), sb("fall", [P, S, U, P]), sb("rise", [P, S, U, P])
        low, prod, inv, inv_t = sb("low", [P, S, U, P]), sb("prod", [P, S, U, P]), sb("inv", [P, S, U, P]), sb("inv_t", [P, S, U, P])

        def bank(n):
            return k.ps[:, n, :].rearrange("p (u t) -> p u t", u=U)

        with nc.Block() as block:
            @block.tensor
            def _(pe):
                for b in range(4):
                    for h in range(NQK):
                        kt = qkv[:, NQK + h, b * P:(b + 1) * P]
                        last = nc.tensor.matmul(k.ps[:, b, h * P:(h + 1) * P], kt, kt, start=True, stop=True)
                    last.then_inc(gram_done, 1)
                for b in range(2):
                    for h in range(NQK):
                        last = nc.tensor.matmul(k.ps[:, 4 + b, h * P:(h + 1) * P], qkv[:, NQK + h, b * P:(b + 1) * P], qkv[:, h, b * P:(b + 1) * P], start=True, stop=True)
                    last.then_inc(gram_done, 1)
                pe.wait_ge(gram_taken, 6)

                def block_of(t):
                    for s in range(S):
                        pe.wait_ge(rows_ready, t * S + s + 1)
                        nc.tensor.matmul(k.ps[:, s, :], k.s("ones"), rows[:, s, :, :].rearrange("p u t -> p (u t)"), start=True, stop=True).then_inc(sums_done, 1)
                    for n in range(LEVELS):
                        for s in range(S):
                            if n == 0:
                                pe.wait_ge(lower_ready, t * S + s + 1)
                            else:
                                pe.wait_ge(step_ready, t * S * LEVELS + (n - 1) * S + s + 2)
                            for u in range(U):
                                last = nc.tensor.matmul(k.ps[:, 2 + s, u * P:(u + 1) * P], low[:, s, u, :], k.s("ident") if n == 0 else inv_t[:, s, u, :], start=True, stop=True)
                            last.then_inc(prod_done, 1)
                        if n == 0:
                            continue
                        for s in range(S):
                            pe.wait_ge(prod_ready, t * S * LEVELS + n * S + s + 1)
                            for u in range(U):
                                last = nc.tensor.matmul(k.ps[:, 4 + s, u * P:(u + 1) * P], inv[:, s, u, :], prod[:, s, u, :], start=True, stop=True)
                            if n < LEVELS - 1:
                                for u in range(U):
                                    last = nc.tensor.matmul(k.ps[:, 6 + s, u * P:(u + 1) * P], prod[:, s, u, :], inv[:, s, u, :], start=True, stop=True)
                            last.then_inc(step_done, 1)

                with pe.Fori(0, 4) as t:
                    block_of(t)

            @block.scalar
            def _(act):
                def block_of(t):
                    for s in range(S):
                        for u in range(U):
                            col = g.log[:, d, bass.ds(t * NV + s * U + u, 1)]
                            last = nc.scalar.activation(rows[:, s, u, :], tri, ACT.Identity, scale=col)
                        last.then_inc(rows_ready, 1)
                    for s in range(S):
                        act.wait_ge(gaps_ready, t * S + s + 1)
                        nc.scalar.activation(fall[:, s, :, :], fall[:, s, :, :], ACT.Exp, scale=-1.0)
                        nc.scalar.activation(rise[:, s, :, :], rise[:, s, :, :], ACT.Exp).then_inc(decay_ready, 1)

                with act.Fori(0, 4) as t:
                    act.wait_ge(step_ready, t * S * LEVELS + 1)
                    block_of(t)

            @block.vector
            def _(dve):
                for b in range(4):
                    dve.wait_ge(gram_done, b + 1)
                    nc.vector.tensor_tensor(gram[:, b * NQK:(b + 1) * NQK, :], bank(b), strict.unsqueeze(1).broadcast_to([P, NQK, P]), ALU.mult).then_inc(gram_taken, 1)
                for b in range(2):
                    dve.wait_ge(gram_done, 4 + b + 1)
                    nc.vector.tensor_tensor(mixed[:, b * NQK:(b + 1) * NQK, :], bank(4 + b), tri.unsqueeze(1).broadcast_to([P, NQK, P]), ALU.mult).then_inc(gram_taken, 1)
                dve.wait_ge(gram_taken, 6)
                dve.sem_inc(step_ready, 1)

                def block_of(t, latents):
                    for s in range(S):
                        dve.wait_ge(sums_done, t * S + s + 1)
                        for u in range(U):
                            col = g.cum[:, d, bass.ds(t * NV + s * U + u, 1)]
                            nc.vector.tensor_scalar(fall[:, s, u, :], bank(s)[:, u, :], col, 0.0, ALU.subtract, ALU.max)
                            last = nc.vector.tensor_scalar(rise[:, s, u, :], bank(s)[:, u, :], col, 0.0, ALU.subtract, ALU.min)
                        last.then_inc(gaps_ready, 1)
                    for s in range(S):
                        dve.wait_ge(decay_ready, t * S + s + 1)
                        for u in range(U):
                            col = g.beta[:, d, bass.ds(t * NV + s * U + u, 1)]
                            kk = gram[:, bass.ds(t * NQK + (s * U + u) // 2, 1), :].rearrange("p a t -> p (a t)")
                            last = nc.vector.scalar_tensor_tensor(low[:, s, u, :], fall[:, s, u, :], col, kk, ALU.mult, ALU.mult)
                        last.then_inc(lower_ready, 1)
                        if latents:
                            for u in range(U):
                                qk = mixed[:, bass.ds(t * NQK + (s * U + u) // 2, 1), :].rearrange("p a t -> p (a t)")
                                out = g.qk[:, bass.ds(t * NV + s * U + u, 1), :].rearrange("p a t -> p (a t)")
                                nc.vector.tensor_tensor(out, rise[:, s, u, :], qk, ALU.mult)
                    for s in range(S):
                        dve.wait_ge(lower_ready, t * S + s + 1)
                        nc.vector.tensor_tensor(inv[:, s, :, :], low[:, s, :, :], wide(level(1 - d, 0)), ALU.mult).then_inc(pairs_ready, 1)
                    for n in range(LEVELS):
                        for s in range(S):
                            dve.wait_ge(prod_done, t * S * LEVELS + n * S + s + 1)
                            nc.vector.tensor_tensor(prod[:, s, :, :], bank(2 + s), wide(level(d, n)), ALU.mult).then_inc(prod_ready, 1)
                        for s in range(S):
                            if n == 0:
                                dve.wait_ge(prod_ready, t * S * LEVELS + s + 1)
                                dve.wait_ge(pairs_ready, t * S + s + 1)
                                nc.vector.tensor_tensor(inv_t[:, s, :, :], wide(k.s("ident")), prod[:, s, :, :], ALU.subtract)
                                nc.vector.tensor_tensor(inv[:, s, :, :], wide(k.s("ident")), inv[:, s, :, :], ALU.subtract).then_inc(step_ready, 1)
                                continue
                            dve.wait_ge(step_done, t * S * (LEVELS - 1) + (n - 1) * S + s + 1)
                            if n < LEVELS - 1:
                                nc.vector.tensor_tensor(inv_t[:, s, :, :], inv_t[:, s, :, :], bank(4 + s), ALU.subtract)
                                nc.vector.tensor_tensor(inv[:, s, :, :], inv[:, s, :, :], bank(6 + s), ALU.subtract).then_inc(step_ready, 1)
                            else:
                                out = g.inv_t[:, bass.ds(t * NV + s * U, U), :]
                                nc.vector.tensor_tensor(out, inv_t[:, s, :, :], bank(4 + s), ALU.subtract).then_inc(step_ready, 1)

                with dve.Fori(0, 2) as t:
                    block_of(t, True)
                with dve.Fori(2, 4) as t:
                    block_of(t, False)


def stage_delta_scan(k, d, qkv, g):
    nc = k.nc
    cleared, asked, scaled, rest_ready, solved, written, updated, state_ready, out_done, out_taken = (sem(k, f"gc{d}_{n}") for n in ("cleared", "asked", "scaled", "rest_ready", "solved", "written", "updated", "state_ready", "out_done", "out_taken"))
    S, U = 2, 4
    blocks = [2, 3, 0, 1] if d == 0 else [3, 2, 1, 0]
    units = [(n, b, s) for n, b in enumerate(blocks) for s in range(S)]
    with ExitStack() as local:
        def sb(name, shape):
            return local.enter_context(nc.sbuf_tensor(f"gc{d}_{name}", shape, F32))
        state, bv, kd, rest, write = sb("state", [P, NV, P]), sb("bv", [P, S, U, P]), sb("kd", [P, S, U, P]), sb("rest", [P, S, U, P]), sb("write", [P, S, U, P])
        with nc.Block() as block:
            @block.gpsimd
            def _(pool):
                nc.gpsimd.memset(state[:, :, :], 0.0).then_inc(cleared, 1)

            @block.tensor
            def _(pe):
                pe.wait_ge(cleared, 1)
                for n, b in enumerate(blocks):
                    for s in range(S):
                        i = n * S + s
                        if n:
                            pe.wait_ge(state_ready, i - S + 1)
                        for u in range(U):
                            h = s * U + u
                            last = nc.tensor.matmul(k.ps[:, s, u * P:(u + 1) * P], qkv[:, NQK + h // 2, b * P:(b + 1) * P], state[:, h, :], start=True, stop=True)
                        last.then_inc(asked, 1)
                    for s in range(S):
                        i = n * S + s
                        pe.wait_ge(rest_ready, i + 1)
                        for u in range(U):
                            last = nc.tensor.matmul(k.ps[:, 2 + s, u * P:(u + 1) * P], g.inv_t[:, b * NV + s * U + u, :], rest[:, s, u, :], start=True, stop=True)
                        last.then_inc(solved, 1)
                    if n >= 2:
                        for s in range(S):
                            j = (n - 2) * S + s
                            if j:
                                pe.wait_ge(out_taken, 2 * j)
                            for u in range(U):
                                h = s * U + u
                                last = nc.tensor.matmul(k.ps[:, 6, u * P:(u + 1) * P], qkv[:, h // 2, b * P:(b + 1) * P], state[:, h, :], start=True, stop=True)
                            last.then_inc(out_done, 1)
                            pe.wait_ge(written, n * S + s + 1)
                            for u in range(U):
                                last = nc.tensor.matmul(k.ps[:, 7, u * P:(u + 1) * P], g.qk[:, b * NV + s * U + u, :], write[:, s, u, :], start=True, stop=True)
                            last.then_inc(out_done, 1)
                    if n < 3:
                        for s in range(S):
                            i = n * S + s
                            pe.wait_ge(written, i + 1)
                            for u in range(U):
                                last = nc.tensor.matmul(k.ps[:, 4 + s, u * P:(u + 1) * P], kd[:, s, u, :], write[:, s, u, :], start=True, stop=True)
                            last.then_inc(updated, 1)

            @block.scalar
            def _(act):
                def scale(i):
                    n, b, s = units[i]
                    if n:
                        act.wait_ge(updated, i - S + 1)
                        act.wait_ge(rest_ready, i - S + 1)
                    for u in range(U):
                        h = s * U + u
                        col = b * NV + h
                        nc.scalar.activation(bv[:, s, u, :], g.v_tok[:, b, h * P:(h + 1) * P], ACT.Identity, scale=g.beta[:, d, col:col + 1])
                        last = nc.scalar.activation(kd[:, s, u, :], g.k_tok[:, b, h // 2 * P:(h // 2 + 1) * P], ACT.Identity, scale=g.to_end[:, d, col:col + 1])
                    last.then_inc(scaled, 1)

                scale(0)
                scale(1)
                for n in range(len(blocks)):
                    for s in range(S):
                        act.wait_ge(solved, n * S + s + 1)
                        if n >= 3:
                            act.wait_ge(out_done, 4 * (n - 2))
                        nc.scalar.activation(write[:, s, :, :], k.ps[:, 2 + s, :].rearrange("p (u t) -> p u t", u=U), ACT.Identity).then_inc(written, 1)
                    if n < 3:
                        scale((n + 1) * S)
                        scale((n + 1) * S + 1)

            @block.vector
            def _(dve):
                steps = k.dve_steps.on(dve)
                for n, b in enumerate(blocks):
                    for s in range(S):
                        i = n * S + s
                        dve.wait_ge(asked, i + 1)
                        dve.wait_ge(scaled, i + 1)
                        for u in range(U):
                            col = b * NV + s * U + u
                            last = nc.vector.scalar_tensor_tensor(rest[:, s, u, :], k.ps[:, s, u * P:(u + 1) * P], g.erase[:, d, col:col + 1], bv[:, s, u, :], ALU.mult, ALU.add)
                        last.then_inc(rest_ready, 1)
                    if n >= 2:
                        for s in range(S):
                            j = (n - 2) * S + s
                            cols = slice(s * U * P, (s + 1) * U * P)
                            dve.wait_ge(out_done, 2 * j + 1)
                            for u in range(U):
                                h = s * U + u
                                col, o = b * NV + h, g.o[:, b, h * P:(h + 1) * P]
                                if d == 0:
                                    last = nc.vector.tensor_scalar(o, k.ps[:, 6, u * P:(u + 1) * P], g.from_start[:, d, col:col + 1], None, ALU.mult)
                                else:
                                    last = nc.vector.scalar_tensor_tensor(o, k.ps[:, 6, u * P:(u + 1) * P], g.from_start[:, d, col:col + 1], o, ALU.mult, ALU.add)
                            last.then_inc(out_taken, 1)
                            dve.wait_ge(out_taken, 2 * j + 1)
                            dve.wait_ge(out_done, 2 * j + 2)
                            nc.vector.tensor_tensor(g.o[:, b, cols], g.o[:, b, cols], k.ps[:, 7, :], ALU.add).then_inc(out_taken, 1)
                    if n < 3:
                        for s in range(S):
                            i = n * S + s
                            dve.wait_ge(updated, i + 1)
                            if n == 2:
                                dve.wait_ge(out_done, 4)
                            for u in range(U):
                                h = s * U + u
                                col = b * NV + h
                                last = nc.vector.scalar_tensor_tensor(state[:, h, :], state[:, h, :], g.end[:, d, col:col + 1], k.ps[:, 4 + s, u * P:(u + 1) * P], ALU.mult, ALU.add)
                            last.then_inc(state_ready, 1)


def stage_fourier(k, ya):
    nc = k.nc
    taken, mid_done, mid_taken, four_done, four_taken, out_done, out_taken = (sem(k, f"ff_{n}") for n in ("taken", "mid_done", "mid_taken", "four_done", "four_taken", "out_done", "out_taken"))
    first, fout = START["g_f"], START["g_fout"]
    with ExitStack() as local:
        ft = local.enter_context(nc.sbuf_tensor("ff_ft", [P, F_GROUPS, T], F32))
        mid = local.enter_context(nc.sbuf_tensor("ff_mid", [P, F_GROUPS, 2, 2 * P], F32))
        out = local.enter_context(nc.sbuf_tensor("ff_out", [P, F_GROUPS, T], F32))
        four_t = k.s("four_t").rearrange("p (a c t) -> p a c t", a=2, c=2)
        with nc.Block() as block:
            @block.sync
            def _(sp):
                refill(k, sp, first, 2 * F_GROUPS)

            @block.tensor
            def _(pe):
                for m in range(F_GROUPS):
                    slab_product(k, take_slab(k, pe, first + m), lambda c: k.h[:, c, 0:T], k.ps[:, m, 0:T])
                for m in range(F_GROUPS):
                    pe.wait_ge(taken, m + 1)
                    for b in range(2):
                        last = nc.tensor.matmul(k.ps[:, 4 + m, b * T:(b + 1) * T], ft[:, m, b * P:(b + 1) * P], k.s("four_g"), start=True, stop=True)
                    last.then_inc(mid_done, 1)
                for m in range(F_GROUPS):
                    pe.wait_ge(mid_taken, m + 1)
                    for n in range(4):
                        part, b = n // 2, n % 2
                        last = nc.tensor.matmul(k.ps[:, m, 0:T], mid[:, m, b, part * P:(part + 1) * P], four_t[:, part, b, :], start=n == 0, stop=n == 3)
                    last.then_inc(four_done, 1)
                pe.wait_ge(four_taken, F_GROUPS)
                for m in range(KC):
                    w = take_slab(k, pe, fout + m // 2).rearrange("p (k c) -> p k c", k=F_GROUPS)
                    for c in range(F_GROUPS):
                        last = nc.tensor.matmul(k.ps[:, m, 0:T], w[:, c, (m % 2) * P:(m % 2 + 1) * P], out[:, c, :], start=c == 0, stop=c == F_GROUPS - 1)
                    last.then_inc(k.slab_used if m % 2 else out_done, 1)

            @block.vector
            def _(dve):
                for m in range(F_GROUPS):
                    dve.wait_ge(k.slab_used, first + m + 1)
                    nc.vector.tensor_copy(ft[:, m, :], k.ps[:, m, 0:T]).then_inc(taken, 1)
                for m in range(F_GROUPS):
                    dve.wait_ge(mid_done, m + 1)
                    nc.vector.tensor_copy(mid[:, m, :, :].rearrange("p b n -> p (b n)"), k.ps[:, 4 + m, :]).then_inc(mid_taken, 1)
                for m in range(F_GROUPS):
                    dve.wait_ge(four_done, m + 1)
                    nc.vector.tensor_copy(out[:, m, :], k.ps[:, m, 0:T]).then_inc(four_taken, 1)
                for m in range(KC):
                    dve.wait_ge(k.slab_used if m % 2 else out_done, fout + m // 2 + 1 if m % 2 else m // 2 + 1)
                    nc.vector.tensor_copy(ya[:, m, :], k.ps[:, m, 0:T])


def stage_delta_out(k, g, yb):
    nc = k.nc
    squared, root, normed, flipped, silu_done, taken = (sem(k, f"go_{n}") for n in ("squared", "root", "normed", "flipped", "silu_done", "taken"))
    first = START["g_z"]
    with ExitStack() as local:
        sq = local.enter_context(nc.sbuf_tensor("go_sq", [P, 2 * D], F32))
        stat = local.enter_context(nc.sbuf_tensor("go_stat", [P, 3, 2 * NV], F32))
        with nc.Block() as block:
            @block.sync
            def _(sp):
                refill(k, sp, first, KC)

            @block.tensor
            def _(pe):
                for m in range(KC):
                    slab = take_slab(k, pe, first + m)
                    if m >= 4:
                        pe.wait_ge(silu_done, m - 3)
                    slab_product(k, slab, lambda c: k.h[:, c, 0:T], k.ps[:, m % 4, 0:T])
                pe.wait_ge(normed, 1)
                for m in range(KC):
                    if m >= 4:
                        pe.wait_ge(taken, m - 3)
                    for b in range(2):
                        last = nc.tensor.transpose(k.ps[:, 4 + m % 4, b * P:(b + 1) * P], g.o[:, b, m * P:(m + 1) * P], k.s("ident"))
                    last.then_inc(flipped, 1)

            @block.scalar
            def _(act):
                for b in range(2):
                    for h in range(NV):
                        n = b * NV + h
                        last = nc.scalar.activation(sq[:, n * P:(n + 1) * P], g.o[:, b, h * P:(h + 1) * P], ACT.Square, accum_out=stat[:, 0, n:n + 1])
                        last.then_inc(squared, 1)
                act.wait_ge(squared, 2 * NV)
                nc.scalar.activation(stat[:, 1, :], stat[:, 0, :], ACT.Sqrt, scale=1.0 / P, bias=k.s("eps")).then_inc(root, 1)
                for m in range(KC):
                    act.wait_ge(k.slab_used, first + m + 1)
                    nc.scalar.activation(yb[:, m, :], k.ps[:, m % 4, 0:T], ACT.Silu).then_inc(silu_done, 1)

            @block.vector
            def _(dve):
                steps = k.dve_steps.on(dve)
                dve.wait_ge(root, 1)
                steps.then(nc.vector.reciprocal(stat[:, 2, :], stat[:, 1, :]))
                for b in range(2):
                    for h in range(NV):
                        n = b * NV + h
                        last = nc.vector.tensor_scalar(g.o[:, b, h * P:(h + 1) * P], g.o[:, b, h * P:(h + 1) * P], stat[:, 2, n:n + 1], None, ALU.mult)
                last.then_inc(normed, 1)
                for m in range(KC):
                    dve.wait_ge(flipped, m + 1)
                    dve.wait_ge(silu_done, m + 1)
                    nc.vector.scalar_tensor_tensor(yb[:, m, :], k.ps[:, 4 + m % 4, 0:T], k.s("gdn_g"), yb[:, m, :], ALU.mult, ALU.mult).then_inc(taken, 1)


def stage_merge(k, ya, yb):
    nc = k.nc
    gated, loaded, split = (sem(k, f"gm_{n}") for n in ("gated", "loaded", "split"))
    E = N_EXPERTS
    first, ga, gb = START["g_out"], START["g_ga"], START["g_gb"]
    with ExitStack() as local:
        gate = local.enter_context(nc.sbuf_tensor("gm_gate", [P, 2, KC, T], F32))
        raw = local.enter_context(nc.sbuf_tensor("gm_raw", [3 * E, 3, D], F32))
        with nc.Block() as block:
            @block.gpsimd
            def _(pool):
                steps = Steps(split).on(pool)
                pool.wait_ge(loaded, 3 * 16)
                for n in range(3):
                    rows = [slice(g * E, (g + 1) * E) for g in range(n, 3)]
                    for r in rows:
                        steps.then(nc.gpsimd.tensor_copy(k.bias[r, :, :], raw[r, :, :]))
                    for r in rows[1:]:
                        steps.then(nc.gpsimd.tensor_tensor(raw[r, :, :], raw[r, :, :], k.bias[r, :, :], ALU.subtract))

            @block.sync
            def _(sp):
                refill(k, sp, first, 3 * KC)

            @block.tensor
            def _(pe):
                for m in range(KC):
                    slab_product(k, take_slab(k, pe, first + m), lambda c: yb[:, c, :], k.ps[:, m // 2, (m % 2) * T:(m % 2 + 1) * T])
                for n in range(2 * KC):
                    if n >= 4:
                        pe.wait_ge(gated, n - 3)
                    slab_product(k, take_slab(k, pe, ga + n), lambda c: k.h[:, c, 0:T], k.ps[:, 4 + n % 4, 0:T])

            @block.scalar
            def _(act):
                for n in range(3):
                    act.dma_start(raw[n * E:(n + 1) * E, :, :], k.dram["bias"]).then_inc(loaded, 16)
                for n in range(2 * KC):
                    act.wait_ge(k.slab_used, ga + n + 1)
                    nc.scalar.activation(gate[:, n // KC, n % KC, :], k.ps[:, 4 + n % 4, 0:T], ACT.Sigmoid).then_inc(gated, 1)

            @block.vector
            def _(dve):
                steps = k.dve_steps.on(dve)
                for m in range(KC):
                    dve.wait_ge(gated, m + 1)
                    steps.done(nc.vector.tensor_tensor(ya[:, m, :], ya[:, m, :], gate[:, 0, m, :], ALU.mult))
                for m in range(KC):
                    dve.wait_ge(gated, KC + m + 1)
                    steps.then(nc.vector.tensor_tensor(gate[:, 1, m, :], k.ps[:, m // 2, (m % 2) * T:(m % 2 + 1) * T], gate[:, 1, m, :], ALU.mult))
                    nc.vector.tensor_tensor(ya[:, m, :], ya[:, m, :], gate[:, 1, m, :], ALU.add)


def delta_layer(k):
    nc = k.nc
    with ExitStack() as local:
        def sb(name, shape):
            return local.enter_context(nc.sbuf_tensor(f"g_{name}", shape, F32))
        g = Core()
        g.o = sb("o", [P, 2, D])
        with ExitStack() as inner:
            def sbi(name, shape):
                return inner.enter_context(nc.sbuf_tensor(f"g_{name}", shape, F32))
            g.k_tok, g.v_tok = sbi("k_tok", [P, 4, NQK * P]), sbi("v_tok", [P, 4, NV * P])
            g.gates = sbi("gates", [P, 4, 4 * NV])
            g.log, g.cum, g.beta, g.end, g.from_start, g.to_end, g.erase = (
                sbi(n, [P, 2, 4 * NV]) for n in ("log", "cum", "beta", "end", "from_start", "to_end", "erase"))
            g.raw_ready, g.soft_ready, g.beta_ready, g.cum_ready, g.start_ready = (
                sem(k, f"gt_{n}") for n in ("raw_ready", "soft_ready", "beta_ready", "cum_ready", "start_ready"))
            qkv = sbi("qkv", [P, QKV_CHUNKS, T2])
            with ExitStack() as first:
                ctx = first.enter_context(nc.sbuf_tensor("g_ctx", [P, KC, T], F32))
                loaded = sem(k, "g_ctx_loaded")
                with nc.Block() as block:
                    @block.scalar
                    def _(act):
                        act.dma_start(ctx[:, :, :], k.x_dram[2]).then_inc(loaded, 16)
                        act.wait_ge(loaded, 16)
                stage_norm(k, "final0", [(lambda c: k.x[:, c, :], None, lambda c: k.x[:, c, :])], KC, k.s("norm_g")[:, 4 * KC:5 * KC])
                stage_norm(k, "g_norm", [(lambda c: k.x[:, c, :], 4, lambda c: k.h[:, c, 0:T]),
                                         (lambda c: ctx[:, c, :], 5, lambda c: k.h[:, c, T:T2])])
            stage_delta_qkv(k, qkv, g.gates)
            stage_delta_norm(k, qkv)
            stage_delta_turn(k, qkv, g)
            g.inv_t = qkv[:, 2 * NQK:QKV_CHUNKS, :].rearrange("p c (a t) -> p (c a) t", t=P)
            g.qk = sbi("qk", [P, 2 * NV, P])
            for d in range(2):
                stage_delta_solve(k, d, qkv, g)
                stage_delta_scan(k, d, qkv, g)
        ya, yb = sb("ya", [P, KC, T]), sb("yb", [P, KC, T])
        stage_fourier(k, ya)
        stage_delta_out(k, g, yb)
        stage_merge(k, ya, yb)
        stage_add_product(k, "g_merge", "g_merge", ya, 2, 2)


def stage_router(k, m):
    nc = k.nc
    less, exped, flipped, weighed, h_flipped, h_copied, counted, blocks, ends, ended, spread, chosen, placed, tables = (
        sem(k, f"rt_{n}") for n in ("less", "exped", "flipped", "weighed", "h_flipped", "h_copied", "counted", "blocks", "ends", "ended",
                                    "spread", "chosen", "placed", "tables"))
    first = START["router"]
    E, B = N_EXPERTS, MAX_BLOCKS
    E3 = 3 * E
    with ExitStack() as local:
        def sb(name, shape, dt=F32):
            return local.enter_context(nc.sbuf_tensor(f"rt_{name}", shape, dt))
        logit, e, more, same, rank, place = (sb(n, [P, 2, E]) for n in ("logit", "e", "more", "same", "rank", "place"))
        top, stat = sb("top", [P, 2, 8]), sb("stat", [P, 2, 5])
        mask3, turned = sb("mask3", [P, 2, E3]), sb("turned", [E, 2, T])
        count, reach = sb("count", [E3, 4]), sb("reach", [E3, 3, B])
        after = sb("after", [E, B])
        with nc.Block() as block:
            @block.sync
            def _(sp):
                refill(k, sp, first, 1)

            @block.tensor
            def _(pe):
                w = take_slab(k, pe, first).rearrange("p (k c) -> p k c", k=KC)
                for b in range(2):
                    for c in range(KC):
                        last = nc.tensor.matmul(k.ps[:, 0, b * E:(b + 1) * E], k.h[:, c, b * P:(b + 1) * P], w[:, c, 0:E], start=c == 0, stop=c == KC - 1)
                last.then_inc(k.slab_used, 1)
                for n in range(4):
                    for c in range(4):
                        last = nc.tensor.transpose(k.ps[:, 4 + n, c * P:(c + 1) * P], k.h[:, (n % 2) * 4 + c, (n // 2) * P:(n // 2 + 1) * P], k.s("ident"))
                    last.then_inc(h_flipped, 1)
                pe.wait_ge(weighed, 2)
                for b in range(2):
                    last = nc.tensor.matmul(k.ps[0:E3, 1, 0:1], mask3[:, b, :], k.s("ones")[:, 0:1], start=b == 0, stop=b == 1)
                last.then_inc(counted, 1)
                before = k.s("strict")[:, P:2 * P]
                nc.tensor.matmul(k.ps[:, 2, 0:E], before, mask3[:, 0, 0:E], start=True, stop=True)
                nc.tensor.matmul(k.ps[:, 2, E:2 * E], before, mask3[:, 1, 0:E], start=True, stop=False)
                nc.tensor.matmul(k.ps[:, 2, E:2 * E], k.s("ones"), mask3[:, 0, 0:E], start=False, stop=True).then_inc(spread, 1)
                pe.wait_ge(blocks, 1)
                nc.tensor.matmul(k.ps[0:E3, 1, 0:1], k.s("tri3")[0:E, :], count[0:E, 1:2], start=True, stop=True).then_inc(ends, 1)
                pe.wait_ge(ended, 1)
                nc.tensor.matmul(k.ps[0:1, 3, 0:B], k.s("ones")[0:E, 0:1], after[:, :], start=True, stop=True)
                nc.tensor.matmul(k.ps[0:1, 3, B:B + 1], count[0:E, 1:2], k.s("ones")[0:E, 0:1], start=True, stop=True).then_inc(tables, 1)
                pe.wait_ge(chosen, 2)
                for b in range(2):
                    nc.tensor.transpose(k.ps[0:E, 0, b * P:(b + 1) * P], e[:, b, :], k.s("ident"))
                    last = nc.tensor.transpose(k.ps[0:E, 0, T + b * P:T + (b + 1) * P], place[:, b, :], k.s("ident"))
                last.then_inc(flipped, 1)
                pe.wait_ge(placed, 1)
                for b in range(2):
                    cols = slice(b * P, (b + 1) * P)
                    nc.tensor.matmul(k.ps[:, 1, b * B:(b + 1) * B], turned[:, 1, cols], reach[0:E, 0, :], start=True, stop=False)
                    nc.tensor.matmul(k.ps[:, 1, b * B:(b + 1) * B], k.s("ones")[0:E, :], reach[0:E, 2, :], start=False, stop=True)
                    last = nc.tensor.matmul(k.ps[:, 1, (2 + b) * B:(3 + b) * B], turned[:, 0, cols], reach[0:E, 0, :], start=True, stop=True)
                last.then_inc(tables, 1)

            @block.scalar
            def _(act):
                for n in range(4):
                    act.wait_ge(h_flipped, n + 1)
                    nc.scalar.activation(m.h_tok[:, n // 2, (n % 2) * BANK:(n % 2 + 1) * BANK], k.ps[:, 4 + n, :], ACT.Identity).then_inc(h_copied, 1)
                for b in range(2):
                    act.wait_ge(less, b + 1)
                    nc.scalar.activation(e[:, b, :], logit[:, b, :], ACT.Exp, bias=stat[:, b, 0:1]).then_inc(exped, 1)

            @block.vector
            def _(dve):
                steps = k.dve_steps.on(dve)
                dve.wait_ge(k.slab_used, first + 1)
                for b in range(2):
                    l, fourth = logit[:, b, :], top[:, b, TOP_K - 1:TOP_K]
                    steps.then(nc.vector.tensor_tensor(l, k.ps[:, 0, b * E:(b + 1) * E], k.s("b_router"), ALU.add))
                    steps.then(nc.vector.max(top[:, b, :], l))
                    nc.vector.tensor_scalar(stat[:, b, 0:1], top[:, b, 0:1], -1.0, None, ALU.mult).then_inc(less, 1)
                    steps.done(nc.vector.tensor_scalar(same[:, b, :], l, fourth, None, ALU.is_equal))
                    steps.then(nc.vector.tensor_scalar(more[:, b, :], l, fourth, None, ALU.is_gt))
                    steps.done(nc.vector.reduce_sum(stat[:, b, 1:2], more[:, b, :], AX_X))
                    steps.then(nc.vector.tensor_tensor_scan(rank[:, b, :], k.s("ones")[:, 0:E], same[:, b, :], 0.0, ALU.mult, ALU.add))
                    steps.then(nc.vector.tensor_scalar(rank[:, b, :], rank[:, b, :], stat[:, b, 1:2], float(TOP_K), ALU.add, ALU.is_le))
                    steps.then(nc.vector.tensor_tensor(same[:, b, :], same[:, b, :], rank[:, b, :], ALU.mult))
                    steps.then(nc.vector.tensor_tensor(more[:, b, :], more[:, b, :], same[:, b, :], ALU.add))
                    dve.wait_ge(exped, b + 1)
                    for n in range(3):
                        nc.vector.tensor_copy(mask3[:, b, n * E:(n + 1) * E], more[:, b, :])
                    steps.then(nc.vector.tensor_tensor(e[:, b, :], e[:, b, :], more[:, b, :], ALU.mult))
                    steps.then(nc.vector.reduce_sum(stat[:, b, 2:3], e[:, b, :], AX_X))
                    steps.then(nc.vector.reciprocal(stat[:, b, 3:4], stat[:, b, 2:3]))
                    nc.vector.tensor_scalar(e[:, b, :], e[:, b, :], stat[:, b, 3:4], None, ALU.mult).then_inc(weighed, 1)
                dve.wait_ge(counted, 1)
                steps.then(nc.vector.tensor_scalar(count[:, 0:1], k.ps[0:E3, 1, 0:1], 0.5, None, ALU.is_gt))
                for n in range(1, T // BLOCK_SLOTS):
                    new, old = count[:, n % 2:n % 2 + 1], count[:, (n - 1) % 2:(n - 1) % 2 + 1]
                    steps.then(nc.vector.tensor_scalar(new, k.ps[0:E3, 1, 0:1], n * BLOCK_SLOTS + 0.5, old, ALU.is_gt, ALU.add))
                nc.vector.tensor_copy(count[:, 0:1], count[:, 1:2]).then_inc(blocks, 1)
                dve.wait_ge(spread, 1)
                for b in range(2):
                    steps.then(nc.vector.scalar_tensor_tensor(place[:, b, :], k.ps[:, 2, b * E:(b + 1) * E], FAR, mask3[:, b, 0:E], ALU.add, ALU.mult))
                    nc.vector.tensor_scalar(place[:, b, :], place[:, b, :], -FAR, None, ALU.add).then_inc(chosen, 1)
                dve.wait_ge(ends, 1)
                iota = k.s("iota")[:, 0:B]
                steps.then(nc.vector.tensor_copy(count[:, 2:3], k.ps[0:E3, 1, 0:1]))
                nc.vector.tensor_scalar(after[:, :], iota[0:E, :], count[0:E, 2:3], None, ALU.is_ge).then_inc(ended, 1)
                steps.then(nc.vector.tensor_tensor(count[:, 3:4], count[:, 2:3], count[:, 1:2], ALU.subtract))
                steps.done(nc.vector.tensor_scalar(reach[:, 0, :], iota[0:E3, :], count[:, 2:3], None, ALU.is_lt))
                steps.then(nc.vector.tensor_scalar(reach[:, 1, :], iota[0:E3, :], count[:, 3:4], None, ALU.is_ge))
                steps.then(nc.vector.tensor_tensor(reach[:, 0, :], reach[:, 0, :], reach[:, 1, :], ALU.mult))
                steps.then(nc.vector.tensor_scalar(reach[:, 2, :], iota[0:E3, :], count[:, 3:4], -float(BLOCK_SLOTS), ALU.subtract, ALU.mult))
                steps.then(nc.vector.tensor_tensor(reach[:, 2, :], reach[:, 2, :], reach[:, 0, :], ALU.mult))
                nc.vector.tensor_copy(m.of_block[:, :], reach[:, 0, :])
                dve.wait_ge(tables, 1)
                nc.vector.tensor_copy(m.table[0:1, :], k.ps[0:1, 3, 0:B + 1])
                dve.wait_ge(flipped, 1)
                nc.vector.tensor_copy(turned[:, :, :].rearrange("e n t -> e (n t)"), k.ps[0:E, 0, :]).then_inc(placed, 1)
                dve.wait_ge(tables, 2)
                nc.vector.tensor_copy(m.places[:, :, :].rearrange("p n i -> p (n i)"), k.ps[:, 1, 0:4 * B])


def stage_experts(k, m, total):
    nc = k.nc
    (sel_ready, pick_ready, gathered, x_ready, gate_ready, sig_ready, act_ready, flipped, turned_ready, weigh_ready, weigh_flipped, weigh_turned,
     y_ready, spread, added, cleared) = (
        sem(k, f"ex_{n}") for n in ("sel_ready", "pick_ready", "gathered", "x_ready", "gate_ready", "sig_ready", "act_ready", "flipped", "turned_ready",
                                    "weigh_ready", "weigh_flipped", "weigh_turned", "y_ready", "spread", "added", "cleared"))
    first, PER_BLOCK, B = START["moe"], 3 * KC, MAX_BLOCKS
    GATE, UP, DOWN = 0, 1, 2
    HALF = [slice(h * BLOCK_SLOTS, (h + 1) * BLOCK_SLOTS) for h in range(2)]
    OUT, TURNED, ROWS_IN, WEIGHED, ADD = (0, 1, 2), 4, 5, 7, ((3, 6), (2, 4))
    with ExitStack() as local:
        def sb(name, shape, dt=F32):
            return local.enter_context(nc.sbuf_tensor(f"ex_{name}", shape, dt))
        sel = sb("sel", [3 * N_EXPERTS, BLOCK_SLOTS], BF16)
        pick, weigh, weigh_t = sb("pick", [P, 2, BLOCK_SLOTS]), sb("weigh", [P, 2, P]), sb("weigh_t", [P, T])
        x = sb("x", [P, KC, BLOCK_SLOTS])
        gate, up, sig, y = sb("gate", [P, BANK]), sb("up", [P, BANK]), sb("sig", [P, BANK]), sb("y", [P, BANK])
        act_t = sb("act_t", [P, 4, P])
        with nc.Block() as block:
            @block.sync
            def _(sp):
                n_blocks = sp.value_load(m.table[0:1, B:B + 1], min_val=1, max_val=B - 1)
                with sp.Fori(0, n_blocks) as i:
                    expert = sp.value_load(m.table[0:1, bass.ds(i, 1)], min_val=0, max_val=N_EXPERTS - 1)
                    for j in range(PER_BLOCK):
                        s = (first + j) % RING
                        sp.wait_ge(k.slab_used, i * PER_BLOCK + first + j - RING + 1)
                        src = k.stream_dram[bass.ds(expert * PER_BLOCK + first + j, 1), :, :].rearrange("a p n -> (a p) n")
                        sp.dma_start(k.ring[:, s, :], src).then_inc(k.slab_filled[s], 16)

            @block.tensor
            def _(pe):
                def gather(i):
                    pe.wait_ge(pick_ready, i + 1)
                    for c in range(KC):
                        for b in range(2):
                            last = nc.tensor.matmul(k.ps[:, ROWS_IN, c * BLOCK_SLOTS:(c + 1) * BLOCK_SLOTS], m.h_tok[:, b, c * P:(c + 1) * P], pick[:, b, :],
                                                    start=b == 0, stop=b == 1)
                    last.then_inc(gathered, 1)

                def product(i, matrix, src):
                    for h in range(2):
                        nc.tensor.matmul(k.ps[HALF[h], OUT[matrix], :], sel[:, :], k.bias[:, matrix, h * BANK:(h + 1) * BANK], start=True, stop=False)
                    for q in range(KC):
                        slab = take_slab(k, pe, first + matrix * KC + q, i, PER_BLOCK)
                        for h in range(2):
                            last = nc.tensor.matmul(k.ps[HALF[h], OUT[matrix], :], src(q), slab[:, h * BANK:(h + 1) * BANK], start=False, stop=q == KC - 1)
                        last.then_inc(k.slab_used, 1)

                n_blocks = pe.value_load(m.table[0:1, B:B + 1], min_val=1, max_val=B - 1)
                gather(0)
                with pe.Fori(0, n_blocks) as i:
                    pe.wait_ge(x_ready, i + 1)
                    pe.wait_ge(sel_ready, i + 1)
                    product(i, GATE, lambda q: x[:, q, :])
                    product(i, UP, lambda q: x[:, q, :])
                    gather(i + 1)
                    pe.wait_ge(weigh_ready, i + 1)
                    for b in range(2):
                        last = nc.tensor.transpose(k.ps[:, WEIGHED, b * P:(b + 1) * P], weigh[:, b, :], k.s("ident"))
                    last.then_inc(weigh_flipped, 1)
                    pe.wait_ge(act_ready, i + 1)
                    pe.wait_ge(added, i * 4 + 1)
                    for c in range(4):
                        last = nc.tensor.transpose(k.ps[:, TURNED, c * P:(c + 1) * P], gate[:, c * P:(c + 1) * P], k.s("ident"))
                    last.then_inc(flipped, 1)
                    pe.wait_ge(turned_ready, i + 1)
                    product(i, DOWN, lambda q: act_t[:, q % 4, HALF[q // 4]])
                    pe.wait_ge(weigh_turned, i + 1)
                    pe.wait_ge(y_ready, i + 1)
                    for r in range(2):
                        for c in range(2):
                            for h in range(2):
                                last = nc.tensor.matmul(k.ps[:, ADD[r][h], c * T:(c + 1) * T], y[HALF[h], (2 * r + c) * P:(2 * r + c + 1) * P],
                                                        weigh_t[HALF[h], :], start=True, stop=True)
                        last.then_inc(spread, 1)

            @block.scalar
            def _(act):
                def take_x(i):
                    act.wait_ge(gathered, i + 1)
                    nc.scalar.activation(x[:, :, :].rearrange("p c s -> p (c s)"), k.ps[:, ROWS_IN, :], ACT.Identity).then_inc(x_ready, 1)

                n_blocks = act.value_load(m.table[0:1, B:B + 1], min_val=1, max_val=B - 1)
                take_x(0)
                with act.Fori(0, n_blocks) as i:
                    act.wait_ge(gate_ready, i + 1)
                    nc.scalar.activation(sig[:, :], gate[:, :], ACT.Sigmoid, scale=ALPHA).then_inc(sig_ready, 1)
                    take_x(i + 1)
                    act.wait_ge(weigh_flipped, i + 1)
                    nc.scalar.activation(weigh_t[:, :], k.ps[:, WEIGHED, 0:T], ACT.Identity).then_inc(weigh_turned, 1)
                    act.wait_ge(flipped, i + 1)
                    nc.scalar.activation(act_t[:, :, :].rearrange("p c s -> p (c s)"), k.ps[:, TURNED, :], ACT.Identity).then_inc(turned_ready, 1)
                    act.wait_ge(k.slab_used, i * PER_BLOCK + first + PER_BLOCK)
                    nc.scalar.activation(y[:, :], k.ps[:, OUT[DOWN], :], ACT.Identity).then_inc(y_ready, 1)

            @block.gpsimd
            def _(pool):
                nc.gpsimd.memset(total[:, :, :], 0.0).then_inc(cleared, 1)

            @block.vector
            def _(dve):
                steps = Steps(sem(k, "ex_dve_steps")).on(dve)
                STEPS = 2

                def choose(i):
                    nc.vector.tensor_scalar(sel[:, :], k.s("ones")[0:3 * N_EXPERTS, 0:BLOCK_SLOTS], m.of_block[:, bass.ds(i, 1)], None, ALU.mult).then_inc(sel_ready, 1)

                def picks(i):
                    for b in range(2):
                        last = nc.vector.tensor_scalar(pick[:, b, :], k.s("iota")[:, 0:BLOCK_SLOTS], m.places[:, b, bass.ds(i, 1)], None, ALU.is_equal)
                    last.then_inc(pick_ready, 1)

                dve.wait_ge(cleared, 1)
                dve.sem_inc(added, 1)
                n_blocks = dve.value_load(m.table[0:1, B:B + 1], min_val=1, max_val=B - 1)
                choose(0)
                picks(0)
                with dve.Fori(0, n_blocks) as i:
                    steps.loop(i, STEPS)
                    dve.wait_ge(gathered, i + 1)
                    picks(i + 1)
                    for b in range(2):
                        last = nc.vector.tensor_scalar(weigh[:, b, :], k.s("slots"), m.places[:, b, bass.ds(i, 1)], m.places[:, 2 + b, bass.ds(i, 1)],
                                                       ALU.is_equal, ALU.mult)
                    last.then_inc(weigh_ready, 1)
                    dve.wait_ge(k.slab_used, i * PER_BLOCK + first + KC)
                    nc.vector.tensor_scalar(gate[:, :], k.ps[:, OUT[GATE], :], LIMIT, None, ALU.min).then_inc(gate_ready, 1)
                    dve.wait_ge(sig_ready, i + 1)
                    steps.done(nc.vector.tensor_tensor(gate[:, :], gate[:, :], sig[:, :], ALU.mult))
                    dve.wait_ge(k.slab_used, i * PER_BLOCK + first + 2 * KC)
                    steps.then(nc.vector.tensor_scalar(up[:, :], k.ps[:, OUT[UP], :], LIMIT, -LIMIT, ALU.min, ALU.max))
                    nc.vector.scalar_tensor_tensor(gate[:, :], up[:, :], 1.0, gate[:, :], ALU.add, ALU.mult).then_inc(act_ready, 1)
                    dve.wait_ge(k.slab_used, i * PER_BLOCK + first + PER_BLOCK)
                    choose(i + 1)
                    for r in range(2):
                        dve.wait_ge(spread, i * 2 + r + 1)
                        for h in range(2):
                            pair = total[:, 4 * h + 2 * r:4 * h + 2 * r + 2, :].rearrange("p c t -> p (c t)")
                            nc.vector.tensor_tensor(pair, pair, k.ps[:, ADD[r][h], :], ALU.add).then_inc(added, 1)


def stage_add(k, total):
    nc = k.nc
    with nc.Block() as block:
        @block.vector
        def _(dve):
            for m in range(KC):
                nc.vector.scalar_tensor_tensor(k.x[:, m, :], total[:, m, :], gate_of(k, 2, 5, m), k.x[:, m, :], ALU.mult, ALU.add)


def stage_store(k):
    nc = k.nc
    stored = sem(k, "stored")
    with nc.Block() as block:
        @block.sync
        def _(sp):
            sp.dma_start(k.out_dram, k.x[:, :, :]).then_inc(stored, 16)
            sp.wait_ge(stored, 16)


def expert_layer(k):
    nc = k.nc
    with ExitStack() as local:
        def sb(name, shape, dt=F32):
            return local.enter_context(nc.sbuf_tensor(f"ex_{name}", shape, dt))
        m = Core()
        total = sb("total", [P, KC, T])
        m.h_tok, m.places = sb("h_tok", [P, 2, D]), sb("places", [P, 4, MAX_BLOCKS])
        m.of_block, m.table = sb("of_block", [3 * N_EXPERTS, MAX_BLOCKS]), sb("table", [1, MAX_BLOCKS + 1], mybir.dt.int32)
        stage_norm(k, "e_norm", [(lambda c: k.x[:, c, :], 7, lambda c: k.h[:, c, 0:T])])
        stage_router(k, m)
        stage_experts(k, m, total)
        stage_add(k, total)
    stage_norm(k, "final1", [(lambda c: k.x[:, c, :], None, lambda c: k.x[:, c, :])], KC, k.s("norm_g")[:, 7 * KC:8 * KC])


def build(nc, dram, out, stop=None):
    k = Core()
    k.nc, k.dram, k.out_dram = nc, dram, out
    k.stream_dram, k.small_dram, k.x_dram = dram["stream"], dram["small"], dram["tokens"]
    layout, columns = small_layout()
    k.norms = [(0, 1, 0), (0, 1, 1), (1, 1, 0), (0, 4, 0), (2, 1, 2), (2, 1, 3), (1, 4, 0), (2, 4, 2)]
    k.norm_of = [0, 0, 1, 2, 5, 5, 3, 6]
    with ExitStack() as stack:
        k.sems, k.sem_stack = [], stack
        k.ring = stack.enter_context(nc.sbuf_tensor("ring", [P, RING, KC * P], F32))
        k.small = stack.enter_context(nc.sbuf_tensor("small", [P, columns], F32))
        k.x = stack.enter_context(nc.sbuf_tensor("x", [P, KC, T], F32))
        k.h = stack.enter_context(nc.sbuf_tensor("h", [P, KC, T2], F32))
        k.mod = stack.enter_context(nc.sbuf_tensor("mod", [P, 4, 3 * MOD_CHUNKS], F32))
        k.gain = stack.enter_context(nc.sbuf_tensor("gain", [P, 8, KC], F32))
        k.bias = stack.enter_context(nc.sbuf_tensor("bias", [3 * N_EXPERTS, 3, D], BF16))
        k.ps = stack.enter_context(nc.psum_tensor("ps", [P, 8, BANK], F32))
        k.s = lambda name: k.small[:, layout[name][0]:layout[name][0] + layout[name][1]]
        k.slab_filled = [sem(k, f"slab_filled{i}") for i in range(RING)]
        k.dve_steps, k.act_steps = Steps(sem(k, "dve_steps")), Steps(sem(k, "act_steps"))
        k.norm_sems = [sem(k, f"norm_{n}") for n in ("squares", "total", "root", "scaled", "inverse")]
        k.norm_chunks = k.norm_parts = 0
        k.slab_used, k.small_loaded, k.x_loaded = (sem(k, n) for n in ("slab_used", "small_loaded", "x_loaded"))
        for name, stage in [("load", stage_load), ("modulation", stage_modulation), ("attention", attention_layer),
                            ("mlp0", lambda k: mlp_layer(k, 0, 3)), ("hyena", hyena_layer), ("mlp1", lambda k: mlp_layer(k, 1, 6)),
                            ("delta", delta_layer), ("experts", expert_layer)]:
            with_own_semaphores(k, stage)
            if name == stop:
                break
        with_own_semaphores(k, stage_store)


def mlp_layer(k, layer, norm):
    stage_norm(k, f"m{layer}_norm", [(lambda c: k.x[:, c, :], norm, lambda c: k.h[:, c, 0:T])])
    stage_mlp(k, layer)


def slabs_of(w, chunks=KC):
    n = w.shape[1] // P
    return w.reshape(chunks, P, n, P).transpose(2, 1, 0, 3).reshape(n, P, chunks * P)


def mod_slabs(w):
    return w.reshape(D, MOD_CHUNKS, P).transpose(1, 2, 0)


def padded_slab(w):
    out = np.zeros((1, P, KC * P), np.float32)
    out[0, :, :w.shape[1]] = w
    return out


def weight_stream(i):
    def columns(w, cols):
        out = np.zeros((D, P), np.float32)
        out[:, cols[0]:cols[0] + w.shape[1]] = w
        return slabs_of(out)
    a = i["a_w_in"][0]
    cq, ckv, kr, gq, gk, gv = np.split(a, np.cumsum([384, 256, 32, 512, 128]), axis=1)
    gq = gq.reshape(D, GQA_KV, 4, HEAD).transpose(0, 2, 1, 3).reshape(D, GQA_HEADS * HEAD)
    qb = i["a_w_q_b"][0].reshape(Q_CHUNKS, P, MLA_HEADS, QK_MLA).transpose(1, 0, 2, 3)
    kvb = i["a_w_kv_b"][0].reshape(KV_CHUNKS, P, MLA_HEADS, NOPE + DV).transpose(1, 0, 2, 3)
    out = i["a_w_out"][0]
    low = out[512:].reshape(GQA_KV, 4, HEAD, D).transpose(1, 0, 2, 3).reshape(512, D)
    parts = [mod_slabs(i["w_mod"][0]),
             slabs_of(cq), slabs_of(gq), slabs_of(ckv), slabs_of(gk), columns(kr, (NOPE,)), slabs_of(gv)]
    for h, n in ((0, 3), (3, 3), (6, 2)):
        wide = np.zeros((P, Q_CHUNKS, 3 * QK_MLA), np.float32)
        wide[:, :, :n * QK_MLA] = qb[:, :, h:h + n].reshape(P, Q_CHUNKS, n * QK_MLA)
        parts.append(padded_slab(wide.reshape(P, -1)))
    parts += [padded_slab(kvb[..., :NOPE].reshape(P, -1)), padded_slab(kvb[..., NOPE:].reshape(P, -1)),
              slabs_of(np.concatenate([out[:512], low]))]

    def mlp(n):
        w2 = i["mlp_w2"][n].reshape(4, KC, P, KC, P).transpose(3, 0, 2, 1, 4).reshape(4 * KC, P, KC * P)
        return [slabs_of(i["mlp_w1"][n]), w2]
    g = i["w_in_2"][0]
    qkv, ba, z, f, ga, gb = np.split(g, np.cumsum([2048, 32, 1024, 512, 1024]), axis=1)
    fout = i["w_fourier_out_2"][0].reshape(F_GROUPS, P, 4, 2 * P).transpose(2, 1, 0, 3).reshape(4, P, KC * P)
    parts += mlp(0) + [slabs_of(i["h_w_in"][0]), slabs_of(i["h_w_out"][0])] + mlp(1)
    parts += [slabs_of(qkv), columns(ba, (0,)), slabs_of(f), fout, slabs_of(z), slabs_of(i["w_gdn_out_2"][0]),
              slabs_of(ga), slabs_of(gb), slabs_of(i["w_merge_out_2"][0]), columns(i["w_router_2"][0], (0,))]
    out = np.empty((SLABS, P, KC * P), np.float32)
    at = 0
    for p in parts:
        out[at:at + len(p)] = p
        at += len(p)
    assert at == START["moe"]
    for e in range(N_EXPERTS):
        for n in ("w_gate_2", "w_up_2", "w_down_2"):
            out[at:at + KC] = i[n][0, e].reshape(KC, P, D)
            at += KC
    return out


def by_feature(v):
    v = np.asarray(v, np.float32).reshape(-1, P)
    return np.ascontiguousarray(v.T)


def rope_tables(half_dim):
    nf = half_dim // 2
    inv = (10000.0 ** (-np.arange(nf, dtype=np.float32) / np.float32(nf))).astype(np.float32)
    t = np.arange(T)
    ang = np.concatenate([(t // GRID_W)[None] * inv[:, None]] * 2 + [(t % GRID_W)[None] * inv[:, None]] * 2).astype(np.float32)
    turn = np.zeros((2 * half_dim, 2 * half_dim), np.float32)
    for half in (0, half_dim):
        for j in range(nf):
            turn[half + nf + j, half + j] = -1.0
            turn[half + j, half + nf + j] = 1.0
    return np.cos(ang), np.sin(ang), turn


def small_columns(i):
    layout, width = small_layout()
    out = np.zeros((P, width), np.float32)

    def put(name, a, row=0):
        a = np.asarray(a, np.float32)
        at, w = layout[name]
        assert a.shape[1] == w, (name, a.shape, w)
        out[row:row + a.shape[0], at:at + w] = a

    def rows(v):
        return np.broadcast_to(np.asarray(v, np.float32).reshape(1, -1), (P, np.size(v)))
    put("b_mod", np.concatenate([by_feature(i["b_mod"]), by_feature(i["b_mod_2"])], 1))
    put("norm_g", np.concatenate([by_feature(i[n]) for n in ("norm1_g", "norm2_g", "final_g", "norm1_g_2", "norm2_g_2", "final_norm_g_2")], 1))
    put("q_a_g", by_feature(i["a_q_a_g"]))
    put("kv_a_g", by_feature(i["a_kv_a_g"]))
    put("q_norm_g", np.tile(i["a_q_norm_g"][0], 2)[:, None])
    put("k_norm_g", np.tile(i["a_k_norm_g"][0], 2)[:, None])
    put("h_conv_w", by_feature(i["h_conv_w"]))
    put("h_conv_b", by_feature(i["h_conv_b"]))
    put("f_b", np.stack([i["h_f_b1"][0], i["h_f_b2"][0], i["h_f_b3"][0]], 1))
    put("f_freq", i["h_f_freq"][0].T)
    put("h_skip", by_feature(i["h_skip"]))
    put("g_conv_w", by_feature(i["conv_w_2"]))
    put("dt_bias", rows(i["dt_bias_2"]))
    put("a_log", rows(i["a_log_2"]))
    put("gdn_g", by_feature(i["gdn_norm_g_2"]))
    put("b_router", rows(i["b_router_2"]))
    put("f_w1", i["h_f_w1"][0])
    put("f_w2", i["h_f_w2"][0])
    put("f_w3", i["h_f_w3"][0])
    put("ident", np.eye(P))
    put("ones", np.ones((P, P)))
    put("iota", np.tile(np.arange(P), (P, 1)))
    put("slots", np.tile(np.arange(P) % BLOCK_SLOTS, (P, 1)))
    put("tri3", np.tile(np.triu(np.ones((N_EXPERTS, N_EXPERTS))), (1, 3)))
    put("blocks64", np.kron(np.eye(2), np.ones((HEAD, HEAD))))
    put("eps", np.full((P, 1), EPS))
    put("one", np.ones((P, 1)))
    cos, sin, turn = rope_tables(HEAD // 2)
    put("rope_cos", np.tile(cos, (2, 1)))
    put("rope_sin", np.tile(sin, (2, 1)))
    put("rope_turn", np.kron(np.eye(2), turn))
    cos, sin, turn = rope_tables(ROPE // 2)
    put("kr_cos", cos, NOPE)
    put("kr_sin", sin, NOPE)
    put("kr_turn", np.concatenate([np.zeros((ROPE, NOPE)), turn], 1), NOPE)
    p, f = np.arange(P)[:, None], np.arange(P)[None]
    put("tri", np.concatenate([p <= f, p >= f], 1))
    put("strict", np.concatenate([p > f, p < f], 1))
    up = [(p // (2 << n) == f // (2 << n)) & ((p >> n) % 2 == 0) & ((f >> n) % 2 == 1) for n in range(LEVELS)]
    put("level", np.concatenate(up + [m.T for m in up], 1))
    norm = 1.0 / math.sqrt(T * P)
    ang = 2 * np.pi * (np.outer(np.arange(P), np.arange(P)) % P) / P
    put("four_g", np.concatenate([np.cos(ang), -np.sin(ang)], 1) * norm)
    ang = 2 * np.pi * (np.outer(np.arange(T), np.arange(T)) % T) / T
    tab = np.stack([np.cos(ang), np.sin(ang)]).reshape(2, 2, P, T).transpose(2, 0, 1, 3)
    put("four_t", tab.reshape(P, -1))
    return out


def filter_constants():
    f32 = np.float32
    t = np.arange(T, dtype=f32)
    t_norm = t / f32(T)
    w = f32(2.0 * math.pi) * t / f32(T)
    bands = np.linspace(1e-4, BANDS - 1, BANDS, dtype=f32)
    fw = w[:, None] * bands[None]
    feats = np.concatenate([t_norm[:, None], np.cos(fw), -np.sin(fw)], 1).astype(f32)
    low, high = math.log(1e-2) / 1.5, math.log(1e-2) / 0.3
    deltas = np.abs(np.linspace(low, high, D, dtype=f32))
    window = np.exp(-t_norm[:, None] * deltas[None]).astype(f32)
    k = (np.outer(np.arange(T), 2 * np.arange(T) + 1) % (4 * T)) * (np.pi / (2 * T))
    by_token = lambda a: np.ascontiguousarray(a.reshape(2, P, -1).transpose(1, 0, 2).astype(f32))
    first = np.ones((P, 2), f32)
    first[0, 0] = 0.0
    return {"feats": np.ascontiguousarray(feats.T), "window": by_token(window), "fc": by_token(np.cos(k)), "fs": by_token(-np.sin(k)),
            "gc": by_token(np.cos(k).T / T), "gs": by_token(-np.sin(k).T / T), "first": first}


def kernel(**inputs):
    import concourse.bacc as bacc
    from concourse.bass_utils import run_bass_kernel_spmd

    i = {n: np.asarray(a) for n, a in inputs.items()}
    tokens = np.concatenate([i["x"], i["ctx"], i["ctx_2"]])
    arrays = {"stream": weight_stream(i), "small": small_columns(i),
              "tokens": np.ascontiguousarray(tokens.reshape(3, T, KC, P).transpose(0, 3, 2, 1)),
              "c4": np.tile(np.stack([i["c"][0], i["c_ctx"], i["c_2"][0], i["c_ctx_2"]]), (P, 1, 1)),
              "mod_later": np.concatenate([mod_slabs(i["w_mod"][1]), mod_slabs(i["w_mod_2"][0])]),
              "bias": np.ascontiguousarray(np.stack([i["b_gate_2"][0], i["b_up_2"][0], i["b_down_2"][0]], 1)),
              "w4": np.ascontiguousarray(i["h_f_w4"][0]), **filter_constants()}
    nc = bacc.Bacc("TRN2", target_bir_lowering=False, num_devices=1)
    dram = {n: nc.dram_tensor(f"in_{n}", a.shape, mybir.dt.from_np(a.dtype), kind="ExternalInput").ap() for n, a in arrays.items()}
    out = nc.dram_tensor("out", (P, KC, T), F32, kind="ExternalOutput").ap()
    build(nc, dram, out)
    got = run_bass_kernel_spmd(nc, [{f"in_{n}": a for n, a in arrays.items()}], core_ids=[0]).results[0]["out"]
    return np.ascontiguousarray(np.asarray(got).transpose(2, 1, 0).reshape(1, T, D))
```
